# Optimizing a Trainium2 kernel written in Bass

```python
import functools
import jax, jax.numpy as jnp
from jax import lax
import numpy as np

D_MODEL = 1024
BATCH = 1
SEQ = 512
DEPTH = 1
DEC_BATCH = 8
DEC_SEQ = 1
PAST_LEN = 1024
PAGE_SIZE = 128

LRU_WIDTH = D_MODEL
LRU_BLOCKS = 16
LRU_BLOCK = LRU_WIDTH // LRU_BLOCKS
CONV_W = 4
LRU_C = 8.0
N_HEADS = 16
N_KV = 4
GROUP = N_HEADS // N_KV
HEAD_DIM = 64
WINDOW = 128
NEG_INF = -1e30
N_GROUPS = 4
EXPERTS_PER_GROUP = 8
N_EXPERTS = N_GROUPS * EXPERTS_PER_GROUP
TOP_K = 2
EXPERT_FF = D_MODEL // 2
MOE_BLOCK = 128
ALPHA = (2 * DEPTH) ** 0.25
BETA = (8 * DEPTH) ** -0.25
LN_EPS = 1e-5
SPLITS = (LRU_WIDTH, LRU_WIDTH, N_HEADS * HEAD_DIM, N_KV * HEAD_DIM, N_KV * HEAD_DIM, D_MODEL, D_MODEL)
IN_WIDTH = sum(SPLITS)

kernel_name = "hawk_swa_sink_hiermoe_deepnorm_step"

def layer_norm(x, g, b):
    xf = x.astype(jnp.float32)
    mu = jnp.mean(xf, axis=-1, keepdims=True)
    var = jnp.mean(jnp.square(xf - mu), axis=-1, keepdims=True)
    return ((xf - mu) * lax.rsqrt(var + LN_EPS) * g + b).astype(x.dtype)

def _lin_combine(e1, e2):
    a1, b1 = e1
    a2, b2 = e2
    return a1 * a2, a2 * b1 + b2

def recurrent_branch(xl, yl, conv_state, h0, w_conv, b_conv, w_rg, b_rg, w_ig, b_ig, lru_lambda):
    B, T, _ = xl.shape
    xp = jnp.concatenate([conv_state.astype(xl.dtype), xl], axis=1)
    new_conv = xp[:, -(CONV_W - 1):]
    xc = sum(w_conv[j] * xp[:, j:j + T] for j in range(CONV_W)) + b_conv
    xb = xc.reshape(B, T, LRU_BLOCKS, LRU_BLOCK)
    r = jax.nn.sigmoid(jnp.einsum('bthi,hij->bthj', xb, w_rg) + b_rg).reshape(B, T, LRU_WIDTH)
    i = jax.nn.sigmoid(jnp.einsum('bthi,hij->bthj', xb, w_ig) + b_ig).reshape(B, T, LRU_WIDTH)
    log_a = (-LRU_C * r.astype(jnp.float32)) * jax.nn.softplus(-lru_lambda.astype(jnp.float32))
    a = jnp.exp(log_a)
    u = jnp.sqrt(-jnp.expm1(2.0 * log_a)) * (i * xc).astype(jnp.float32)
    u = u.at[:, 0].add(a[:, 0] * h0.astype(jnp.float32))
    _, h = lax.associative_scan(_lin_combine, (a, u), axis=1)
    out = h.astype(xl.dtype) * jax.nn.gelu(yl)
    return out, new_conv, h[:, -1].astype(h0.dtype)

def _attend(q, k, v, mask, sinks):
    scores = jnp.einsum('...qkgd,...skd->...kgqs', q, k).astype(jnp.float32) * (HEAD_DIM ** -0.5)
    scores = jnp.where(mask, scores, NEG_INF)
    sink = jnp.broadcast_to(sinks.reshape(N_KV, GROUP, 1, 1).astype(jnp.float32), scores.shape[:-1] + (1,))
    probs = jax.nn.softmax(jnp.concatenate([scores, sink], axis=-1), axis=-1)[..., :-1]
    return jnp.einsum('...kgqs,...skd->...qkgd', probs.astype(v.dtype), v)

def prompt_window_attention(q, k, v, sinks):
    B, T = q.shape[:2]
    nb = T // WINDOW
    qb = q.reshape(B, nb, WINDOW, N_KV, GROUP, HEAD_DIM)
    kb = k.reshape(B, nb, WINDOW, N_KV, HEAD_DIM)
    vb = v.reshape(B, nb, WINDOW, N_KV, HEAD_DIM)

    def with_prev(z):
        prev = jnp.concatenate([jnp.zeros_like(z[:, :1]), z[:, :-1]], axis=1)
        return jnp.concatenate([prev, z], axis=2)

    qi = jnp.arange(WINDOW)[:, None]
    kj = jnp.arange(2 * WINDOW)[None, :]
    band = (kj > qi) & (kj <= qi + WINDOW)
    valid = (jnp.arange(nb)[:, None, None] > 0) | (kj >= WINDOW)[None]
    mask = (band[None] & valid)[:, None, None]
    out = _attend(qb, with_prev(kb), with_prev(vb), mask, sinks)
    return out.reshape(B, T, N_HEADS * HEAD_DIM), k[:, -WINDOW:], v[:, -WINDOW:]

def sample_window_attention(q, k, v, sinks, k_buf, v_buf):
    B, T = q.shape[:2]
    kk = jnp.concatenate([k_buf.astype(k.dtype), k], axis=1)
    vv = jnp.concatenate([v_buf.astype(v.dtype), v], axis=1)
    diff = (WINDOW + jnp.arange(T))[:, None] - jnp.arange(WINDOW + T)[None, :]
    mask = (diff >= 0) & (diff < WINDOW)
    out = _attend(q, kk, vv, mask, sinks)
    return out.reshape(B, T, N_HEADS * HEAD_DIM), kk[:, -WINDOW:], vv[:, -WINDOW:]

def hier_moe(x, w_group, b_group, w_router, b_router, w_gate, w_up, w_down):
    N = x.shape[0]
    xf = x.astype(jnp.float32)
    g_logits = xf @ w_group.astype(jnp.float32) + b_group.astype(jnp.float32)
    g_prob = jax.nn.softmax(g_logits, axis=-1)
    g_idx = jnp.argmax(g_logits, axis=-1)
    p_g = jnp.take_along_axis(g_prob, g_idx[:, None], axis=1)[:, 0]
    e_logits = (xf @ w_router.astype(jnp.float32) + b_router.astype(jnp.float32)).reshape(N, N_GROUPS, EXPERTS_PER_GROUP)
    e_sel = jnp.take_along_axis(e_logits, g_idx[:, None, None], axis=1)[:, 0]
    top_v, top_i = lax.top_k(e_sel, TOP_K)
    w_tok = jax.nn.softmax(top_v, axis=-1) * p_g[:, None]
    e_id = g_idx[:, None].astype(jnp.int32) * EXPERTS_PER_GROUP + top_i.astype(jnp.int32)
    A = N * TOP_K
    flat_e = e_id.reshape(A)
    flat_t = jnp.arange(A, dtype=jnp.int32) // TOP_K
    flat_w = w_tok.reshape(A)
    order = jnp.argsort(flat_e)
    se = flat_e[order]
    counts = jnp.bincount(flat_e, length=N_EXPERTS)
    padded = (counts + MOE_BLOCK - 1) // MOE_BLOCK * MOE_BLOCK
    pad_end = jnp.cumsum(padded)
    pad_start = pad_end - padded
    start = jnp.cumsum(counts) - counts
    dest = pad_start[se] + jnp.arange(A, dtype=jnp.int32) - start[se]
    n_blocks = (A + MOE_BLOCK - 1) // MOE_BLOCK + N_EXPERTS
    P = n_blocks * MOE_BLOCK
    slot_t = jnp.full((P,), N, dtype=jnp.int32).at[dest].set(flat_t[order])
    slot_w = jnp.zeros((P,), jnp.float32).at[dest].set(flat_w[order])
    block_e = jnp.minimum(jnp.searchsorted(pad_end, jnp.arange(n_blocks) * MOE_BLOCK, side='right'), N_EXPERTS - 1)
    x_pad = jnp.concatenate([x, jnp.zeros((1, x.shape[1]), x.dtype)], axis=0)
    xb = x_pad[slot_t].reshape(n_blocks, MOE_BLOCK, x.shape[1])

    def expert_block(args):
        xi, e = args
        h = jax.nn.silu(xi @ w_gate[e]) * (xi @ w_up[e])
        return h @ w_down[e]

    yb = lax.map(expert_block, (xb, block_e)).reshape(P, x.shape[1])
    y = jnp.zeros((N + 1, x.shape[1]), jnp.float32).at[slot_t].add(yb.astype(jnp.float32) * slot_w[:, None])
    return y[:N].astype(x.dtype)

def trunk_layer(x, conv_state, h0, attn_fn, w_in, b_in, w_conv, b_conv, w_rg, b_rg, w_ig, b_ig, lru_lambda,
                sinks, w_lru_out, w_attn_out, w_o, ln1_g, ln1_b, w_group, b_group, w_router, b_router,
                w_gate, w_up, w_down, ln2_g, ln2_b):
    B, T, D = x.shape
    u = x @ w_in + b_in
    xl, yl, q, k, v, g_l, g_a = jnp.split(u, np.cumsum(SPLITS)[:-1].tolist(), axis=-1)
    rec, new_conv, h_last = recurrent_branch(xl, yl, conv_state, h0, w_conv, b_conv, w_rg, b_rg, w_ig, b_ig, lru_lambda)
    q = q.reshape(B, T, N_KV, GROUP, HEAD_DIM)
    k = k.reshape(B, T, N_KV, HEAD_DIM)
    v = v.reshape(B, T, N_KV, HEAD_DIM)
    att, k_state, v_state = attn_fn(q, k, v, sinks)
    merged = jax.nn.sigmoid(g_l) * (rec @ w_lru_out) + jax.nn.sigmoid(g_a) * (att @ w_attn_out)
    x1 = layer_norm(ALPHA * x + merged @ w_o, ln1_g, ln1_b)
    ff = hier_moe(x1.reshape(B * T, D), w_group, b_group, w_router, b_router, w_gate, w_up, w_down).reshape(B, T, D)
    y = layer_norm(ALPHA * x1 + ff, ln2_g, ln2_b)
    return y, k_state, v_state, new_conv, h_last

def setup_inputs(seed: int = 0) -> dict:
    key = jax.random.key(seed)
    ks = jax.random.split(key, 32)
    nrm = lambda k, s: jax.random.normal(k, s, jnp.float32)
    s_d = D_MODEL ** -0.5
    a_c = jax.random.uniform(ks[12], (LRU_WIDTH,), jnp.float32, 0.9, 0.999)
    sig = a_c ** (1.0 / LRU_C)
    return {
        "x_prompt": nrm(ks[0], (BATCH, SEQ, D_MODEL)),
        "x_sample": nrm(ks[1], (DEC_BATCH, DEC_SEQ, D_MODEL)),
        "cache_k": nrm(ks[2], (DEC_BATCH, WINDOW, N_KV, HEAD_DIM)),
        "cache_v": nrm(ks[3], (DEC_BATCH, WINDOW, N_KV, HEAD_DIM)),
        "state_conv": nrm(ks[4], (DEC_BATCH, CONV_W - 1, LRU_WIDTH)),
        "state_lru_h": nrm(ks[5], (DEC_BATCH, LRU_WIDTH)),
        "w_in": nrm(ks[6], (D_MODEL, IN_WIDTH)) * s_d,
        "b_in": nrm(ks[7], (IN_WIDTH,)) * 0.01,
        "w_conv": nrm(ks[8], (CONV_W, LRU_WIDTH)) * CONV_W ** -0.5,
        "b_conv": nrm(ks[9], (LRU_WIDTH,)) * 0.01,
        "w_rg": nrm(ks[10], (LRU_BLOCKS, LRU_BLOCK, LRU_BLOCK)) * LRU_BLOCK ** -0.5,
        "b_rg": nrm(ks[11], (LRU_BLOCKS, LRU_BLOCK)) * 0.01,
        "w_ig": nrm(ks[13], (LRU_BLOCKS, LRU_BLOCK, LRU_BLOCK)) * LRU_BLOCK ** -0.5,
        "b_ig": nrm(ks[14], (LRU_BLOCKS, LRU_BLOCK)) * 0.01,
        "lru_lambda": jnp.log(sig) - jnp.log1p(-sig),
        "sinks": nrm(ks[15], (N_HEADS,)),
        "w_lru_out": nrm(ks[16], (LRU_WIDTH, D_MODEL)) * LRU_WIDTH ** -0.5 * BETA,
        "w_attn_out": nrm(ks[17], (N_HEADS * HEAD_DIM, D_MODEL)) * (N_HEADS * HEAD_DIM) ** -0.5 * BETA,
        "w_o": nrm(ks[18], (D_MODEL, D_MODEL)) * s_d * BETA,
        "ln1_g": 1.0 + 0.01 * nrm(ks[19], (D_MODEL,)),
        "ln1_b": 0.01 * nrm(ks[20], (D_MODEL,)),
        "w_group": nrm(ks[21], (D_MODEL, N_GROUPS)) * s_d,
        "b_group": 0.01 * nrm(ks[22], (N_GROUPS,)),
        "w_router": nrm(ks[23], (D_MODEL, N_EXPERTS)) * s_d,
        "b_router": 0.01 * nrm(ks[24], (N_EXPERTS,)),
        "w_gate": nrm(ks[25], (N_EXPERTS, D_MODEL, EXPERT_FF)) * s_d,
        "w_up": nrm(ks[26], (N_EXPERTS, D_MODEL, EXPERT_FF)) * s_d * BETA,
        "w_down": nrm(ks[27], (N_EXPERTS, EXPERT_FF, D_MODEL)) * EXPERT_FF ** -0.5 * BETA,
        "ln2_g": 1.0 + 0.01 * nrm(ks[28], (D_MODEL,)),
        "ln2_b": 0.01 * nrm(ks[29], (D_MODEL,)),
    }

def reference(x_prompt, x_sample, cache_k, cache_v, state_conv, state_lru_h, w_in, b_in, w_conv, b_conv,
              w_rg, b_rg, w_ig, b_ig, lru_lambda, sinks, w_lru_out, w_attn_out, w_o, ln1_g, ln1_b,
              w_group, b_group, w_router, b_router, w_gate, w_up, w_down, ln2_g, ln2_b):
    weights = (w_in, b_in, w_conv, b_conv, w_rg, b_rg, w_ig, b_ig, lru_lambda, sinks, w_lru_out, w_attn_out,
               w_o, ln1_g, ln1_b, w_group, b_group, w_router, b_router, w_gate, w_up, w_down, ln2_g, ln2_b)
    yp, ykp, yvp, ycp, yhp = x_prompt, None, None, None, None
    ys, yks, yvs, ycs, yhs = x_sample, None, None, None, None
    for _ in range(DEPTH):
        conv0 = jnp.zeros((yp.shape[0], CONV_W - 1, LRU_WIDTH), yp.dtype)
        h0 = jnp.zeros((yp.shape[0], LRU_WIDTH), yp.dtype)
        yp, ykp, yvp, ycp, yhp = trunk_layer(yp, conv0, h0, prompt_window_attention, *weights)
        sample_attn = functools.partial(sample_window_attention, k_buf=cache_k, v_buf=cache_v)
        ys, yks, yvs, ycs, yhs = trunk_layer(ys, state_conv, state_lru_h, sample_attn, *weights)
    return (yp, ys, ykp, yvp, ycp, yhp, yks, yvs, ycs, yhs)


_drawn_inputs = setup_inputs


def setup_inputs(seed=0):
    import zlib

    import numpy as np

    out = dict(_drawn_inputs(seed))
    spreads = {}
    factors = {'b_rg': 21.861,
     'b_ig': 8.0,
     'sinks': 8.0,
     'ln1_g': 4.655,
     'ln1_b': 5.095,
     'b_group': 8.0,
     'b_router': 8.0,
     'ln2_g': 29.845,
     'ln2_b': 31.91}
    for name, (base, spread) in spreads.items():
        noise = np.random.default_rng([zlib.crc32(name.encode()), seed]).standard_normal(out[name].shape)
        drawn = base * np.exp(spread * noise) if base else spread * noise
        out[name] = __import__('jax').numpy.asarray(drawn.astype(out[name].dtype))
    for name, factor in factors.items():
        out[name] = (out[name] * factor).astype(out[name].dtype)
    return out
```

```python
from contextlib import ExitStack

import concourse.bass as bass
from concourse import mybir

F32 = mybir.dt.float32
F32R = mybir.dt.float32r
BF16 = mybir.dt.bfloat16
U32 = mybir.dt.uint32
I32 = mybir.dt.int32
ALU = mybir.AluOpType
ACT = mybir.ActivationFunctionType
AX = mybir.AxisListType

P = 128
D = 1024
KT = D // P
SEQ = 512
NS = 8
T = SEQ + NS
HT = T // 2
TT = 5
ROWS = [P, P, P, P, NS]
CONV = 4
NQ, NKV, GRP, HD, WIN = 16, 4, 4, 64, 128
NB = SEQ // WIN
NG, EPG = 4, 8
NE = NG * EPG
FF = D // 2
ALPHA = 2.0 ** 0.25
EPS = 1e-5
BIG = 1e30
CAP = 64
NOV = 16
NBLK = NE + NOV
FARAWAY = 8192
XPW = 3 + SEQ + NS * CONV
XCW = XPW - 3
XS = SEQ + 3
BODY = 6
E_LOOP, E_TAIL = 4, 28
RING = 9
SLOT = 16384
AHEAD = 3

TILES = ([("lx", i) for i in range(8)] + [("k", i) for i in range(2)] + [("v", i) for i in range(2)]
         + [("q", i) for i in range(8)] + [("ly", i) for i in range(8)]
         + [("gl", i) for i in range(4)] + [("lo", i) for i in range(4)]
         + [("gl", i) for i in range(4, 8)] + [("lo", i) for i in range(4, 8)]
         + [("ga", i) for i in range(4)] + [("ao", i) for i in range(4)]
         + [("ga", i) for i in range(4, 8)] + [("ao", i) for i in range(4, 8)]
         + [("wo", i) for i in range(8)])
NT = len(TILES)
FIRST = {kind: min(t for t in range(NT) if TILES[t][0] == kind) for kind in dict(TILES)}
W_IN_COL = {"lx": 0, "ly": D, "q": 2 * D, "k": 3 * D, "v": 3 * D + 256, "gl": 3 * D + 512, "ga": 4 * D + 512}
BROW = {"lx": 0, "ly": 8, "q": 16, "k": 24, "v": 26, "gl": 28, "ga": 36}
R_WCONV, R_BCONV, R_BRG, R_BIG, R_LAM, NVEC = 44, 76, 84, 92, 100, 108

LAST = {"lx": "act", "k": "act", "v": "act", "q": "act", "ly": "act", "gl": "act", "ga": "act",
        "lo": "dve", "ao": "dve", "wo": "act"}

AFTER = {}


def _place(t, *steps):
    AFTER.setdefault(t, []).extend(steps)


for _i in range(8):
    _place(_i + 1, ("gate", _i))
_place(9, ("exp", 0))
_place(10, ("exp", 4), ("sq", 0))
_place(11, ("sq", 4))
_place(12, ("root",), ("kv",))
_place(13, ("oc",), ("scan", 0))
_place(14, ("scan", 4))
_UNITS = [(p, n) for p in range(2) for n in range(NB)]
for _u in range(8):
    _t = 16 if _u == 0 else 21 + 3 * _u
    _place(_t, ("sc", _u, 0))
    _place(_t + 1, ("sc", _u, 1), ("nrm", _u, 0))
    _place(_t + 2, ("nrm", _u, 1), ("tr", _u, 0))
    _place(_t + 3, ("tr", _u, 1))
    _place(_t + 4, ("pv", _u))
_place(20, ("oh",))
_place(21, ("sk", 0))
_place(22, ("sk", 1))
_place(23, ("ss",))
_place(24, ("st",))
_place(25, ("sp",))
STEPS = []
for _t in range(NT):
    STEPS.append(("tile", _t))
    STEPS += AFTER.get(_t, [])


def build(nc, A, O):
    ctx = ExitStack()
    with ctx:
        base = 16512

        def at(name, shape, dt, off):
            return nc.alloc_sbuf_tensor_at(name, shape, dt, offset=base + off)

        def sem(name):
            return ctx.enter_context(nc.semaphore(name))

        KB2 = T * 4
        oA, oB, oC, oD = 0, 33280, 67328, 102144
        oE, oF, oG, oH, oI, oJ = 126720, 139136, 147456, 172032, 188416, 204800
        xTh = at("xTh", [P, KT, T], F32R, oA)
        xTl = at("xTl", [P, KT, T], F32R, oA + KT * KB2)
        qT = at("qT", [P, 8, T], F32, oB)
        attH = at("attH", [P, 8, T], F32R, oB)
        vT = at("vT", [P, 2, T], F32, oB + 6 * KB2)
        gT = at("gT", [P, 8, XCW], F32, oB + 8 * KB2)
        attL = at("attL", [P, 8, T], F32R, oB + 8 * KB2)
        hL = at("hL", [P, 8, XCW], F32, oC)
        recH = at("recH", [P, 8, XCW], F32R, oC)
        aL = at("aL", [P, 8, XCW], F32, oC + 8 * XCW * 4)
        recL = at("recL", [P, 8, XCW], F32R, oC + 8 * XCW * 4)
        mgL = at("mgL", [P, 8, XCW], F32R, oC + 8 * XCW * 4)
        xrow = [at(f"xrow{n}", [P, D], F32, oC + 4096 * n) for n in range(TT)]
        vec = at("vec", [NVEC, P], F32, oC + 4096 * 5)
        st = at("st", [32, D], F32, oC + 4096 * 6)
        xp = at("xp", [P, 8, XPW], F32, oD)
        cK = at("cK", [P, NS, 256], F32, oD)
        kS = at("kS", [P, 2, NS, P], F32, oD + 8192)
        cV = at("cV", [P, NS, 256], F32, oD + 16384)
        m1 = at("m1", [P, 8, T], F32, oD)
        mgH = at("mgH", [P, 8, T], F32R, oD)
        kz = at("kz", [P, 2, 2, T], F32, oE)
        vtok = at("vtok", [P, NB, 256], F32, oE + 4 * KB2)
        mixT = at("mixT", [P, 8, T], F32, oE)
        wrg = at("wrg", [P, 8, P], F32, oF)
        wig = at("wig", [P, 8, P], F32, oF + 4096)
        oc = at("oc", [XPW - SEQ, D], F32, oF)
        qz = at("qz", [P, 16, 32], F32, oF)
        oh = at("oh", [NS + 1, D], F32, oF + 4096)
        sg = at("sg", [P, 4, T], F32, oF)
        raw = [at(f"raw{n}", [P, KT, 256], F32, oG + 8192 * n) for n in range(3)]
        rawL = [at(f"rawL{n}", [P, KT, 256], F32R, oG + 8192 * n) for n in range(3)]
        wh = [at(f"wh{n}", [P, KT, P], F32R, oH + 4096 * n) for n in range(AHEAD + 1)]
        xc = [at(f"xc{n}", [P, XCW], F32, oI + 2176 * n) for n in range(2)]
        si = [at(f"si{n}", [P, XCW], F32, oI + 4352 + 2176 * n) for n in range(2)]
        a2 = at("a2", [P, XCW], F32, oI + 8704)
        kwin = at("kwin", [P, 256], F32, oI + 12288)
        snew = at("snew", [NS, 512], F32, oI + 13312)
        kl = at("kl", [P, 2, P + NS], F32, oI + 10880)
        sS = [at(f"sS{n}", [P, 4, 256], F32, oI + 4096 * n) for n in range(2)]
        pT = at("pT", [P, 2, 2, 512], F32, oI + 8192)
        sSm = at("sSm", [P, 4, P], F32, oI + 8192)
        pTs = at("pTs", [P, 4, P], F32, oI + 10240)
        ident = at("ident", [P, P], F32, oJ)
        mask = at("mask", [P, 256], F32, oJ + 512)
        col = at("col", [P, NVEC], F32, oJ + 1536)
        colh = at("colh", [P, 16], F32, oJ + 1984)
        sk8 = at("sk8", [P, NQ], F32, oJ + 2048)
        sks = at("sks", [P, 1], F32, oJ + 2112)
        h0 = at("h0", [P, 8, NS], F32, oJ + 2176)
        cf = at("cf", [P, 8], F32, oJ + 2432)
        ncf = at("ncf", [P, 8], F32, oJ + 2464)
        lam = at("lam", [P, 4, 8], F32, oJ + 2496)
        mx = at("mx", [P, 2, 4], F32, oJ + 2624)
        nm = at("nm", [P, 2, 4], F32, oJ + 2656)
        es = at("es", [P, 2, 4], F32, oJ + 2688)
        dn = at("dn", [P, 2, 4], F32, oJ + 2720)
        smx = at("smx", [P, 4, 4], F32, oJ + 2752)
        epsT = at("epsT", [P, 1], F32, oJ + 2816)
        yb = at("yb", [P, T], F32, oJ + 3072)
        y2 = at("y2", [P, T], F32, oJ + 3072 + KB2)

        lnG = at("lnG", [P, D], F32, oI)
        lnB = at("lnB", [P, D], F32, oI + 4096)
        xre = [at(f"xre{n}", [P, D], F32, oI + 8192 + 4096 * n) for n in range(2)]
        z1 = [at(f"z1{n}", [P, D], F32, oG + 4096 * n) for n in range(2)]
        x1 = [at(f"x1{n}", [P, D], F32, oG + 8192 + 4096 * n) for n in range(2)]
        x1T = [at(f"x1T{n}", [P, KT, P], F32, oG + 16384 + 4096 * n) for n in range(2)]
        wr = at("wr", [P, KT, NG + NE], F32, oJ + 3072)
        rb = at("rb", [P, NG + NE], F32, oJ + 3072 + 1152)
        st6 = at("st6", [P, 2, 2, 6], F32, oJ + 4480)
        mv = at("mv", [P, 2, 4], F32, oJ + 4608)
        ro = [oH]

        def rt(name, shape, dt=F32):
            n = 1
            for s in shape[1:]:
                n *= s
            t = at(name, shape, dt, ro[0])
            ro[0] += (n * (2 if dt == BF16 else 4) + 31) // 32 * 32
            return t
        lg = rt("lg", [P, TT, NG + NE])
        io4 = rt("io4", [P, NG])
        io32 = rt("io32", [P, NE])
        io128 = rt("io128", [P, P])
        io48 = rt("io48", [P, NBLK])
        tri = rt("tri", [P, P])
        triB = rt("triB", [P, P], BF16)
        oneB = rt("oneB", [P, P], BF16)
        valid = rt("valid", [P, TT])
        tokv = rt("tokv", [P, 2, TT])
        off = rt("off", [P, 1])
        w5 = [rt(f"w5{n}", [P, TT]) for n in range(8)]
        w10 = [rt(f"w10{n}", [P, 2, TT]) for n in range(8)]
        g20 = [rt(f"g20{n}", [P, TT, NG]) for n in range(3)]
        e160 = [rt(f"e160{n}", [P, TT, NE]) for n in range(2)]
        esel = rt("esel", [P, TT, NE])
        hot = rt("hot", [P, 2, TT, NE])
        hotB = rt("hotB", [P, TT, NE], BF16)
        cum = rt("cum", [P, 4, NE])
        ov16 = rt("ov16", [P, NOV, NE])
        assert ro[0] <= oI
        tabG = at("tabG", [P, NBLK], U32, oJ + 4672)
        tabD = at("tabD", [P, NBLK], U32, oJ + 4864)
        tabW = at("tabW", [P, NBLK], F32, oJ + 5056)
        ovT = at("ovT", [P, NOV + 1], I32, oJ + 5248)
        ovf = at("ovf", [P, NOV + 1], F32, oJ + 5344)
        rk = [at(f"rk{n}", [P, P], F32, oJ + 5440 + 512 * n) for n in range(2)]
        bk = [at(f"bk{n}", [P, 3, NBLK], F32, oJ + 6464 + 576 * n) for n in range(2)]
        slot = [at(f"slot{n}", [P, 8, 512], F32, SLOT * n) for n in range(RING)]
        xg = [at(f"xg{n}", [P, 512], F32, oG + 2048 * n) for n in range(BODY)]
        xt = [at(f"xt{n}", [P, 512], F32, oG + 12288 + 2048 * n) for n in range(3)]
        gu = [at(f"gu{n}", [P, 512], F32, oG + 18432 + 2048 * n) for n in range(3)]
        ys = [at(f"ys{n}", [P, 512], F32, oH + 8192 + 2048 * n) for n in range(3)]
        sgm = [at(f"sgm{n}", [P, 4, CAP], F32, oH + 1024 * n) for n in range(3)]
        hT = [at(f"hT{n}", [P, 4, CAP], F32, oH + 3072 + 1024 * n) for n in range(3)]
        idG = [at(f"idG{n}", [P, 1], U32, oH + 6144 + 32 * n) for n in range(BODY)]
        idD = [at(f"idD{n}", [P, 1], U32, oH + 6336 + 32 * n) for n in range(3)]
        f0 = [at(f"f0{n}", [P, D], F32, 4096 * n) for n in range(2)]
        f1 = [at(f"f1{n}", [P, D], F32, 8192 + 4096 * n) for n in range(2)]
        z2 = [at(f"z2{n}", [P, D], F32, 16384 + 4096 * n) for n in range(2)]
        y_out = [at(f"yout{n}", [P, D], F32, 24576 + 4096 * n) for n in range(2)]
        xr2 = [at(f"xr2{n}", [P, D], F32, 32768 + 4096 * n) for n in range(2)]
        ln2G = at("ln2G", [P, D], F32, oI)
        ln2B = at("ln2B", [P, D], F32, oI + 4096)

        pair = [ctx.enter_context(nc.psum_tensor(f"ps{n}", [P, 2, 512], F32)) for n in range(4)]
        flat = [p[:, :, :].rearrange("p a b -> p (a b)") for p in pair]
        bank = [pair[n // 2][:, n % 2, :] for n in range(8)]

        x1_half = nc.dram_tensor("x1_half", [2 * T, 512], F32, kind="Internal").ap()
        ff_half = nc.dram_tensor("ff_half", [4 * T, 512], F32, kind="Internal").ap()
        x1_rows = x1_half.rearrange("(t h) n -> t (h n)", h=2)
        ff_rows = ff_half.rearrange("(k t h) n -> k t (h n)", k=2, h=2)

        s_vec, s_st, s_wg, s_snk, s_snr = sem("vec_loaded"), sem("state_loaded"), sem("gate_w_loaded"), sem("sinks_loaded"), sem("row_sinks_loaded")
        s_x = [sem(f"x_loaded{n}") for n in range(TT)]
        s_raw = [sem(f"raw_loaded{n}") for n in range(3)]
        s_cst = sem("constants_built")
        s_xT = sem("x_transposed")
        s_xh, s_xl = sem("x_hi"), sem("x_lo")
        s_vT, s_col = sem("vectors_transposed"), sem("vectors_in_columns")
        s_stT, s_stc = sem("states_transposed"), sem("states_placed")
        s_cf = sem("decay_ready")
        s_lamE = sem("lambda_exp")
        s_lam = sem("lambda_ready")
        s_hi, s_lo = sem("w_hi"), sem("w_lo")
        s_proj = sem("tile_projected")
        s_eva, s_evd = sem("tile_read_by_act"), sem("tile_read_by_dve")
        s_cv = sem("conv_done")
        s_gate = sem("gates_projected")
        s_sig = sem("gates_activated")
        s_gx = sem("gated_input")
        s_a = sem("decay_exp")
        s_om = sem("one_minus_a2")
        s_rt = sem("root_taken")
        s_h = sem("h_scanned")
        s_kvT, s_kva, s_kvd = sem("kv_transposed"), sem("v_tokens"), sem("k_window")
        s_ocT, s_ocv, s_ohT, s_ohv = sem("conv_state_T"), sem("conv_state"), sem("h_T"), sem("h_state")
        s_kv_out = sem("kv_stored")
        s_oc_out, s_oh_out = sem("conv_stored"), sem("h_stored")
        s_copy = sem("cache_copied")
        s_ck, s_cv_ld = sem("cache_k_loaded"), sem("cache_v_loaded")
        s_sc, s_ttr, s_nm = sem("scores"), sem("scores_masked"), sem("neg_max")
        s_ex, s_nrm = sem("exps"), sem("probs")
        s_tr, s_pa, s_pd = sem("probs_T"), sem("probs_T_by_act"), sem("probs_T_by_dve")
        s_pv, s_atth, s_attl = sem("attended"), sem("att_hi"), sem("att_lo")
        s_skT, s_ska, s_skd = sem("cache_T"), sem("cache_T_act"), sem("cache_T_dve")
        s_qz, s_ss, s_sm, s_se, s_sn = sem("sample_q"), sem("sample_scores"), sem("sample_max"), sem("sample_exp"), sem("sample_probs")
        s_spT, s_spc, s_spv, s_sah, s_sal = sem("sample_pT"), sem("sample_pT_copied"), sem("sample_pv"), sem("sample_att_hi"), sem("sample_att_lo")
        s_y, s_yq, s_yt, s_rec = sem("ly_read"), sem("gelu_inner"), sem("gelu_tanh"), sem("rec_ready")
        s_mg = sem("merged")
        s_ln = sem("ln1_loaded")
        s_mT, s_z, s_sd, s_xn = sem("mix_T"), sem("ln1_stats"), sem("ln1_root"), sem("ln1_scaled")
        s_x1 = sem("x1_ready")
        s_x1o = [sem(f"x1_stored{n}") for n in range(2)]
        s_x1T, s_x1c, s_lg, s_lgc = sem("x1_T"), sem("x1_T_copied"), sem("logits"), sem("logits_kept")
        s_rd, s_re = sem("route_differences"), sem("route_exps")
        s_hot, s_pre, s_oh10, s_tab, s_tabc = sem("one_hots"), sem("ranks"), sem("slot_one_hots"), sem("tables"), sem("tables_kept")
        s_rcst, s_turn = sem("router_constants"), sem("pool_turn")
        s_wx = [sem(f"chunk_loaded{n}") for n in range(RING)]
        s_ig, s_id = sem("gather_index"), sem("scatter_index")
        s_g = [sem(f"gathered{n}") for n in range(BODY)]
        s_sct = [sem(f"scattered{n}") for n in range(3)]
        s_xtp, s_xte = sem("block_T"), sem("block_T_copied")
        s_gup, s_gue = sem("gate_up"), sem("gate_up_copied")
        s_gt, s_sgm, s_h1, s_hh = sem("gate_up_T"), sem("gate_sigmoid"), sem("gate_silu"), sem("hidden")
        s_yp, s_ye = sem("block_out"), sem("block_out_scaled")
        s_ov = {n: sem("ov_" + n) for n in ("w", "ix", "g", "xt", "xe", "gu", "ge", "gt", "sg", "h1", "h", "y", "ye", "sc", "free")}
        s_l2 = sem("ln2_loaded")
        s_f = [sem(f"ff_loaded{n}") for n in range(2)]
        s_z2, s_sd2, s_y2, s_y3 = sem("ln2_stats"), sem("ln2_root"), sem("ln2_scaled"), sem("y_ready")
        s_yo = [sem(f"y_stored{n}") for n in range(2)]
        d_c, p_c = sem("dve_order"), sem("pool_order")

        block = ctx.enter_context(nc.Block())

        def dmas(hc):
            return {"q": 4, "ao": 4}.get(TILES[2 * hc][0], 1)

        def raw_full(t):
            hc = t // 2
            return s_raw[hc % 3], 16 * sum(dmas(n) for n in range(hc % 3, hc + 1, 3))

        def emptied(t):
            who = LAST[TILES[t][0]]
            n = sum(LAST[TILES[m][0]] == who for m in range(t + 1))
            return (s_eva if who == "act" else s_evd), n

        def wcol(t, buf):
            return buf[(t // 2) % 3][:, :, (t % 2) * P:(t % 2 + 1) * P]

        def whi(t):
            return wh[t % (AHEAD + 1)][:, :, :]

        def halves(ap):
            return ap.rearrange("p (a b) -> p a b", a=2)

        def sample_cols(ap):
            return ap[:, SEQ + 3:XCW + 3:CONV] if False else ap[:, XS:XCW:CONV]

        NUNIT = len(_UNITS)

        def uses(i, c, r):
            return i * (BODY // r) + c // r + 1

        @block.sync
        def _(sp):
            sp.dma_start(xrow[0][:, :], A["x_prompt"][0, 0:P, :]).then_inc(s_x[0], 16)

            w_in = A["w_in"].rearrange("(k p) n -> p k n", p=P)
            w_q = A["w_in"][:, 2 * D:3 * D].rearrange("(k p) (P a m) -> p k P a m", p=P, P=2, a=2)
            w_lo = A["w_lru_out"].rearrange("(k p) n -> p k n", p=P)
            w_ao = A["w_attn_out"].rearrange("(P a h c) n -> P a c h n", P=2, a=2, h=4)
            w_o = A["w_o"].rearrange("(k p) n -> p k n", p=P)

            def half_chunk(hc):
                kind, i = TILES[2 * hc]
                dst, s = raw[hc % 3], s_raw[hc % 3]
                if hc >= 3:
                    sp.wait_ge(s_proj, 2 * (hc - 3) + 2)
                if kind == "q":
                    p2, m = i // 4, (i % 4) // 2
                    for a in range(2):
                        for h in range(2):
                            sp.dma_start(dst[:, :, h * P + a * HD:h * P + (a + 1) * HD],
                                         w_q[:, :, p2, a, m * P + h * HD:m * P + (h + 1) * HD]).then_inc(s, 16)
                elif kind == "ao":
                    for p2 in range(2):
                        for a in range(2):
                            sp.dma_start(dst[a * HD:(a + 1) * HD, 4 * p2:4 * p2 + 4, :],
                                         w_ao[p2, a, :, :, i * P:i * P + 256]).then_inc(s, 16)
                else:
                    w = {"lo": w_lo, "wo": w_o}.get(kind, w_in)
                    c = W_IN_COL.get(kind, 0) + i * P
                    sp.dma_start(dst[:, :, :], w[:, :, c:c + 256]).then_inc(s, 16)

            for n in range(1, 4):
                sp.dma_start(xrow[n][:, :], A["x_prompt"][0, n * P:(n + 1) * P, :]).then_inc(s_x[n], 16)
            sp.dma_start(xrow[4][0:NS, :], A["x_sample"][:, 0, :]).then_inc(s_x[4], 16)
            half_chunk(0)
            half_chunk(1)
            sp.wait_ge(s_cst, 2)
            for dst, src in ((wrg, A["w_rg"]), (wig, A["w_ig"])):
                blocks = src.rearrange("(k a) i j -> a i k j", a=2)
                for a in range(2):
                    sp.dma_start(dst[a * HD:(a + 1) * HD, :, a * HD:(a + 1) * HD], blocks[a, :, :, :]).then_inc(s_wg, 16)
            sp.dma_start(sk8[:, :], A["sinks"].rearrange("(a n) -> a n", a=1).to_broadcast([P, NQ])).then_inc(s_snk, 16)

            def chunk(c, e, j):
                n = 3 * j + c
                if c < 2:
                    src = A["w_gate" if c == 0 else "w_up"][bass.ds(e, 1), :, :]
                    src = src.rearrange("e (h p j) f -> p (e h) (j f)", h=2, p=P)
                    dst = slot[n][:, :, :].rearrange("p (h j) f -> p h (j f)", h=2)
                else:
                    src = A["w_down"][bass.ds(e, 1), :, :].rearrange("e (p j) d -> p (e j d)", p=P)
                    dst = slot[n][:, :, :].rearrange("p a b -> p (a b)")
                sp.dma_start(dst, src).then_inc(s_wx[n], 16)

            for hc in range(2, NT // 2):
                half_chunk(hc)
                if hc == 30:
                    sp.wait_ge(s_proj, 56)
                    chunk(0, 0, 0)
                    chunk(1, 0, 0)
                if hc == 32:
                    sp.wait_ge(s_proj, 60)
                    chunk(2, 0, 0)
                    chunk(0, 1, 1)
            sp.wait_ge(s_pv, NUNIT)
            for dst, src in ((lnG, A["ln1_g"]), (lnB, A["ln1_b"])):
                sp.dma_start(dst[:, :], src.rearrange("(a n) -> a n", a=1).to_broadcast([P, D])).then_inc(s_ln, 16)
            sp.wait_ge(s_rec, 8)
            sp.dma_start(wr[:, :, 0:NG], A["w_group"].rearrange("(k p) n -> p k n", p=P)).then_inc(s_ln, 16)
            sp.dma_start(wr[:, :, NG:], A["w_router"].rearrange("(k p) n -> p k n", p=P)).then_inc(s_ln, 16)
            sp.dma_start(rb[:, 0:NG], A["b_group"].rearrange("(a n) -> a n", a=1).to_broadcast([P, NG])).then_inc(s_ln, 16)
            sp.dma_start(rb[:, NG:], A["b_router"].rearrange("(a n) -> a n", a=1).to_broadcast([P, NE])).then_inc(s_ln, 16)

            def x_again(n):
                src = A["x_prompt"][0, n * P:(n + 1) * P, :] if n < 4 else A["x_sample"][:, 0, :]
                sp.dma_start(xre[n % 2][0:ROWS[n], :], src).then_inc(s_x[n], 16)

            x_again(0)
            x_again(1)
            sp.wait_ge(s_proj, NT)
            for e, c in ((1, 1), (1, 2), (2, 0)):
                chunk(c, e, e)
            for n in range(TT):
                if n + 2 < TT:
                    sp.wait_ge(s_z, n + 1)
                    x_again(n + 2)
                if n == TT - 1:
                    sp.wait_ge(s_mT, TT)
                    chunk(1, 2, 2)
                    chunk(2, 2, 2)
                sp.wait_ge(s_x1, n + 1)
                sp.dma_start(x1_rows[n * P:n * P + ROWS[n], :], x1[n % 2][0:ROWS[n], :]).then_inc(s_x1o[n % 2], 16)

            def next_chunks(i, c):
                e = i * BODY + c
                sp.wait_ge(s_gup, e - 2)
                chunk(0, e, c % 3)
                chunk(1, e, c % 3)
                sp.wait_ge(s_yp, e - 2)
                chunk(2, e, c % 3)

            for c in range(3, E_LOOP):
                next_chunks(0, c)
            with sp.Fori(0, (E_TAIL - E_LOOP) // BODY) as i:
                for c in range(E_LOOP, E_LOOP + BODY):
                    next_chunks(i, c)
            for c in range(E_TAIL, NE):
                next_chunks(0, c)

            sp.wait_ge(s_tabc, 4)
            n_over = sp.value_load(ovT[0:1, NOV:NOV + 1], min_val=0, max_val=NOV)
            with sp.If(n_over > 0):
                with sp.Fori(0, NOV) as i:
                    ex = sp.value_load(ovT[0:1, bass.ds(i, 1)], min_val=0, max_val=NE - 1)
                    sp.wait_ge(s_ov["free"], i + 1)
                    for c in range(2):
                        src = A["w_gate" if c == 0 else "w_up"][bass.ds(ex, 1), :, :]
                        sp.dma_start(slot[c][:, :, :].rearrange("p (h j) f -> p h (j f)", h=2),
                                     src.rearrange("e (h p j) f -> p (e h) (j f)", h=2, p=P)).then_inc(s_ov["w"], 16)
                    sp.dma_start(slot[2][:, :, :].rearrange("p a b -> p (a b)"),
                                 A["w_down"][bass.ds(ex, 1), :, :].rearrange("e (p j) d -> p (e j d)", p=P)).then_inc(s_ov["w"], 16)
                sp.wait_ge(s_ov["free"], NOV + 1)

            for dst, src in ((ln2G, A["ln2_g"]), (ln2B, A["ln2_b"])):
                sp.dma_start(dst[:, :], src.rearrange("(a n) -> a n", a=1).to_broadcast([P, D])).then_inc(s_l2, 16)
            for j in range(3):
                sp.wait_ge(s_sct[j], 16 * len(range(j, NE, 3)))

            def last_in(n):
                r, k = ROWS[n], n % 2
                sp.dma_start(xr2[k][0:r, :], x1_rows[n * P:n * P + r, :]).then_inc(s_f[k], 16)
                sp.dma_start(f0[k][0:r, :], ff_rows[0, n * P:n * P + r, :]).then_inc(s_f[k], 16)
                sp.dma_start(f1[k][0:r, :], ff_rows[1, n * P:n * P + r, :]).then_inc(s_f[k], 16)

            last_in(0)
            last_in(1)
            for n in range(TT):
                if n + 2 < TT:
                    sp.wait_ge(s_z2, n + 1)
                    last_in(n + 2)
                sp.wait_ge(s_y3, n + 1)
                dst = O["y_prompt"][0, n * P:(n + 1) * P, :] if n < 4 else O["y_sample"][:, 0, :]
                sp.dma_start(dst, y_out[n % 2][0:ROWS[n], :]).then_inc(s_yo[n % 2], 16)
            sp.wait_ge(s_yo[0], 48)
            sp.wait_ge(s_yo[1], 32)
            sp.wait_ge(s_x1o[0], 48)
            sp.wait_ge(s_x1o[1], 32)
            sp.wait_ge(s_kv_out, 64)
            sp.wait_ge(s_copy, 32)
            sp.wait_ge(s_oc_out, 16 * 9)
            sp.wait_ge(s_oh_out, 32)

        @block.gpsimd
        def _(pool):
            gp = nc.gpsimd
            pc = [0]

            def link(ins):
                pc[0] += 1
                ins.then_inc(p_c, 1)
                pool.wait_ge(p_c, pc[0])

            def turn():
                pool.sem_inc(s_turn, 1)

            gp.memset(wrg[:, :, :], 0.0).then_inc(s_cst, 1)
            gp.memset(wig[:, :, :], 0.0).then_inc(s_cst, 1)
            link(gp.memset(ident[:, :], 0.0))
            gp.affine_select(out=ident[:, :], in_=ident[:, :], compare_op=ALU.not_equal, fill=1.0, base=0,
                             pattern=[[-1, P]], channel_multiplier=1).then_inc(s_cst, 1)
            gp.memset(xp[:, :, 0:3], 0.0).then_inc(s_cst, 1)
            gp.memset(epsT[:, :], EPS).then_inc(s_cst, 1)
            link(gp.memset(mask[:, :], 0.0))
            link(gp.affine_select(out=mask[:, :], in_=mask[:, :], compare_op=ALU.is_gt, fill=-BIG * 8, base=0,
                                  pattern=[[1, 256]], channel_multiplier=-1))
            gp.affine_select(out=mask[:, :], in_=mask[:, :], compare_op=ALU.is_ge, fill=-BIG * 8, base=WIN,
                             pattern=[[-1, 256]], channel_multiplier=1).then_inc(s_cst, 1)
            pool.wait_ge(s_cst, 6)
            gp.memset(kz[0:HD, :, 1, :], 0.0).then_inc(s_cst, 1)
            pool.wait_ge(s_cst, 7)
            gp.memset(kz[HD:P, :, 0, :], 0.0).then_inc(s_cst, 1)
            pool.wait_ge(s_cst, 8)
            link(gp.memset(sks[:, :], 0.0))
            for g in range(4):
                src = A["sinks"][(g % 2) * 8:(g % 2) * 8 + 8].rearrange("(n a) -> n a", a=1)
                with nc.allow_non_contiguous_dma(reason="eight words"):
                    pool.dma_start(sks[32 * g:32 * g + 8, :], src).then_inc(s_snr, 16)
            pool.dma_start(O["k_win_sample"][:, 0:WIN - 1, :, :].rearrange("b w k d -> b (w k d)"),
                           A["cache_k"][:, 1:WIN, :, :].rearrange("b w k d -> b (w k d)")).then_inc(s_copy, 16)
            pool.dma_start(O["v_win_sample"][:, 0:WIN - 1, :, :].rearrange("b w k d -> b (w k d)"),
                           A["cache_v"][:, 1:WIN, :, :].rearrange("b w k d -> b (w k d)")).then_inc(s_copy, 16)
            pool.wait_ge(s_kva, 1)
            pool.dma_start(O["v_win_prompt"][0, :, :, :].rearrange("w k d -> w (k d)"), vtok[:, NB - 1, :]).then_inc(s_kv_out, 16)
            pool.wait_ge(s_kvd, 2)
            pool.dma_start(O["k_win_prompt"][0, :, :, :].rearrange("w k d -> w (k d)"), kwin[:, :]).then_inc(s_kv_out, 16)
            pool.dma_start(O["k_win_sample"][:, WIN - 1, :, :].rearrange("b k d -> b (k d)"), snew[:, 0:256]).then_inc(s_kv_out, 16)
            pool.dma_start(O["v_win_sample"][:, WIN - 1, :, :].rearrange("b k d -> b (k d)"), snew[:, 256:512]).then_inc(s_kv_out, 16)
            pool.wait_ge(s_cv, 8)
            pool.wait_ge(s_ocT, 1)
            pool.dma_start(cK[:, :, :], A["cache_k"].rearrange("b w k d -> w b (k d)")).then_inc(s_ck, 16)
            pool.dma_start(cV[1:P, :, :], A["cache_v"][:, 1:WIN, :, :].rearrange("b w k d -> w b (k d)")).then_inc(s_cv_ld, 16)
            pool.dma_start(cV[0:1, :, :], snew[:, 256:512]).then_inc(s_cv_ld, 16)
            pool.wait_ge(s_ocv, 2)
            pool.dma_start(O["conv_prompt"][0, :, :], oc[0:3, :]).then_inc(s_oc_out, 16)
            for b in range(NS):
                pool.dma_start(O["conv_sample"][b, :, :], oc[4 + 4 * b:7 + 4 * b, :]).then_inc(s_oc_out, 16)
            pool.wait_ge(s_oc_out, 16 * 9)
            gp.memset(qz[:, :, :], 0.0).then_inc(s_qz, 1)
            pool.wait_ge(s_ohv, 2)
            pool.dma_start(O["h_prompt"], oh[0:1, :]).then_inc(s_oh_out, 16)
            pool.dma_start(O["h_sample"], oh[1:NS + 1, :]).then_inc(s_oh_out, 16)

            pool.wait_ge(s_proj, NT)
            gp.memset(lg[:, :, :], 0.0).then_inc(s_rcst, 1)
            gp.iota(io4[:, :], [[1, NG]], base=0, channel_multiplier=0, allow_small_or_imprecise_dtypes=True).then_inc(s_rcst, 1)
            gp.iota(io32[:, :], [[1, NE]], base=0, channel_multiplier=0, allow_small_or_imprecise_dtypes=True).then_inc(s_rcst, 1)
            gp.iota(io128[:, :].rearrange("p (a b) -> p a b", a=2), [[0, 2], [1, CAP]], base=0, channel_multiplier=0,
                    allow_small_or_imprecise_dtypes=True).then_inc(s_rcst, 1)
            gp.iota(io48[:, :], [[1, NBLK]], base=0, channel_multiplier=0, allow_small_or_imprecise_dtypes=True).then_inc(s_rcst, 1)
            gp.iota(tokv[:, :, :], [[0, 2], [2 * P, TT]], base=-FARAWAY, channel_multiplier=2,
                    allow_small_or_imprecise_dtypes=True).then_inc(s_rcst, 1)
            link(gp.memset(tri[:, :], 1.0))
            link(gp.affine_select(out=tri[:, :], in_=tri[:, :], compare_op=ALU.is_gt, fill=0.0, base=0,
                                  pattern=[[1, P]], channel_multiplier=-1))
            gp.tensor_copy(triB[:, :], tri[:, :]).then_inc(s_rcst, 1)
            gp.memset(oneB[:, :], 1.0).then_inc(s_rcst, 1)
            link(gp.memset(valid[:, :], 1.0))
            gp.affine_select(out=valid[:, TT - 1:TT], in_=valid[:, TT - 1:TT], compare_op=ALU.is_gt, fill=0.0, base=NS,
                             pattern=[[0, 1]], channel_multiplier=-1).then_inc(s_rcst, 1)
            pool.wait_ge(s_rcst, 9)
            gp.memset(off[0:CAP, :], float(FARAWAY)).then_inc(s_rcst, 1)
            pool.wait_ge(s_rcst, 10)
            gp.memset(off[CAP:P, :], float(FARAWAY + 1)).then_inc(s_rcst, 1)

            pool.wait_ge(s_rcst, 11)
            for n in range(TT):
                r = ROWS[n]
                pool.wait_ge(s_ln, 96)
                if n == TT - 1:
                    pool.wait_ge(s_x1, n)
                pool.wait_ge(s_xn, n + 1)
                if n >= 2:
                    pool.wait_ge(s_x1o[n % 2], 16 * (n // 2))
                    pool.wait_ge(s_x1T, n - 1)
                gp.tensor_tensor(x1[n % 2][0:r, :], z1[n % 2][0:r, :], lnB[0:r, :], ALU.add).then_inc(s_x1, 1)

            pool.wait_ge(s_x1, TT)
            pool.wait_ge(s_tabc, 4)
            pool.wait_ge(s_x1o[0], 48)
            pool.wait_ge(s_x1o[1], 32)
            pool.wait_ge(s_lg, TT)
            for j in range(BODY):
                link(gp.memset(xg[j][:, :], 0.0))

            def fetch(dst, index, signal):
                pool.indirect_dma_start(out=dst[:, :], out_offset=None, in_=x1_half,
                                        in_offset=bass.IndirectOffsetOnAxis(ap=index[:, 0:1], axis=0),
                                        bounds_check=2 * T - 1, oob_is_err=False).then_inc(signal, 16)

            def store(src, index, signal):
                pool.indirect_dma_start(out=ff_half, out_offset=bass.IndirectOffsetOnAxis(ap=index[:, 0:1], axis=0),
                                        in_=src[:, :], in_offset=None,
                                        bounds_check=4 * T - 1, oob_is_err=False).then_inc(signal, 16)

            def gather(i, c, first=False):
                e, j = i * BODY + c, c % BODY
                if not first:
                    pool.wait_ge(s_xtp, e - 5)
                gp.tensor_copy(idG[j][:, :], tabG[:, bass.ds(e, 1)]).then_inc(s_ig, 1)
                pool.wait_ge(s_ig, e + 1)
                turn()
                fetch(xg[j], idG[j], s_g[j])

            def scatter(i, c):
                e, j = i * BODY + c, c % 3
                if c >= 3:
                    pool.wait_ge(s_sct[j], uses(i, c - 3, 3) * 16)
                gp.tensor_copy(idD[j][:, :], tabD[:, bass.ds(e, 1)]).then_inc(s_id, 1)
                pool.wait_ge(s_id, e + 1)
                pool.wait_ge(s_ye, e + 1)
                turn()
                store(ys[j], idD[j], s_sct[j])

            for e in range(4):
                gather(0, e, True)
            for e in range(E_LOOP):
                gather(0, e + 4, e < 2)
                if e:
                    scatter(0, e - 1)
            with pool.Fori(0, (E_TAIL - E_LOOP) // BODY) as i:
                for c in range(E_LOOP, E_LOOP + BODY):
                    gather(i, c + 4)
                    scatter(i, c - 1)
            for e in range(E_TAIL, NE + 1):
                scatter(0, e - 1)

            n_over = pool.value_load(ovT[0:1, NOV:NOV + 1], min_val=0, max_val=NOV)
            with pool.If(n_over > 0):
                for j in range(3):
                    pool.wait_ge(s_sct[j], 16 * len(range(j, NE, 3)))
                pool.sem_inc(s_ov["free"], 1)
                with pool.Fori(0, NOV) as i:
                    pool.wait_ge(s_ov["free"], i + 1)
                    gp.tensor_copy(idG[0][:, :], tabG[:, bass.ds(i + NE, 1)]).then_inc(s_ov["ix"], 1)
                    gp.tensor_copy(idD[0][:, :], tabD[:, bass.ds(i + NE, 1)]).then_inc(s_ov["ix"], 1)
                    pool.wait_ge(s_ov["ix"], i * 2 + 2)
                    turn()
                    fetch(xg[0], idG[0], s_ov["g"])
                    pool.wait_ge(s_ov["ye"], i + 1)
                    turn()
                    store(ys[0], idD[0], s_ov["sc"])
                    pool.wait_ge(s_ov["sc"], i * 16 + 16)
                    pool.sem_inc(s_ov["free"], 1)

            for n in range(TT):
                r = ROWS[n]
                pool.wait_ge(s_l2, 32)
                pool.wait_ge(s_y2, n + 1)
                if n == TT - 1:
                    pool.wait_ge(s_y3, n)
                if n >= 2:
                    pool.wait_ge(s_yo[n % 2], 16 * (n // 2))
                gp.tensor_tensor(y_out[n % 2][0:r, :], z2[n % 2][0:r, :], ln2B[0:r, :], ALU.add).then_inc(s_y3, 1)

        @block.tensor
        def _(pe):
            mm = nc.tensor.matmul

            def passes(out_of, hi, lo, rhs_h, rhs_l):
                last = None
                for k in range(KT):
                    for n, (w, x) in enumerate(((hi, rhs_h), (hi, rhs_l), (lo, rhs_h))):
                        for a in range(2):
                            last = mm(out_of[:, a, 0:HT], w[:, k, :], x[:, k, a * HT:(a + 1) * HT],
                                      start=(k == 0 and n == 0), stop=(k == KT - 1 and n == 2))
                return last

            pe.wait_ge(s_cst, 3)
            for n in range(TT):
                r = ROWS[n]
                pe.wait_ge(s_x[n], 16)
                if n >= 2:
                    pe.wait_ge(s_xl, n - 1)
                for k in range(KT):
                    last = nc.tensor.transpose(flat[n % 2][:, k * P:k * P + r], xrow[n][0:r, k * P:(k + 1) * P], ident[0:r, 0:r])
                last.then_inc(s_xT, 1)
            pe.wait_ge(s_vec, 16 * 11)
            nc.tensor.transpose(bank[4][:, 0:NVEC], vec[:, :], ident[0:NVEC, 0:NVEC]).then_inc(s_vT, 1)
            pe.wait_ge(s_st, 32)
            for k in range(KT):
                last = nc.tensor.transpose(bank[5][:, k * 32:(k + 1) * 32], st[:, k * P:(k + 1) * P], ident[0:32, 0:32])
            last.then_inc(s_stT, 1)

            def tile(t):
                kind, i = TILES[t]
                rhs_h, rhs_l = {"lo": (recH, recL), "ao": (attH, attL), "wo": (mgH, mgL)}.get(kind, (xTh, xTl))
                if t == 0:
                    pe.wait_ge(s_xl, TT)
                if kind == "lo" and i == 0:
                    pe.wait_ge(s_rec, 8)
                if kind == "ao" and i == 0:
                    pe.wait_ge(s_attl, NUNIT)
                    pe.wait_ge(s_sal, 2)
                    pe.wait_ge(s_sah, 2)
                if kind == "wo" and i == 0:
                    pe.wait_ge(s_mg, 8)
                pe.wait_ge(s_hi, t + 1)
                pe.wait_ge(s_lo, t + 1)
                if t >= 2:
                    pe.wait_ge(*emptied(t - 2))
                passes(pair[t % 2], wh[t % (AHEAD + 1)], wcol(t, rawL), rhs_h, rhs_l).then_inc(s_proj, 1)

            def gate(i):
                if i == 0:
                    pe.wait_ge(s_wg, 64)
                    pe.wait_ge(s_stc, 2)
                    pe.wait_ge(s_col, 1)
                else:
                    pe.wait_ge(s_sig, 3 * i - 1)
                pe.wait_ge(s_cv, i + 1)
                for w, out in ((wrg, pair[2]), (wig, pair[3])):
                    for a in range(2):
                        last = mm(out[:, a, 0:XCW // 2], w[:, i, :], xc[i % 2][:, a * (XCW // 2):(a + 1) * (XCW // 2)],
                                  start=True, stop=True)
                last.then_inc(s_gate, 1)

            def kv():
                pe.wait_ge(s_sig, 3 * 7 + 2)
                pe.wait_ge(*emptied(11))
                for n in range(NB):
                    for p2 in range(2):
                        nc.tensor.transpose(flat[3][:, n * 256 + p2 * P:n * 256 + (p2 + 1) * P], vT[:, p2, n * P:(n + 1) * P], ident[:, :])
                for p2 in range(2):
                    nc.tensor.transpose(bank[4][:, p2 * P:(p2 + 1) * P], kl[:, p2, 0:P], ident[:, :])
                    nc.tensor.transpose(bank[5][0:NS, p2 * P:(p2 + 1) * P], kl[:, p2, P:P + NS], ident[:, :])
                    last = nc.tensor.transpose(bank[5][0:NS, 256 + p2 * P:256 + (p2 + 1) * P], vT[:, p2, SEQ:T], ident[:, :])
                last.then_inc(s_kvT, 1)

            def conv_state():
                pe.wait_ge(s_kvd, 2)
                for k in range(KT):
                    last = nc.tensor.transpose(flat[2][0:XPW - SEQ, k * P:(k + 1) * P], xp[:, k, SEQ:XPW], ident[:, :])
                last.then_inc(s_ocT, 1)

            def h_state():
                pe.wait_ge(s_h, 16)
                pe.wait_ge(s_ttr, 8)
                for k in range(KT):
                    last = nc.tensor.transpose(flat[2][0:NS + 1, k * P:(k + 1) * P], hL[:, k, SEQ - 1:T], ident[:, :])
                last.then_inc(s_ohT, 1)

            def scores(u, par):
                p2, n = _UNITS[u]
                if par == 0:
                    if n == 0:
                        pe.wait_ge(*emptied(FIRST["q"] + 4 * p2 + 3))
                    if u == 0:
                        pe.wait_ge(s_ocv, 2)
                    elif u == 1:
                        pe.wait_ge(s_ohv, 2)
                        pe.wait_ge(s_sm, 1)
                    else:
                        pe.wait_ge(s_ttr, 4 * 2 * u)
                else:
                    pe.wait_ge(s_ttr, 4 * (2 * u + 1))
                lo = 0 if n else P
                for h in range(GRP):
                    last = mm(pair[2][:, h // 2, (h % 2) * 256 + lo:(h % 2) * 256 + 256], qT[:, 4 * p2 + h, n * P:(n + 1) * P],
                              kz[:, p2, par, (n - 1) * P + lo:(n + 1) * P], start=True, stop=True)
                last.then_inc(s_sc, 1)

            def probs_t(u, par):
                p2, n = _UNITS[u]
                pe.wait_ge(s_nrm, 4 * (2 * u + par + 1))
                m = 2 * u + par
                if m == 0:
                    pe.wait_ge(s_kva, 1)
                elif m == 2:
                    pe.wait_ge(s_sah, 2)
                    pe.wait_ge(s_sal, 2)
                    pe.wait_ge(s_spc, 1)
                if u >= 1 and par == 0:
                    pe.wait_ge(s_attl, u)
                if m >= 1:
                    pe.wait_ge(s_pa, m)
                    pe.wait_ge(s_pd, m)
                for kt in range(2):
                    if n == 0 and kt == 0:
                        continue
                    for h in range(GRP):
                        to = 6 + (kt if n else h // 2)
                        last = nc.tensor.transpose(bank[to][:, h * P:(h + 1) * P], sS[par][:, h, kt * P:(kt + 1) * P], ident[:, :])
                last.then_inc(s_tr, 1)

            def attend(u):
                p2, n = _UNITS[u]
                pe.wait_ge(s_pa, 2 * u + 2)
                pe.wait_ge(s_pd, 2 * u + 2)
                kts = (1,) if n == 0 else (0, 1)
                for kt in kts:
                    for par in range(2):
                        last = mm(bank[6][par * HD:(par + 1) * HD, :], vtok[:, n - 1 + kt, (2 * p2 + par) * HD:(2 * p2 + par + 1) * HD],
                                  pT[:, par, kt, :], start=(kt == kts[0]), stop=(kt == 1))
                last.then_inc(s_pv, 1)

            def cache_t(r):
                if r == 0:
                    pe.wait_ge(s_ck, 16)
                    pe.wait_ge(s_attl, 1)
                    pe.wait_ge(s_pd, 2)
                else:
                    pe.wait_ge(s_ska, 1)
                    pe.wait_ge(s_skd, 1)
                for b in range(4 * r, 4 * r + 4):
                    for p2 in range(2):
                        last = nc.tensor.transpose(bank[6 + p2][:, (b % 4) * P:(b % 4 + 1) * P], cK[:, b, p2 * P:(p2 + 1) * P], ident[:, :])
                last.then_inc(s_skT, 1)

            def sample_scores():
                pe.wait_ge(s_skd, 6)
                pe.wait_ge(s_ska, 2)
                pe.wait_ge(s_qz, 5)
                pe.wait_ge(s_ohv, 2)
                for m in range(16):
                    last = mm(bank[4][32 * (m % 4):32 * (m % 4) + 32, (m // 4) * P:(m // 4 + 1) * P], qz[:, m, :],
                              kS[:, m % 2, m // 2, :], start=True, stop=True)
                last.then_inc(s_ss, 1)

            def sample_t():
                pe.wait_ge(s_sn, 4)
                for m in range(4):
                    last = nc.tensor.transpose(bank[7][:, m * P:(m + 1) * P], sSm[:, m, :], ident[:, :])
                last.then_inc(s_spT, 1)

            def sample_pv():
                pe.wait_ge(s_spc, 1)
                pe.wait_ge(s_cv_ld, 32)
                for m in range(16):
                    last = mm(bank[6][:, m * 8:(m + 1) * 8], cV[:, m // 2, (m % 2) * P:(m % 2 + 1) * P],
                              pTs[:, m // 4, 32 * (m % 4):32 * (m % 4) + 8], start=True, stop=True)
                last.then_inc(s_spv, 1)

            for step in STEPS:
                what, args = step[0], step[1:]
                if what == "tile":
                    tile(*args)
                elif what == "gate":
                    gate(*args)
                elif what == "kv":
                    kv()
                elif what == "oc":
                    conv_state()
                elif what == "oh":
                    h_state()
                elif what == "sc":
                    scores(*args)
                elif what == "tr":
                    probs_t(*args)
                elif what == "pv":
                    attend(*args)
                elif what == "sk":
                    cache_t(*args)
                elif what == "ss":
                    sample_scores()
                elif what == "st":
                    sample_t()
                elif what == "sp":
                    sample_pv()

            def mix_t(n):
                if n == 0:
                    pe.wait_ge(*emptied(NT - 1))
                if n >= 2:
                    pe.wait_ge(s_z, n - 1)
                for k in range(KT):
                    last = nc.tensor.transpose(flat[n % 2][0:ROWS[n], k * P:(k + 1) * P], mixT[:, k, n * P:n * P + ROWS[n]], ident[:, :])
                last.then_inc(s_mT, 1)

            def logits(n):
                r = ROWS[n]
                pe.wait_ge(s_x1, n + 1)
                if n >= 1:
                    pe.wait_ge(s_x1c, n)
                for k in range(KT):
                    last = nc.tensor.transpose(flat[2][:, k * P:k * P + r], x1[n % 2][0:r, k * P:(k + 1) * P], ident[0:r, 0:r])
                last.then_inc(s_x1T, 1)
                pe.wait_ge(s_x1c, n + 1)
                if n >= 2:
                    pe.wait_ge(s_lgc, n - 1)
                for k in range(KT):
                    last = mm(bank[6 + n % 2][0:r, n * 64:n * 64 + NG + NE], x1T[n % 2][:, k, 0:r], wr[:, k, :], start=(k == 0), stop=(k == KT - 1))
                last.then_inc(s_lg, 1)

            mix_t(0)
            mix_t(1)
            for n in range(TT):
                logits(n)
                if n + 2 < TT:
                    mix_t(n + 2)

            pe.wait_ge(s_rcst, 11)
            pe.wait_ge(s_hot, 1)
            for n in range(TT):
                mm(bank[7][:, n * NE:(n + 1) * NE], triB[:, :], hotB[:, n, :], start=True, stop=(n == 0))
                for m in range(n):
                    mm(bank[7][:, n * NE:(n + 1) * NE], oneB[:, :], hotB[:, m, :], start=False, stop=(m == n - 1))
            for m in range(TT):
                last = mm(bank[7][:, TT * NE:(TT + 1) * NE], oneB[:, :], hotB[:, m, :], start=(m == 0), stop=(m == TT - 1))
            last.then_inc(s_pre, 1)
            for m in range(2 * TT):
                pe.wait_ge(s_oh10, 4 * (m + 1))
                last = mm(bank[6][:, 0:3 * NBLK], rk[m % 2][:, :], bk[m % 2][:, :, :].rearrange("p a b -> p (a b)"),
                          start=(m == 0), stop=(m == 2 * TT - 1))
                last.then_inc(s_tab, 1)

            def block_t(i, c):
                pe.wait_ge(s_g[c % BODY], uses(i, c, BODY) * 16)
                if c:
                    pe.wait_ge(s_xte, i * BODY + c)
                transpose_x(xg[c % BODY], s_xtp)

            def transpose_x(src, signal):
                for q in range(4):
                    last = nc.tensor.transpose(bank[0][:, q * P:(q + 1) * P], src[:, q:512:4], ident[:, :])
                last.then_inc(signal, 1)

            def gate_up(i, c):
                e, j = i * BODY + c, c % 3
                pe.wait_ge(s_xte, e + 1)
                pe.wait_ge(s_wx[3 * j], uses(i, c, 3) * 16)
                pe.wait_ge(s_wx[3 * j + 1], uses(i, c, 3) * 16)
                if c >= 3:
                    pe.wait_ge(s_gue, e - 2)
                product_gu(bank[1 + j], xt[j], slot[3 * j], slot[3 * j + 1], s_gup)

            def product_gu(out, x, w_gate, w_up, signal):
                for k in range(8):
                    w = x[:, (k % 4) * P + (k // 4) * CAP:(k % 4) * P + (k // 4) * CAP + CAP]
                    mm(out[0:CAP, :], w, w_gate[:, k, :], start=(k == 0), stop=(k == 7))
                    last = mm(out[CAP:P, :], w, w_up[:, k, :], start=(k == 0), stop=(k == 7))
                last.then_inc(signal, 1)

            def gate_up_t(i, c):
                e = i * BODY + c
                pe.wait_ge(s_gue, e + 1)
                if c:
                    pe.wait_ge(s_hh, e)
                transpose_gu(gu[c % 3], s_gt)

            def transpose_gu(src, signal):
                for q in range(4):
                    last = nc.tensor.transpose(bank[4][:, q * P:(q + 1) * P], src[:, q:512:4], ident[:, :])
                last.then_inc(signal, 1)

            def down(i, c):
                e, j = i * BODY + c, c % 3
                pe.wait_ge(s_hh, e + 1)
                pe.wait_ge(s_wx[3 * j + 2], uses(i, c, 3) * 16)
                if c >= 3:
                    pe.wait_ge(s_ye, e - 2)
                product_down(bank[5 + j], hT[j], slot[3 * j + 2], s_yp)

            def product_down(out, h, w_down, signal):
                for q in range(4):
                    for a in range(2):
                        last = mm(out[a * CAP:(a + 1) * CAP, :], h[:, q, :], w_down[:, 2 * q + a, :],
                                  start=(q == 0), stop=(q == 3))
                last.then_inc(signal, 1)

            def expert(i, c):
                gate_up(i, c)
                if not (isinstance(i, int) and c + 1 == NE):
                    block_t(i, c + 1)
                if c:
                    down(i, c - 1)
                gate_up_t(i, c)

            pe.wait_ge(s_tabc, 4)
            block_t(0, 0)
            for e in range(E_LOOP):
                expert(0, e)
            with pe.Fori(0, (E_TAIL - E_LOOP) // BODY) as i:
                for c in range(E_LOOP, E_LOOP + BODY):
                    expert(i, c)
            for e in range(E_TAIL, NE):
                expert(0, e)
            down(0, NE - 1)

            n_over = pe.value_load(ovT[0:1, NOV:NOV + 1], min_val=0, max_val=NOV)
            with pe.If(n_over > 0):
                with pe.Fori(0, NOV) as i:
                    pe.wait_ge(s_ov["free"], i + 1)
                    pe.wait_ge(s_ov["g"], i * 16 + 16)
                    transpose_x(xg[0], s_ov["xt"])
                    pe.wait_ge(s_ov["xe"], i + 1)
                    pe.wait_ge(s_ov["w"], i * 48 + 48)
                    product_gu(bank[1], xt[0], slot[0], slot[1], s_ov["gu"])
                    pe.wait_ge(s_ov["ge"], i + 1)
                    transpose_gu(gu[0], s_ov["gt"])
                    pe.wait_ge(s_ov["h"], i + 1)
                    product_down(bank[5], hT[0], slot[2], s_ov["y"])

        @block.scalar
        def _(act):
            sc = nc.scalar
            b_rows = A["b_in"].rearrange("(r c) -> r c", c=P)
            act.dma_start(vec[0:16, :], b_rows[0:16, :]).then_inc(s_vec, 16)
            bq = A["b_in"][2 * D:3 * D].rearrange("(P a h c) -> P a h c", P=2, a=2, h=4)
            for p2 in range(2):
                for a in range(2):
                    act.dma_start(vec[16 + 4 * p2:20 + 4 * p2, a * HD:(a + 1) * HD], bq[p2, a, :, :]).then_inc(s_vec, 16)
            act.dma_start(vec[24:44, :], b_rows[24:44, :]).then_inc(s_vec, 16)
            act.dma_start(vec[R_WCONV:R_BCONV, :], A["w_conv"].rearrange("j (k c) -> (j k) c", c=P)).then_inc(s_vec, 16)
            act.dma_start(vec[R_BCONV:R_BRG, :], A["b_conv"].rearrange("(k c) -> k c", c=P)).then_inc(s_vec, 16)
            act.dma_start(vec[R_BRG:R_BIG, :], A["b_rg"].rearrange("(k a) c -> k (a c)", a=2)).then_inc(s_vec, 16)
            act.dma_start(vec[R_BIG:R_LAM, :], A["b_ig"].rearrange("(k a) c -> k (a c)", a=2)).then_inc(s_vec, 16)
            act.dma_start(vec[R_LAM:NVEC, :], A["lru_lambda"].rearrange("(k c) -> k c", c=P)).then_inc(s_vec, 16)
            act.dma_start(st[0:24, :], A["state_conv"].rearrange("b j d -> (b j) d")).then_inc(s_st, 16)
            act.dma_start(st[24:32, :], A["state_lru_h"]).then_inc(s_st, 16)

            for n in range(TT):
                r = ROWS[n]
                act.wait_ge(s_xT, n + 1)
                sc.activation(xTh[:, :, n * P:n * P + r], flat[n % 2].rearrange("p (k c) -> p k c", k=KT)[:, :, 0:r],
                              ACT.Copy).then_inc(s_xh, 1)

            def w_hi(t):
                act.wait_ge(*raw_full(t))
                if t > AHEAD:
                    act.wait_ge(s_proj, t - AHEAD)
                sc.activation(whi(t), wcol(t, raw), ACT.Copy).then_inc(s_hi, 1)

            def read_tile(t):
                kind, i = TILES[t]
                ps = pair[t % 2]
                both = ps[:, :, 0:HT]
                if LAST[kind] == "act":
                    act.wait_ge(s_proj, t + 1)
                if kind in BROW:
                    bias = col[:, BROW[kind] + i:BROW[kind] + i + 1]
                if kind == "lx":
                    if i == 0:
                        act.wait_ge(s_cst, 4)
                        act.wait_ge(s_col, 1)
                    sc.activation(xp[:, i, 3:3 + HT], ps[:, 0, 0:HT], ACT.Identity, bias=bias)
                    sc.activation(xp[:, i, 3 + HT:3 + SEQ], ps[:, 1, 0:SEQ - HT], ACT.Identity, bias=bias)
                    sc.activation(xp[:, i, 3 + SEQ + 3:XPW:CONV], ps[:, 1, SEQ - HT:HT], ACT.Identity, bias=bias).then_inc(s_eva, 1)
                elif kind == "k":
                    if i == 0:
                        act.wait_ge(s_cst, 8)
                    for a in range(2):
                        half = slice(a * HD, (a + 1) * HD)
                        sc.activation(halves(kz[half, i, a, :]), both[half], ACT.Identity, bias=bias[half])
                    lo = SEQ - P - HT
                    sc.activation(kl[:, i, :], ps[:, 1, lo:HT], ACT.Identity, bias=bias).then_inc(s_eva, 1)
                elif kind == "v":
                    sc.activation(halves(vT[:, i, :]), both, ACT.Identity, bias=bias).then_inc(s_eva, 1)
                elif kind == "q":
                    if i == 6:
                        act.wait_ge(s_kvT, 1)
                    sc.activation(halves(qT[:, i, :]), both, ACT.Identity, bias=bias).then_inc(s_eva, 1)
                elif kind == "ly":
                    if i >= 1:
                        act.wait_ge(s_rec, i)
                    sc.activation(yb[:, :].rearrange("p (a b) -> p a b", a=2), both, ACT.Identity, bias=bias).then_inc(s_y, 1)
                    sc.activation(y2[:, :].rearrange("p (a b) -> p a b", a=2), both, ACT.Square, bias=bias).then_inc(s_eva, 1)
                    act.wait_ge(s_yq, 2 * (i + 1))
                    sc.activation(y2[:, :], y2[:, :], ACT.Tanh, scale=0.7978845608028654).then_inc(s_yt, 1)
                elif kind in ("gl", "ga"):
                    if kind == "gl" and i == 0:
                        act.wait_ge(s_oh_out, 32)
                        act.wait_ge(s_ss, 1)
                    if kind == "gl" and i == 4:
                        act.wait_ge(*emptied(FIRST["lo"] + 3))
                    if kind == "ga" and i == 0:
                        act.wait_ge(*emptied(FIRST["ga"] - 1))
                    if kind == "ga" and i == 4:
                        act.wait_ge(s_mg, 4)
                    b2 = colh[:, BROW[kind] - 28 + i:BROW[kind] - 28 + i + 1]
                    sc.activation(halves(sg[:, i % 4, :]), both, ACT.Tanh, bias=b2, scale=0.5).then_inc(s_eva, 1)
                elif kind == "wo":
                    if i == 0:
                        act.wait_ge(s_mg, 8)
                    sc.activation(halves(mixT[:, i, :]), both, ACT.Copy, scale=0.5).then_inc(s_eva, 1)

            def gate(i):
                act.wait_ge(s_gate, i + 1)
                if i == 0:
                    act.wait_ge(s_cf, 1)
                if i >= 2:
                    act.wait_ge(s_gx, i - 1)
                sc.activation(aL[:, i, :].rearrange("p (a b) -> p a b", a=2), pair[2][:, :, 0:XCW // 2], ACT.Sigmoid,
                              bias=col[:, R_BRG + i:R_BRG + i + 1]).then_inc(s_sig, 1)
                sc.activation(si[i % 2][:, :].rearrange("p (a b) -> p a b", a=2), pair[3][:, :, 0:XCW // 2], ACT.Sigmoid,
                              bias=col[:, R_BIG + i:R_BIG + i + 1]).then_inc(s_sig, 1)
                act.wait_ge(s_sig, 3 * i + 1)
                sc.activation(hL[:, i, :], aL[:, i, :], ACT.Tanh, scale=ncf[:, i:i + 1]).then_inc(s_sig, 1)

            def decay(first):
                for i in range(first, first + 4):
                    act.wait_ge(s_sig, 3 * (i + 1))
                    sc.activation(aL[:, i, :], aL[:, i, :], ACT.Exp, scale=cf[:, i:i + 1]).then_inc(s_a, 1)

            def root():
                for i in range(8):
                    act.wait_ge(s_om, 2 * (i + 1))
                    sc.activation(hL[:, i, :], hL[:, i, :], ACT.Sqrt).then_inc(s_rt, 1)

            def kv():
                act.wait_ge(s_kvT, 1)
                sc.activation(vtok[:, :, :].rearrange("p n c -> p (n c)"), flat[3], ACT.Copy).then_inc(s_kva, 1)

            def exps(u, par):
                p2, n = _UNITS[u]
                lo = 0 if n else P
                m = 2 * u + par
                act.wait_ge(s_nm, 2 * m + 2)
                for h in range(GRP):
                    sc.activation(sS[par][:, h, lo:256], sS[par][:, h, lo:256], ACT.Exp, bias=nm[:, par, h:h + 1],
                                  accum_out=dn[:, par, h:h + 1]).then_inc(s_ex, 1)
                sc.activation(es[:, par, :], es[:, par, :], ACT.Exp).then_inc(s_ex, 1)

            def probs_t(u, par):
                p2, n = _UNITS[u]
                act.wait_ge(s_tr, 2 * u + par + 1)
                if u >= 1:
                    act.wait_ge(s_pv, u)
                if u == 1:
                    act.wait_ge(s_spv, 1)
                if n:
                    sc.activation(pT[:, par, 0, :], bank[6], ACT.Copy).then_inc(s_pa, 1)
                else:
                    sc.activation(pT[:, par, 1, 0:256], bank[6][:, 0:256], ACT.Copy).then_inc(s_pa, 1)

            def attend(u):
                p2, n = _UNITS[u]
                act.wait_ge(s_pv, u + 1)
                sc.activation(attH[:, 4 * p2:4 * p2 + 4, n * P:(n + 1) * P], bank[6].rearrange("p (h q) -> p h q", h=4),
                              ACT.Copy).then_inc(s_atth, 1)

            def cache_t(r):
                act.wait_ge(s_skT, r + 1)
                sc.activation(kS[:, 0, 4 * r:4 * r + 4, :], bank[6].rearrange("p (b w) -> p b w", b=4), ACT.Copy).then_inc(s_ska, 1)

            def sample_exps():
                act.wait_ge(s_sm, 7)
                for m in range(4):
                    sc.activation(sSm[:, m, :], sSm[:, m, :], ACT.Exp, bias=smx[:, 1, m:m + 1],
                                  accum_out=smx[:, 3, m:m + 1]).then_inc(s_se, 1)
                sc.activation(smx[:, 2, :], smx[:, 2, :], ACT.Exp).then_inc(s_se, 1)

            def sample_att():
                act.wait_ge(s_spv, 1)
                o = bank[6][:, 0:P].rearrange("p (b P a h) -> p P a h b", b=NS, P=2, a=2)
                for a in range(2):
                    half = slice(a * HD, (a + 1) * HD)
                    for p2 in range(2):
                        ins = sc.activation(attH[half, 4 * p2:4 * p2 + 4, SEQ:T], o[half, p2, a, :, :], ACT.Copy)
                    ins.then_inc(s_sah, 1)

            for t in range(AHEAD):
                w_hi(t)
            act.wait_ge(s_lam, 1)
            sc.activation(lam[:, 1, :], lam[:, 0, :], ACT.Exp, scale=-1.0).then_inc(s_lamE, 1)
            for step in STEPS:
                what, args = step[0], step[1:]
                if what == "tile":
                    t = args[0]
                    if t + AHEAD < NT:
                        w_hi(t + AHEAD)
                    if LAST[TILES[t][0]] == "act":
                        read_tile(t)
                elif what == "gate":
                    gate(*args)
                elif what == "exp":
                    decay(*args)
                elif what == "root":
                    root()
                elif what == "kv":
                    kv()
                elif what == "sc":
                    exps(*args)
                elif what == "tr":
                    probs_t(*args)
                elif what == "pv":
                    attend(*args)
                elif what == "sk":
                    cache_t(*args)
                elif what == "ss":
                    sample_exps()
                elif what == "sp":
                    sample_att()

            def ln1_root(n):
                act.wait_ge(s_z, n + 1)
                sc.activation(mv[0:ROWS[n], n % 2, 2:3], mv[0:ROWS[n], n % 2, 1:2], ACT.Sqrt, bias=epsT[0:ROWS[n], :]).then_inc(s_sd, 1)

            def x1_t(n):
                r = ROWS[n]
                act.wait_ge(s_x1T, n + 1)
                if n >= 2:
                    act.wait_ge(s_lg, n - 1)
                sc.activation(x1T[n % 2][:, :, 0:r], flat[2].rearrange("p (k c) -> p k c", k=KT)[:, :, 0:r], ACT.Copy).then_inc(s_x1c, 1)

            act.wait_ge(s_cst, 5)
            ln1_root(0)
            ln1_root(1)
            for n in range(TT):
                x1_t(n)
                if n + 2 < TT:
                    ln1_root(n + 2)
            act.wait_ge(s_rd, 1)
            sc.activation(g20[0][:, :, :], g20[0][:, :, :], ACT.Exp).then_inc(s_re, 1)
            act.wait_ge(s_rd, 2)
            sc.activation(w5[3][:, :], w5[3][:, :], ACT.Exp).then_inc(s_re, 1)

            def copy_gu(i, c):
                e, j = i * BODY + c, c % 3
                act.wait_ge(s_gup, e + 1)
                if c >= 3:
                    act.wait_ge(s_gt, e - 2)
                sc.activation(gu[j][:, :], bank[1 + j], ACT.Copy).then_inc(s_gue, 1)

            def scale_out(i, c):
                e, j = i * BODY + c, c % 3
                act.wait_ge(s_yp, e + 1)
                if c >= 3:
                    act.wait_ge(s_sct[j], uses(i, c - 3, 3) * 16)
                sc.activation(ys[j][:, :], bank[5 + j], ACT.Copy, scale=tabW[:, bass.ds(e, 1)]).then_inc(s_ye, 1)

            def sigmoid(i, c):
                e, j = i * BODY + c, c % 3
                act.wait_ge(s_gt, e + 1)
                if c >= 3:
                    act.wait_ge(s_hh, e - 2)
                sc.activation(sgm[j][:, :, :], bank[4].rearrange("p (q s) -> p q s", q=4)[:, :, 0:CAP], ACT.Sigmoid).then_inc(s_sgm, 1)

            def expert(i, c):
                copy_gu(i, c)
                if c:
                    scale_out(i, c - 1)
                sigmoid(i, c)

            act.wait_ge(s_tabc, 4)
            for e in range(E_LOOP):
                expert(0, e)
            with act.Fori(0, (E_TAIL - E_LOOP) // BODY) as i:
                for c in range(E_LOOP, E_LOOP + BODY):
                    expert(i, c)
            for e in range(E_TAIL, NE):
                expert(0, e)
            scale_out(0, NE - 1)

            n_over = act.value_load(ovT[0:1, NOV:NOV + 1], min_val=0, max_val=NOV)
            with act.If(n_over > 0):
                with act.Fori(0, NOV) as i:
                    act.wait_ge(s_ov["free"], i + 1)
                    act.wait_ge(s_ov["gu"], i + 1)
                    sc.activation(gu[0][:, :], bank[1], ACT.Copy).then_inc(s_ov["ge"], 1)
                    act.wait_ge(s_ov["gt"], i + 1)
                    sc.activation(sgm[0][:, :, :], bank[4].rearrange("p (q s) -> p q s", q=4)[:, :, 0:CAP], ACT.Sigmoid).then_inc(s_ov["sg"], 1)
                    act.wait_ge(s_ov["y"], i + 1)
                    sc.activation(ys[0][:, :], bank[5], ACT.Copy, scale=tabW[:, bass.ds(i + NE, 1)]).then_inc(s_ov["ye"], 1)

            for n in range(TT):
                act.wait_ge(s_z2, n + 1)
                sc.activation(mv[0:ROWS[n], n % 2, 2:3], mv[0:ROWS[n], n % 2, 1:2], ACT.Sqrt, bias=epsT[0:ROWS[n], :]).then_inc(s_sd2, 1)

        @block.vector
        def _(dve):
            v = nc.vector
            dc = [0]

            def mark(ins):
                dc[0] += 1
                ins.then_inc(d_c, 1)
                return dc[0]

            def link(ins):
                dve.wait_ge(d_c, mark(ins))

            def split_x(n):
                r = ROWS[n]
                dve.wait_ge(s_xh, n + 1)
                v.tensor_tensor(xTl[:, :, n * P:n * P + r], flat[n % 2].rearrange("p (k c) -> p k c", k=KT)[:, :, 0:r],
                                xTh[:, :, n * P:n * P + r].bitcast(F32), ALU.subtract).then_inc(s_xl, 1)

            def w_lo(t):
                dve.wait_ge(s_hi, t + 1)
                v.tensor_tensor(wcol(t, rawL), wcol(t, raw), whi(t).bitcast(F32), ALU.subtract).then_inc(s_lo, 1)

            for n in range(TT):
                split_x(n)
            for t in range(2):
                w_lo(t)
            dve.wait_ge(s_vT, 1)
            v.tensor_copy(col[:, :], bank[4][:, 0:NVEC]).then_inc(s_col, 1)
            dve.wait_ge(s_col, 1)
            dve.wait_ge(s_cst, 4)
            link(v.tensor_scalar(colh[:, :], col[:, 28:44], 0.5, None, ALU.mult))
            la = col[:, R_LAM:R_LAM + 8]
            link(v.tensor_scalar(lam[:, 2, :], la, -1.0, None, ALU.mult))
            v.tensor_tensor(lam[:, 0, :], lam[:, 2, :], la, ALU.max).then_inc(s_lam, 1)
            dve.wait_ge(s_stT, 1)
            stp = bank[5][:, 0:256].rearrange("p (k r) -> p k r", k=KT)
            for j in range(3):
                ins = v.tensor_copy(xp[:, :, 3 + SEQ + j:XPW:CONV], stp[:, :, j:24:3])
            ins.then_inc(s_stc, 1)
            v.tensor_copy(h0[:, :, :], stp[:, :, 24:32]).then_inc(s_stc, 1)
            dve.wait_ge(s_lamE, 1)
            z_, s_, q_, p_ = lam[:, 1, :], lam[:, 0, :], lam[:, 3, :], cf[:, :]
            link(v.tensor_scalar(s_, z_, 2.0, None, ALU.add))
            link(v.reciprocal(s_, s_))
            link(v.tensor_tensor(s_, s_, z_, ALU.mult))
            link(v.tensor_tensor(q_, s_, s_, ALU.mult))
            link(v.tensor_scalar(p_, q_, 1.0 / 17, 1.0 / 15, ALU.mult, ALU.add))
            for n in (13, 11, 9, 7, 5, 3, 1):
                link(v.tensor_tensor(p_, p_, q_, ALU.mult))
                link(v.tensor_scalar(p_, p_, 1.0 / n, None, ALU.add))
            link(v.tensor_tensor(p_, p_, s_, ALU.mult))
            link(v.tensor_scalar(lam[:, 2, :], lam[:, 2, :], 0.0, None, ALU.max))
            link(v.scalar_tensor_tensor(out=q_, in0=p_, scalar=2.0, in1=lam[:, 2, :], op0=ALU.mult, op1=ALU.add))
            link(v.tensor_scalar(cf[:, :], q_, -8.0, None, ALU.mult))
            v.tensor_scalar(ncf[:, :], q_, 8.0, None, ALU.mult).then_inc(s_cf, 1)

            def conv(i):
                dve.wait_ge(*emptied(i))
                if i == 0:
                    dve.wait_ge(s_stc, 2)
                if i >= 2:
                    dve.wait_ge(s_gate, i - 1)
                    dve.wait_ge(s_gx, i - 1)
                x = xc[i % 2]
                link(v.tensor_scalar(x[:, :], xp[:, i, 0:XCW], col[:, R_WCONV + i:R_WCONV + i + 1],
                                     col[:, R_BCONV + i:R_BCONV + i + 1], ALU.mult, ALU.add))
                for j in range(1, CONV):
                    r = R_WCONV + 8 * j + i
                    ins = v.scalar_tensor_tensor(out=x[:, :], in0=xp[:, i, j:j + XCW], scalar=col[:, r:r + 1], in1=x[:, :],
                                                 op0=ALU.mult, op1=ALU.add)
                    if j < CONV - 1:
                        link(ins)
                ins.then_inc(s_cv, 1)

            def gated(i):
                dve.wait_ge(s_cv, i + 1)
                dve.wait_ge(s_sig, 3 * i + 2)
                v.tensor_tensor(gT[:, i, :], si[i % 2][:, :], xc[i % 2][:, :], ALU.mult).then_inc(s_gx, 1)

            def square(first):
                for i in range(first, first + 4):
                    dve.wait_ge(s_a, i + 1)
                    if i:
                        dve.wait_ge(s_om, 2 * i)
                    v.tensor_tensor(a2[:, :], aL[:, i, :], aL[:, i, :], ALU.mult).then_inc(s_om, 1)
                    dve.wait_ge(s_om, 2 * i + 1)
                    v.scalar_tensor_tensor(out=hL[:, i, :], in0=a2[:, :], scalar=1.0, in1=hL[:, i, :],
                                           op0=ALU.add, op1=ALU.mult).then_inc(s_om, 1)

            def scan(first):
                for i in range(first, first + 4):
                    dve.wait_ge(s_rt, i + 1)
                    dve.wait_ge(s_gx, 8)
                    link(v.tensor_tensor(gT[:, i, :], gT[:, i, :], hL[:, i, :], ALU.mult))
                    v.tensor_tensor_scan(hL[:, i, 0:SEQ], aL[:, i, 0:SEQ], gT[:, i, 0:SEQ], 0.0, ALU.mult, ALU.add).then_inc(s_h, 1)
                    link(v.tensor_tensor(h0[:, i, :], h0[:, i, :], sample_cols(aL[:, i, :]), ALU.mult))
                    v.tensor_tensor(hL[:, i, SEQ:T], h0[:, i, :], sample_cols(gT[:, i, :]), ALU.add).then_inc(s_h, 1)

            def kv():
                dve.wait_ge(s_kvT, 1)
                v.tensor_copy(kwin[:, :], bank[4][:, 0:256]).then_inc(s_kvd, 1)
                v.tensor_copy(snew[:, :], bank[5][0:NS, :]).then_inc(s_kvd, 1)

            def conv_state():
                dve.wait_ge(s_ocT, 1)
                for n in range(2):
                    v.tensor_copy(oc[:, n * 512:(n + 1) * 512], pair[2][0:XPW - SEQ, n, :]).then_inc(s_ocv, 1)

            def h_state():
                dve.wait_ge(s_ohT, 1)
                for n in range(2):
                    v.tensor_copy(oh[:, n * 512:(n + 1) * 512], pair[2][0:NS + 1, n, :]).then_inc(s_ohv, 1)

            def masked(u, par):
                p2, n = _UNITS[u]
                lo = 0 if n else P
                m = 2 * u + par
                dve.wait_ge(s_sc, m + 1)
                if m == 0:
                    dve.wait_ge(s_snk, 16)
                    dve.wait_ge(s_cst, 6)
                if m >= 2:
                    dve.wait_ge(s_tr, m - 1)
                    dve.wait_ge(s_nrm, 4 * (m - 1))
                for h in range(GRP):
                    head = (2 * p2 + par) * GRP + h
                    v.tensor_tensor_reduce(out=sS[par][:, h, lo:256], in0=pair[2][:, h // 2, (h % 2) * 256 + lo:(h % 2) * 256 + 256],
                                           in1=mask[:, lo:256], scale=HD ** -0.5, scalar=sk8[:, head:head + 1],
                                           op0=ALU.add, op1=ALU.max, accum_out=mx[:, par, h:h + 1]).then_inc(s_ttr, 1)
                dve.wait_ge(s_ttr, 4 * (m + 1))
                v.tensor_scalar(nm[:, par, :], mx[:, par, :], -1.0, None, ALU.mult).then_inc(s_nm, 1)
                g = (2 * p2 + par) * GRP
                v.tensor_tensor(es[:, par, :], sk8[:, g:g + GRP], mx[:, par, :], ALU.subtract).then_inc(s_nm, 1)

            def normal(u, par):
                p2, n = _UNITS[u]
                lo = 0 if n else P
                m = 2 * u + par
                dve.wait_ge(s_ex, 5 * (m + 1))
                link(v.tensor_tensor(dn[:, par, :], dn[:, par, :], es[:, par, :], ALU.add))
                link(v.reciprocal(dn[:, par, :], dn[:, par, :]))
                for h in range(GRP):
                    v.tensor_scalar(sS[par][:, h, lo:256], sS[par][:, h, lo:256], dn[:, par, h:h + 1], None, ALU.mult).then_inc(s_nrm, 1)

            def probs_t(u, par):
                p2, n = _UNITS[u]
                dve.wait_ge(s_tr, 2 * u + par + 1)
                if u == 0:
                    dve.wait_ge(s_kv_out, 64)
                    dve.wait_ge(s_cv_ld, 32)
                else:
                    dve.wait_ge(s_pv, u)
                if u == 1:
                    dve.wait_ge(s_spv, 1)
                if n:
                    v.tensor_copy(pT[:, par, 1, :], bank[7]).then_inc(s_pd, 1)
                else:
                    v.tensor_copy(pT[:, par, 1, 256:512], bank[7][:, 256:512]).then_inc(s_pd, 1)

            def attend(u):
                p2, n = _UNITS[u]
                dve.wait_ge(s_atth, u + 1)
                if u == 0:
                    dve.wait_ge(s_h, 16)
                v.tensor_tensor(attL[:, 4 * p2:4 * p2 + 4, n * P:(n + 1) * P], bank[6].rearrange("p (h q) -> p h q", h=4),
                                attH[:, 4 * p2:4 * p2 + 4, n * P:(n + 1) * P].bitcast(F32), ALU.subtract).then_inc(s_attl, 1)

            def cache_t(r):
                dve.wait_ge(s_skT, r + 1)
                v.tensor_copy(kS[:, 1, 4 * r:4 * r + 4, :], bank[7].rearrange("p (b w) -> p b w", b=4)).then_inc(s_skd, 1)
                if r == 1:
                    dve.wait_ge(s_ska, 2)
                    dve.wait_ge(s_skd, 2)
                    for p2 in range(2):
                        for a in range(2):
                            half = slice(a * HD, (a + 1) * HD)
                            v.tensor_copy(kS[half, p2, :, 0], kz[half, p2, a, SEQ:T]).then_inc(s_skd, 1)
                    dve.wait_ge(s_qz, 1)
                    dve.wait_ge(*emptied(FIRST["q"] + 7))
                    q4 = qz[:, :, :].rearrange("p (b P) (z a h) -> p P z a h b", P=2, a=2, h=4)
                    for p2 in range(2):
                        for a in range(2):
                            half = slice(a * HD, (a + 1) * HD)
                            v.tensor_copy(q4[half, p2, 0, a, :, :], qT[half, 4 * p2:4 * p2 + 4, SEQ:T]).then_inc(s_qz, 1)

            def sample_max():
                dve.wait_ge(s_ss, 1)
                dve.wait_ge(s_snr, 64)
                dve.wait_ge(s_pv, 1)
                s4 = bank[4].rearrange("p (m w) -> p m w", m=4)
                v.tensor_scalar(sSm[:, :, :], s4, HD ** -0.5, None, ALU.mult).then_inc(s_sm, 1)
                dve.wait_ge(s_sm, 1)
                v.tensor_reduce(smx[:, 0, :], sSm[:, :, :], AX.X, ALU.max).then_inc(s_sm, 1)
                dve.wait_ge(s_sm, 2)
                v.tensor_scalar(smx[:, 0, :], smx[:, 0, :], sks[:, 0:1], None, ALU.max).then_inc(s_sm, 1)
                dve.wait_ge(s_sm, 3)
                v.tensor_scalar(smx[:, 1, :], smx[:, 0, :], -1.0, None, ALU.mult).then_inc(s_sm, 1)
                dve.wait_ge(s_sm, 4)
                v.tensor_scalar(smx[:, 2, :], smx[:, 1, :], sks[:, 0:1], None, ALU.add).then_inc(s_sm, 1)
                link(v.tensor_copy(smx[:, 3, :], smx[:, 0, :]))
                v.tensor_copy(mx[:, 0, :], smx[:, 0, :]).then_inc(s_sm, 1)
                v.tensor_copy(mx[:, 1, :], smx[:, 0, :]).then_inc(s_sm, 1)

            def sample_normal():
                dve.wait_ge(s_se, 5)
                link(v.tensor_tensor(smx[:, 3, :], smx[:, 3, :], smx[:, 2, :], ALU.add))
                link(v.reciprocal(smx[:, 3, :], smx[:, 3, :]))
                for m in range(4):
                    v.tensor_scalar(sSm[:, m, :], sSm[:, m, :], smx[:, 3, m:m + 1], None, ALU.mult).then_inc(s_sn, 1)
                dve.wait_ge(s_spT, 1)
                v.tensor_copy(pTs[:, :, :].rearrange("p a b -> p (a b)"), bank[7]).then_inc(s_spc, 1)

            def sample_att():
                dve.wait_ge(s_sah, 2)
                o = bank[6][:, 0:P].rearrange("p (b P a h) -> p P a h b", b=NS, P=2, a=2)
                for a in range(2):
                    half = slice(a * HD, (a + 1) * HD)
                    for p2 in range(2):
                        ins = v.tensor_tensor(attL[half, 4 * p2:4 * p2 + 4, SEQ:T], o[half, p2, a, :, :],
                                              attH[half, 4 * p2:4 * p2 + 4, SEQ:T].bitcast(F32), ALU.subtract)
                    ins.then_inc(s_sal, 1)

            def read_tile(t):
                kind, i = TILES[t]
                if kind == "ly":
                    dve.wait_ge(*emptied(t))
                    v.tensor_scalar(y2[:, :], y2[:, :], 0.044715, 1.0, ALU.mult, ALU.add).then_inc(s_yq, 1)
                    dve.wait_ge(s_yq, 2 * i + 1)
                    v.tensor_tensor(y2[:, :], y2[:, :], yb[:, :], ALU.mult).then_inc(s_yq, 1)
                    dve.wait_ge(s_yt, i + 1)
                    dve.wait_ge(s_h, 16)
                    dve.wait_ge(s_ohT, 1)
                    link(v.scalar_tensor_tensor(out=yb[:, :], in0=y2[:, :], scalar=1.0, in1=yb[:, :], op0=ALU.add, op1=ALU.mult))
                    link(v.scalar_tensor_tensor(out=yb[:, :], in0=yb[:, :], scalar=0.5, in1=hL[:, i, 0:T], op0=ALU.mult, op1=ALU.mult))
                    link(v.tensor_copy(recH[:, i, 0:T], yb[:, :]))
                    v.tensor_tensor(recL[:, i, 0:T], yb[:, :], recH[:, i, 0:T].bitcast(F32), ALU.subtract).then_inc(s_rec, 1)
                elif kind == "lo":
                    dve.wait_ge(s_proj, t + 1)
                    dve.wait_ge(*emptied(FIRST["gl"] + i if i < 4 else FIRST["gl"] + 8 + i - 4))
                    if i == 0:
                        dve.wait_ge(s_spv, 1)
                    v.scalar_tensor_tensor(out=halves(m1[:, i, :]), in0=halves(sg[:, i % 4, :]), scalar=1.0,
                                           in1=pair[t % 2][:, :, 0:HT], op0=ALU.add, op1=ALU.mult).then_inc(s_evd, 1)
                elif kind == "ao":
                    dve.wait_ge(s_proj, t + 1)
                    dve.wait_ge(*emptied(FIRST["ga"] + i if i < 4 else FIRST["ga"] + 8 + i - 4))
                    v.scalar_tensor_tensor(out=halves(sg[:, i % 4, :]), in0=halves(sg[:, i % 4, :]), scalar=1.0,
                                           in1=pair[t % 2][:, :, 0:HT], op0=ALU.add, op1=ALU.mult).then_inc(s_evd, 1)
                    dve.wait_ge(*emptied(t))
                    link(v.tensor_tensor(sg[:, i % 4, :], sg[:, i % 4, :], m1[:, i, :], ALU.add))
                    link(v.tensor_copy(mgH[:, i, :], sg[:, i % 4, :]))
                    v.tensor_tensor(mgL[:, i, 0:T], sg[:, i % 4, :], mgH[:, i, :].bitcast(F32), ALU.subtract).then_inc(s_mg, 1)

            for t in range(2, AHEAD):
                w_lo(t)
            for step in STEPS:
                what, args = step[0], step[1:]
                if what == "tile":
                    t = args[0]
                    if t + AHEAD < NT:
                        w_lo(t + AHEAD)
                    kind, i = TILES[t]
                    if kind == "lx":
                        conv(i)
                    if kind in ("ly", "lo", "ao"):
                        read_tile(t)
                elif what == "gate":
                    gated(*args)
                elif what == "sq":
                    square(*args)
                elif what == "kv":
                    kv()
                elif what == "scan":
                    scan(*args)
                elif what == "oc":
                    conv_state()
                elif what == "oh":
                    h_state()
                elif what == "sc":
                    masked(*args)
                elif what == "nrm":
                    normal(*args)
                elif what == "tr":
                    probs_t(*args)
                elif what == "pv":
                    attend(*args)
                elif what == "sk":
                    cache_t(*args)
                elif what == "ss":
                    sample_max()
                elif what == "st":
                    sample_normal()
                elif what == "sp":
                    sample_att()

            def norm_stats(z, r, k, signal):
                m1_ = mark(v.bn_stats(st6[0:r, k, 0, :], z[0:r, 0:512]))
                m2_ = mark(v.bn_stats(st6[0:r, k, 1, :], z[0:r, 512:D]))
                dve.wait_ge(d_c, m2_)
                v.bn_aggr(mv[0:r, k, 0:2], st6[0:r, k, :, :]).then_inc(signal, 1)

            def norm_scale(z, r, k, gain, signal):
                link(v.reciprocal(mv[0:r, k, 3:4], mv[0:r, k, 2:3]))
                link(v.tensor_scalar(z[0:r, :], z[0:r, :], mv[0:r, k, 0:1], mv[0:r, k, 3:4], ALU.subtract, ALU.mult))
                v.tensor_tensor(z[0:r, :], z[0:r, :], gain[0:r, :], ALU.mult).then_inc(signal, 1)

            def stats1(n):
                r, k = ROWS[n], n % 2
                dve.wait_ge(s_mT, n + 1)
                dve.wait_ge(s_x[n], 32)
                if n == 0:
                    dve.wait_ge(s_proj, NT)
                if n >= 2:
                    dve.wait_ge(s_x1, n - 1)
                link(v.scalar_tensor_tensor(out=z1[k][0:r, :], in0=xre[k][0:r, :], scalar=ALPHA, in1=flat[k][0:r, :],
                                            op0=ALU.mult, op1=ALU.add))
                norm_stats(z1[k], r, k, s_z)

            def scale1(n):
                dve.wait_ge(s_ln, 96)
                dve.wait_ge(s_sd, n + 1)
                norm_scale(z1[n % 2], ROWS[n], n % 2, lnG, s_xn)

            def keep_logits(n):
                r = ROWS[n]
                dve.wait_ge(s_lg, n + 1)
                dve.wait_ge(s_rcst, 11)
                v.tensor_tensor(lg[0:r, n, :], bank[6 + n % 2][0:r, n * 64:n * 64 + NG + NE], rb[0:r, :], ALU.add).then_inc(s_lgc, 1)

            stats1(0)
            stats1(1)
            scale1(0)
            for n in range(1, TT):
                scale1(n)
                if n + 1 < TT:
                    stats1(n + 1)
                keep_logits(n - 1)
            keep_logits(TT - 1)
            dve.wait_ge(s_lgc, TT)

            def wide(ap, n):
                return ap.rearrange("p (t a) -> p t a", a=1).to_broadcast([P, TT, n])

            def first_hot(x, n, io, big, out):
                best, idx = big
                link(v.tensor_reduce(best, x, AX.X, ALU.max))
                link(v.tensor_tensor(out, x, wide(best, n), ALU.is_equal))
                link(v.tensor_scalar(out, out, -64.0, 64.0, ALU.mult, ALU.add))
                io3 = io[:, :].rearrange("p (a n) -> p a n", a=1).to_broadcast([P, TT, n])
                link(v.tensor_tensor(out, out, io3, ALU.add))
                link(v.tensor_reduce(idx, out, AX.X, ALU.min))
                link(v.tensor_tensor(out, io3, wide(idx, n), ALU.is_equal))

            grp = lg[:, :, 0:NG]
            exp_l = lg[:, :, NG:]
            link(v.tensor_reduce(w5[0][:, :], grp, AX.X, ALU.max))
            v.tensor_tensor(g20[0][:, :, :], grp, wide(w5[0][:, :], NG), ALU.subtract).then_inc(s_rd, 1)
            first_hot(grp, NG, io4, (w5[1][:, :], w5[2][:, :]), g20[1][:, :, :])
            g4 = g20[1][:, :, :].rearrange("p t (g a) -> p t g a", a=1).to_broadcast([P, TT, NG, EPG])
            e4 = exp_l.rearrange("p t (g e) -> p t g e", g=NG)
            sel4 = esel[:, :, :].rearrange("p t (g e) -> p t g e", g=NG)
            link(v.tensor_scalar(g20[2][:, :, :], g20[1][:, :, :], BIG, -BIG, ALU.mult, ALU.add))
            b4 = g20[2][:, :, :].rearrange("p t (g a) -> p t g a", a=1).to_broadcast([P, TT, NG, EPG])
            for n in range(TT):
                v.tensor_tensor(sel4[:, n], e4[:, n], g4[:, n], ALU.mult)
            link(v.tensor_copy(w5[7][:, :], w5[1][:, :]))
            for n in range(TT):
                v.tensor_tensor(sel4[:, n], sel4[:, n], b4[:, n], ALU.add)
            link(v.tensor_copy(w5[7][:, :], w5[1][:, :]))
            k0, k1 = hot[:, 0, :, :], hot[:, 1, :, :]
            first_hot(esel[:, :, :], NE, io32, (w5[1][:, :], w10[0][:, 0, :]), k0)
            link(v.scalar_tensor_tensor(out=esel[:, :, :], in0=k0, scalar=-2.0 * BIG, in1=esel[:, :, :], op0=ALU.mult, op1=ALU.add))
            first_hot(esel[:, :, :], NE, io32, (w5[2][:, :], w10[0][:, 1, :]), k1)
            v.tensor_tensor(w5[3][:, :], w5[2][:, :], w5[1][:, :], ALU.subtract).then_inc(s_rd, 1)
            link(v.tensor_tensor(e160[0][:, :, :], k0, k1, ALU.add))
            v.tensor_tensor(hotB[:, :, :], e160[0][:, :, :], wide(valid[:, :], NE), ALU.mult).then_inc(s_hot, 1)
            dve.wait_ge(s_re, 2)
            link(v.tensor_reduce(w5[4][:, :], g20[0][:, :, :], AX.X, ALU.add))
            link(v.scalar_tensor_tensor(out=w5[4][:, :], in0=w5[3][:, :], scalar=1.0, in1=w5[4][:, :], op0=ALU.add, op1=ALU.mult))
            link(v.reciprocal(w5[4][:, :], w5[4][:, :]))
            link(v.tensor_tensor(w10[1][:, 0, :], w5[4][:, :], valid[:, :], ALU.mult))
            link(v.tensor_tensor(w10[1][:, 1, :], w10[1][:, 0, :], w5[3][:, :], ALU.mult))
            for k in range(2):
                link(v.tensor_tensor(w10[2][:, k, :], tokv[:, k, :], valid[:, :], ALU.mult))
            link(v.tensor_copy(w10[3][:, 0, :], w10[2][:, 0, :]))
            link(v.scalar_tensor_tensor(out=w10[3][:, 1, :], in0=valid[:, :], scalar=2.0 * T, in1=w10[2][:, 1, :], op0=ALU.mult, op1=ALU.add))

            dve.wait_ge(s_pre, 1)
            link(v.tensor_copy(cum[:, 0, :], bank[7][:, TT * NE:(TT + 1) * NE]))

            def floor64(x, tmp):
                link(v.tensor_scalar(x, x, 1.0 / CAP, 0.5 / CAP - 0.5, ALU.mult, ALU.add))
                link(v.tensor_scalar(x, x, 12582912.0, None, ALU.add))
                link(v.tensor_scalar(x, x, -12582912.0, None, ALU.add))

            link(v.tensor_scalar(cum[:, 1, :], cum[:, 0, :], 1.0, -1.0, ALU.max, ALU.add))
            floor64(cum[:, 1, :], None)
            link(v.memset(cum[:, 3, :], 1.0))
            link(v.tensor_tensor_scan(cum[:, 2, :], cum[:, 3, :], cum[:, 1, :], 0.0, ALU.mult, ALU.add))
            link(v.tensor_tensor(cum[:, 3, :], cum[:, 2, :], cum[:, 1, :], ALU.subtract))
            inc = cum[:, 2, :].rearrange("p (a e) -> p a e", a=1).to_broadcast([P, NOV, NE])
            i16 = io48[:, 0:NOV].rearrange("p (n a) -> p n a", a=1).to_broadcast([P, NOV, NE])
            link(v.tensor_tensor(ov16[:, :, :], inc, i16, ALU.is_le))
            link(v.tensor_reduce(ovf[:, 0:NOV], ov16[:, :, :], AX.X, ALU.add))
            link(v.tensor_scalar(ovf[:, 0:NOV], ovf[:, 0:NOV], float(NE - 1), None, ALU.min))
            link(v.tensor_copy(ovf[:, NOV:NOV + 1], cum[:, 2, NE - 1:NE]))
            v.tensor_copy(ovT[:, :], ovf[:, :]).then_inc(s_tabc, 1)
            pre = bank[7][:, 0:TT * NE].rearrange("p (t e) -> p t e", t=TT)
            base3 = cum[:, 3, :].rearrange("p (a e) -> p a e", a=1).to_broadcast([P, TT, NE])
            for k, hk in ((0, k0), (1, k1)):
                link(v.tensor_tensor(e160[0][:, :, :], hk, pre, ALU.mult))
                link(v.tensor_reduce(w10[4][:, k, :], e160[0][:, :, :], AX.X, ALU.add))
                link(v.tensor_tensor(e160[1][:, :, :], hk, base3, ALU.mult))
                link(v.tensor_reduce(w10[5][:, k, :], e160[1][:, :, :], AX.X, ALU.add))
            f = [w[:, :, :].rearrange("p k t -> p (k t)") for w in w10]
            link(v.tensor_copy(f[6], f[4]))
            floor64(f[6], None)
            link(v.scalar_tensor_tensor(out=f[4], in0=f[6], scalar=-float(CAP), in1=f[4], op0=ALU.mult, op1=ALU.add))
            link(v.tensor_scalar(f[7], f[6], 1.0, None, ALU.min))
            link(v.scalar_tensor_tensor(out=f[5], in0=f[5], scalar=float(NE - 1), in1=f[6], op0=ALU.add, op1=ALU.add))
            link(v.tensor_tensor(f[5], f[5], f[0], ALU.subtract))
            link(v.tensor_tensor(f[5], f[5], f[7], ALU.mult))
            link(v.tensor_tensor(f[5], f[5], f[0], ALU.add))
            for m in range(2 * TT):
                if m >= 2:
                    dve.wait_ge(s_tab, m - 1)
                v.tensor_scalar(rk[m % 2][:, :], io128[:, :], f[4][:, m:m + 1], None, ALU.is_equal).then_inc(s_oh10, 1)
                for n, val in enumerate((f[2], f[3], f[1])):
                    v.tensor_scalar(bk[m % 2][:, n, :], io48[:, :], f[5][:, m:m + 1], val[:, m:m + 1],
                                    ALU.is_equal, ALU.mult).then_inc(s_oh10, 1)
            dve.wait_ge(s_tab, 2 * TT)
            v.tensor_scalar(tabG[:, :], bank[6][:, 0:NBLK], off[:, 0:1], None, ALU.add).then_inc(s_tabc, 1)
            v.tensor_scalar(tabD[:, :], bank[6][:, NBLK:2 * NBLK], off[:, 0:1], None, ALU.add).then_inc(s_tabc, 1)
            v.tensor_copy(tabW[:, :], bank[6][:, 2 * NBLK:3 * NBLK]).then_inc(s_tabc, 1)
            dve.wait_ge(s_tabc, 4)

            def copy_xt(i, c):
                e, j = i * BODY + c, c % 3
                dve.wait_ge(s_xtp, e + 1)
                if c >= 3:
                    dve.wait_ge(s_gup, e - 2)
                v.tensor_copy(xt[j][:, :], bank[0]).then_inc(s_xte, 1)

            def hidden(i, c):
                e, j = i * BODY + c, c % 3
                dve.wait_ge(s_sgm, e + 1)
                v.tensor_tensor(sgm[j][:, :, :], sgm[j][:, :, :], t4[:, :, 0:CAP], ALU.mult).then_inc(s_h1, 1)
                dve.wait_ge(s_h1, e + 1)
                if c >= 3:
                    dve.wait_ge(s_yp, e - 2)
                v.tensor_tensor(hT[j][:, :, :], sgm[j][:, :, :], t4[:, :, CAP:P], ALU.mult).then_inc(s_hh, 1)

            def expert(i, c):
                if not (isinstance(i, int) and c + 1 == NE):
                    copy_xt(i, c + 1)
                hidden(i, c)

            t4 = bank[4].rearrange("p (q s) -> p q s", q=4)
            copy_xt(0, 0)
            for e in range(E_LOOP):
                expert(0, e)
            with dve.Fori(0, (E_TAIL - E_LOOP) // BODY) as i:
                for c in range(E_LOOP, E_LOOP + BODY):
                    expert(i, c)
            for e in range(E_TAIL, NE):
                expert(0, e)

            n_over = dve.value_load(ovT[0:1, NOV:NOV + 1], min_val=0, max_val=NOV)
            with dve.If(n_over > 0):
                with dve.Fori(0, NOV) as i:
                    dve.wait_ge(s_ov["xt"], i + 1)
                    v.tensor_copy(xt[0][:, :], bank[0]).then_inc(s_ov["xe"], 1)
                    dve.wait_ge(s_ov["sg"], i + 1)
                    v.tensor_tensor(sgm[0][:, :, :], sgm[0][:, :, :], t4[:, :, 0:CAP], ALU.mult).then_inc(s_ov["h1"], 1)
                    dve.wait_ge(s_ov["h1"], i + 1)
                    v.tensor_tensor(hT[0][:, :, :], sgm[0][:, :, :], t4[:, :, CAP:P], ALU.mult).then_inc(s_ov["h"], 1)

            def stats2(n):
                r, k = ROWS[n], n % 2
                dve.wait_ge(s_f[k], 48 * (n // 2 + 1))
                if n >= 2:
                    dve.wait_ge(s_y3, n - 1)
                link(v.scalar_tensor_tensor(out=z2[k][0:r, :], in0=xr2[k][0:r, :], scalar=ALPHA, in1=f0[k][0:r, :],
                                            op0=ALU.mult, op1=ALU.add))
                link(v.tensor_tensor(z2[k][0:r, :], z2[k][0:r, :], f1[k][0:r, :], ALU.add))
                norm_stats(z2[k], r, k, s_z2)

            def scale2(n):
                dve.wait_ge(s_l2, 32)
                dve.wait_ge(s_sd2, n + 1)
                norm_scale(z2[n % 2], ROWS[n], n % 2, ln2G, s_y2)

            stats2(0)
            for n in range(TT):
                if n + 1 < TT:
                    stats2(n + 1)
                scale2(n)


_INS = ["x_prompt", "x_sample", "cache_k", "cache_v", "state_conv", "state_lru_h", "w_in", "b_in", "w_conv", "b_conv",
        "w_rg", "b_rg", "w_ig", "b_ig", "lru_lambda", "sinks", "w_lru_out", "w_attn_out", "w_o", "ln1_g", "ln1_b",
        "w_group", "b_group", "w_router", "b_router", "w_gate", "w_up", "w_down", "ln2_g", "ln2_b"]
_OUTS = [("y_prompt", (1, SEQ, D)), ("y_sample", (NS, 1, D)),
         ("k_win_prompt", (1, WIN, NKV, HD)), ("v_win_prompt", (1, WIN, NKV, HD)),
         ("conv_prompt", (1, CONV - 1, D)), ("h_prompt", (1, D)),
         ("k_win_sample", (NS, WIN, NKV, HD)), ("v_win_sample", (NS, WIN, NKV, HD)),
         ("conv_sample", (NS, CONV - 1, D)), ("h_sample", (NS, D))]


def kernel(**inputs):
    import numpy as np
    import concourse.bacc as bacc
    from concourse.bass_utils import run_bass_kernel_spmd

    nc = bacc.Bacc("TRN2", target_bir_lowering=False, num_devices=1)
    arrays = {"in_" + name: np.ascontiguousarray(inputs[name]) for name in _INS}
    ins = {name: nc.dram_tensor("in_" + name, arrays["in_" + name].shape, F32, kind="ExternalInput").ap() for name in _INS}
    outs = {name: nc.dram_tensor("out_" + name, shape, F32, kind="ExternalOutput").ap() for name, shape in _OUTS}
    build(nc, ins, outs)
    results = run_bass_kernel_spmd(nc, [arrays], core_ids=[0]).results[0]
    return tuple(results["out_" + name] for name, _ in _OUTS)
```

```python
from contextlib import ExitStack

import concourse.bass as bass
from concourse import mybir

F32 = mybir.dt.float32
F32R = mybir.dt.float32r
BF16 = mybir.dt.bfloat16
U32 = mybir.dt.uint32
I32 = mybir.dt.int32
ALU = mybir.AluOpType
ACT = mybir.ActivationFunctionType
AX = mybir.AxisListType

P = 128
D = 1024
KT = D // P
SEQ = 512
NS = 8
T = SEQ + NS
HT = T // 2
TT = 5
ROWS = [P, P, P, P, NS]
CONV = 4
NQ, NKV, GRP, HD, WIN = 16, 4, 4, 64, 128
NB = SEQ // WIN
NG, EPG = 4, 8
NE = NG * EPG
FF = D // 2
ALPHA = 2.0 ** 0.25
EPS = 1e-5
BIG = 1e30
CAP = 64
NOV = 16
NBLK = NE + NOV
FARAWAY = 8192
XPW = 3 + SEQ + NS * CONV
XCW = XPW - 3
XS = SEQ + 3
BODY = 6
E_LOOP, E_TAIL = 4, 28
RING = 9
SLOT = 16384
AHEAD = 3

TILES = ([("lx", i) for i in range(8)] + [("k", i) for i in range(2)] + [("v", i) for i in range(2)]
         + [("q", i) for i in range(8)] + [("ly", i) for i in range(8)]
         + [("gl", i) for i in range(4)] + [("lo", i) for i in range(4)]
         + [("gl", i) for i in range(4, 8)] + [("lo", i) for i in range(4, 8)]
         + [("ga", i) for i in range(4)] + [("ao", i) for i in range(4)]
         + [("ga", i) for i in range(4, 8)] + [("ao", i) for i in range(4, 8)])
NT = len(TILES)
FIRST = {kind: min(t for t in range(NT) if TILES[t][0] == kind) for kind in dict(TILES)}
W_IN_COL = {"lx": 0, "ly": D, "q": 2 * D, "k": 3 * D, "v": 3 * D + 256, "gl": 3 * D + 512, "ga": 4 * D + 512}
BROW = {"lx": 0, "ly": 8, "q": 16, "k": 24, "v": 26, "gl": 28, "ga": 36}
R_WCONV, R_BCONV, R_BRG, R_BIG, R_LAM, NVEC = 44, 76, 84, 92, 100, 108

LAST = {"lx": "act", "k": "act", "v": "act", "q": "act", "ly": "act", "gl": "act", "ga": "act",
        "lo": "dve", "ao": "dve"}

AFTER = {}


def _place(t, *steps):
    AFTER.setdefault(t, []).extend(steps)


for _i in range(8):
    _place(_i + 1, ("gate", _i))
_place(9, ("exp", 0))
_place(10, ("exp", 4), ("sq", 0))
_place(11, ("sq", 4))
_place(12, ("root",), ("kv",))
_place(13, ("oc",), ("scan", 0))
_place(14, ("scan", 4))
_UNITS = [(p, n) for p in range(2) for n in range(NB)]
for _u in range(8):
    _t = 16 if _u == 0 else 22 + 3 * _u
    _place(_t, ("sc", _u, 0))
    _place(_t + 1, ("sc", _u, 1), ("nrm", _u, 0))
    _place(_t + 2, ("nrm", _u, 1), ("tr", _u, 0))
    _place(_t + 3, ("tr", _u, 1))
    _place(_t + 4, ("pv", _u))
_place(20, ("oh",))
_place(21, ("sk", 0))
_place(22, ("sk", 1))
_place(23, ("ss",))
_place(24, ("sn",))
_place(25, ("st",))
_place(26, ("sp",))
for _k in range(KT):
    _place(FIRST["ga"] + 11 + _k // 2, ("wo", _k))
EARLY, LATE = slice(0, 3), slice(3, TT)
ORDER = [TT - 1] + list(range(TT - 1))
STEPS = []
for _t in range(NT):
    STEPS.append(("tile", _t))
    STEPS += AFTER.get(_t, [])


def build(nc, A, O):
    ctx = ExitStack()
    with ctx:
        base = 16512

        def at(name, shape, dt, off):
            return nc.alloc_sbuf_tensor_at(name, shape, dt, offset=base + off)

        def sem(name):
            return ctx.enter_context(nc.semaphore(name))

        KB2 = T * 4
        oA, oB, oC, oD = 0, 33280, 67328, 102144
        oE, oF, oG, oH, oI, oJ = 126720, 139136, 147456, 172032, 188416, 204800
        xTh = at("xTh", [P, KT, T], F32R, oA)
        xTl = at("xTl", [P, KT, T], F32R, oA + KT * KB2)
        qT = at("qT", [P, 8, T], F32, oB)
        attH = at("attH", [P, 8, T], F32R, oB)
        vT = at("vT", [P, 2, T], F32, oB + 6 * KB2)
        gT = at("gT", [P, 8, XCW], F32, oB + 8 * KB2)
        attL = at("attL", [P, 8, T], F32R, oB + 8 * KB2)
        hL = at("hL", [P, 8, XCW], F32, oC)
        recH = at("recH", [P, 8, XCW], F32R, oC)
        aL = at("aL", [P, 8, XCW], F32, oC + 8 * XCW * 4)
        recL = at("recL", [P, 8, XCW], F32R, oC + 8 * XCW * 4)
        mgL = at("mgL", [P, 8, XCW], F32R, oC + 8 * XCW * 4)
        xrow = [at(f"xrow{n}", [P, D], F32, oC + 4096 * n) for n in range(TT)]
        vec = at("vec", [NVEC, P], F32, oC + 4096 * 5)
        st = at("st", [32, D], F32, oC + 4096 * 6)
        xp = at("xp", [P, 8, XPW], F32, oD)
        cK = at("cK", [P, NS, 256], F32, oD)
        kS = at("kS", [P, 2, NS, P], F32, oD + 8192)
        cV = at("cV", [P, NS, 256], F32, oD + 16384)
        m1 = at("m1", [P, 8, T], F32, oD)
        mgH = at("mgH", [P, 8, T], F32R, oD)
        kz = at("kz", [P, 2, 2, T], F32, oE)
        vtok = at("vtok", [P, NB, 256], F32, oE + 4 * KB2)
        wrg = at("wrg", [P, 8, P], F32, oF)
        wig = at("wig", [P, 8, P], F32, oF + 4096)
        oc = at("oc", [XPW - SEQ, D], F32, oF)
        qz = at("qz", [P, 16, 32], F32, oF)
        oh = at("oh", [NS + 1, D], F32, oF + 4096)
        sg = at("sg", [P, 4, T], F32, oF)
        raw = [at(f"raw{n}", [P, KT, 256], F32, oG + 8192 * n) for n in range(3)]
        rawL = [at(f"rawL{n}", [P, KT, 256], F32R, oG + 8192 * n) for n in range(3)]
        wh = [at(f"wh{n}", [P, KT, P], F32R, oH + 4096 * n) for n in range(AHEAD + 1)]
        xc = [at(f"xc{n}", [P, XCW], F32, oI + 2176 * n) for n in range(2)]
        si = [at(f"si{n}", [P, XCW], F32, oI + 4352 + 2176 * n) for n in range(2)]
        a2 = at("a2", [P, XCW], F32, oI + 8704)
        kwin = at("kwin", [P, 256], F32, oI + 12288)
        snew = at("snew", [NS, 512], F32, oI + 13312)
        kl = at("kl", [P, 2, P + NS], F32, oI + 10880)
        sS = [at(f"sS{n}", [P, 4, 256], F32, oI + 4096 * n) for n in range(2)]
        pT = at("pT", [P, 2, 2, 512], F32, oI + 8192)
        sSm = at("sSm", [P, 4, P], F32, oI + 8192)
        pTs = at("pTs", [P, 4, P], F32, oI + 10240)
        ident = at("ident", [P, P], F32, oJ)
        mask = at("mask", [P, 256], F32, oJ + 512)
        col = at("col", [P, NVEC], F32, oJ + 1536)
        colh = at("colh", [P, 16], F32, oJ + 1984)
        sk8 = at("sk8", [P, NQ], F32, oJ + 2048)
        sks = at("sks", [P, 1], F32, oJ + 2112)
        h0 = at("h0", [P, 8, NS], F32, oJ + 2176)
        cf = at("cf", [P, 8], F32, oJ + 2432)
        ncf = at("ncf", [P, 8], F32, oJ + 2464)
        lam = at("lam", [P, 4, 8], F32, oJ + 2496)
        mx = at("mx", [P, 2, 4], F32, oJ + 2624)
        nm = at("nm", [P, 2, 4], F32, oJ + 2656)
        es = at("es", [P, 2, 4], F32, oJ + 2688)
        dn = at("dn", [P, 2, 4], F32, oJ + 2720)
        smx = at("smx", [P, 4, 4], F32, oJ + 2752)
        epsT = at("epsT", [P, 1], F32, oJ + 2816)
        yb = at("yb", [P, T], F32, oJ + 3072)
        y2 = at("y2", [P, T], F32, oJ + 3072 + KB2)

        woH = at("woH", [P, KT, D], F32R, oA)
        wo_raw = [at(f"wo_raw{n}", [P, 4, D], F32, o) for n, o in enumerate((oC, oI))]
        woL = [at(f"woL{n}", [P, 4, D], F32R, o) for n, o in enumerate((oC, oI))]
        lnG = at("lnG", [P, D], F32, oE)
        lnB = at("lnB", [P, D], F32, oE + 4096)
        xre = [at(f"xre{n}", [P, D], F32, oF + 4096 * n) for n in range(2)]
        z1 = [at(f"z1{n}", [P, D], F32, oG + 4096 * n) for n in range(2)]
        x1 = [at(f"x1{n}", [P, D], F32, oG + 8192 + 4096 * n) for n in range(2)]
        x1T = [at(f"x1T{n}", [P, KT, P], F32, oG + 16384 + 4096 * n) for n in range(2)]
        wr = at("wr", [P, KT, NG + NE], F32, oJ + 3072)
        rb = at("rb", [P, NG + NE], F32, oJ + 3072 + 1152)
        st6 = at("st6", [P, 2, 2, 6], F32, oJ + 4480)
        mv = at("mv", [P, 3, 4], F32, oJ + 4608)
        ro = [oH]

        def rt(name, shape, dt=F32):
            n = 1
            for s in shape[1:]:
                n *= s
            t = at(name, shape, dt, ro[0])
            ro[0] += (n * (2 if dt == BF16 else 4) + 31) // 32 * 32
            return t
        lgG, lgE = rt("lgG", [P, TT, NG]), rt("lgE", [P, TT, NE])
        io4 = rt("io4", [P, NG])
        io32 = rt("io32", [P, NE])
        io128 = rt("io128", [P, P])
        io48 = rt("io48", [P, NBLK])
        tri = rt("tri", [P, P])
        triB = rt("triB", [P, P], BF16)
        oneB = rt("oneB", [P, P], BF16)
        valid = rt("valid", [P, TT])
        tokv = rt("tokv", [P, 2, TT])
        off = rt("off", [P, 1])
        w5 = [rt(f"w5{n}", [P, TT]) for n in range(8)]
        w10 = [rt(f"w10{n}", [P, 2, TT]) for n in range(8)]
        g20 = [rt(f"g20{n}", [P, TT, NG]) for n in range(3)]
        e160 = [rt("e160", [P, TT, NE])]
        e320 = [rt(f"e320{n}", [P, 2 * TT, NE]) for n in range(2)]
        esel = rt("esel", [P, TT, NE])
        hot = rt("hot", [P, 2, TT, NE])
        hotB = rt("hotB", [P, TT, NE], BF16)
        cum = rt("cum", [P, 4, NE])
        ov16 = rt("ov16", [P, NOV, NE])
        assert ro[0] <= oI
        tabG = at("tabG", [P, NBLK], U32, oJ + 4672)
        tabD = at("tabD", [P, NBLK], U32, oJ + 4864)
        tabW = at("tabW", [P, NBLK], F32, oJ + 5056)
        ovT = at("ovT", [P, NOV + 1], I32, oJ + 5248)
        ovf = at("ovf", [P, NOV + 1], F32, oJ + 5344)
        rk = at("rk", [P, 2 * TT, P], F32, oG + 12288)
        bk = at("bk", [P, 2 * TT, 3, NBLK], F32, oG + 12288 + 5120)
        bkE = at("bkE", [P, 2 * TT, NBLK], F32, oJ + 5440)
        slot = [at(f"slot{n}", [P, 8, 512], F32, SLOT * n) for n in range(RING)]
        xg = [at(f"xg{n}", [P, 512], F32, oG + 2048 * n) for n in range(BODY)]
        xt = [at(f"xt{n}", [P, 512], F32, oG + 12288 + 2048 * n) for n in range(3)]
        gu = [at(f"gu{n}", [P, 512], F32, oG + 18432 + 2048 * n) for n in range(3)]
        ys = [at(f"ys{n}", [P, 512], F32, oH + 8192 + 2048 * n) for n in range(3)]
        sgm = [at(f"sgm{n}", [P, 4, CAP], F32, oH + 1024 * n) for n in range(3)]
        hT = [at(f"hT{n}", [P, 4, CAP], F32, oH + 3072 + 1024 * n) for n in range(3)]
        idG = [at(f"idG{n}", [P, 1], U32, oH + 6144 + 32 * n) for n in range(BODY)]
        idD = [at(f"idD{n}", [P, 1], U32, oH + 6336 + 32 * n) for n in range(3)]
        f0 = [at(f"f0{n}", [P, D], F32, 4096 * n) for n in range(TT)]
        f1 = [at(f"f1{n}", [P, D], F32, 4096 * (TT + n)) for n in range(TT)]
        z2 = [at(f"z2{n}", [P, D], F32, 3 * SLOT + 4096 * n) for n in range(3)]
        y_out = [at(f"yout{n}", [P, D], F32, 3 * SLOT + 12288 + 4096 * n) for n in range(2)]
        xr2 = [at(f"xr2{n}", [P, D], F32, 6 * SLOT + 4096 * n) for n in range(TT)]
        ln2G = at("ln2G", [P, D], F32, oI)
        ln2B = at("ln2B", [P, D], F32, oI + 4096)

        pair = [ctx.enter_context(nc.psum_tensor(f"ps{n}", [P, 2, 512], F32)) for n in range(4)]
        flat = [p[:, :, :].rearrange("p a b -> p (a b)") for p in pair]
        bank = [pair[n // 2][:, n % 2, :] for n in range(8)]

        x1_half = nc.dram_tensor("x1_half", [2 * T, 512], F32, kind="Internal").ap()
        ff_half = nc.dram_tensor("ff_half", [4 * T, 512], F32, kind="Internal").ap()
        x1_rows = x1_half.rearrange("(t h) n -> t (h n)", h=2)
        ff_rows = ff_half.rearrange("(k t h) n -> k t (h n)", k=2, h=2)

        s_vec, s_st, s_wg, s_snk, s_snr = sem("vec_loaded"), sem("state_loaded"), sem("gate_w_loaded"), sem("sinks_loaded"), sem("row_sinks_loaded")
        s_x = [sem(f"token_tile_loaded{n}") for n in range(TT)]
        s_raw = [sem(f"raw_loaded{n}") for n in range(3)]
        s_cst = sem("constants_built")
        s_xT = sem("x_transposed")
        s_xh, s_xl = sem("x_hi"), sem("x_lo")
        s_vT, s_col = sem("vectors_transposed"), sem("vectors_in_columns")
        s_stT, s_stc = sem("states_transposed"), sem("states_placed")
        s_cf = sem("decay_ready")
        s_lamE = sem("lambda_exp")
        s_lam = sem("lambda_ready")
        s_hi, s_lo = sem("w_hi"), sem("w_lo")
        s_proj = sem("tile_projected")
        s_eva, s_evd = sem("tile_read_by_act"), sem("tile_read_by_dve")
        s_cv = sem("conv_done")
        s_gate = sem("gates_projected")
        s_sig = sem("gates_activated")
        s_gx = sem("gated_input")
        s_a = sem("decay_exp")
        s_om = sem("one_minus_a2")
        s_rt = sem("root_taken")
        s_h = sem("h_scanned")
        s_kvT, s_kva, s_kvd = sem("kv_transposed"), sem("v_tokens"), sem("k_window")
        s_ocT, s_ocv, s_ohT, s_ohv = sem("conv_state_T"), sem("conv_state"), sem("h_T"), sem("h_state")
        s_kv_out = sem("kv_stored")
        s_oc_out, s_oh_out = sem("conv_stored"), sem("h_stored")
        s_copy = sem("cache_copied")
        s_ck, s_cv_ld = sem("cache_k_loaded"), sem("cache_v_loaded")
        s_sc, s_ttr, s_nm = sem("scores"), sem("scores_masked"), sem("neg_max")
        s_ex, s_nrm = sem("exps"), sem("probs")
        s_tr, s_pa, s_pd = sem("probs_T"), sem("probs_T_by_act"), sem("probs_T_by_dve")
        s_pv, s_atth, s_attl = sem("attended"), sem("att_hi"), sem("att_lo")
        s_skT, s_ska, s_skd = sem("cache_T"), sem("cache_T_act"), sem("cache_T_dve")
        s_qz, s_ss, s_sm, s_se, s_sn = sem("sample_q"), sem("sample_scores"), sem("sample_max"), sem("sample_exp"), sem("sample_probs")
        s_spT, s_spc, s_spv, s_sah, s_sal = sem("sample_pT"), sem("sample_pT_copied"), sem("sample_pv"), sem("sample_att_hi"), sem("sample_att_lo")
        s_y, s_yq, s_yt, s_rec = sem("ly_read"), sem("gelu_inner"), sem("gelu_tanh"), sem("rec_ready")
        s_mg = sem("merged")
        s_ln = sem("ln1_loaded")
        s_wo = sem("w_o_loaded")
        s_mix, s_z, s_sd = sem("sum_ready"), sem("ln_stats"), sem("ln_root")
        s_x1 = sem("x1_ready")
        s_x1o = [sem(f"x1_stored{n}") for n in range(2)]
        s_x1T, s_x1c, s_lg, s_lgc = sem("x1_T"), sem("x1_T_copied"), sem("logits"), sem("logits_kept")
        s_rd, s_re = sem("route_differences"), sem("route_exps")
        s_hot, s_pre, s_oh10, s_tab, s_tabc, s_tabo = sem("one_hots"), sem("ranks"), sem("slot_one_hots"), sem("tables"), sem("tables_kept"), sem("overflow_table")
        s_rcst, s_turn = sem("router_constants"), sem("pool_turn")
        s_wx = [sem(f"chunk_loaded{n}") for n in range(RING)]
        s_ig, s_id = sem("gather_index"), sem("scatter_index")
        s_g = [sem(f"gathered{n}") for n in range(BODY)]
        s_sct = [sem(f"scattered{n}") for n in range(3)]
        s_xtp, s_xte = sem("block_T"), sem("block_T_copied")
        s_gup, s_gue = sem("gate_up"), sem("gate_up_copied")
        s_gt, s_sgm, s_h1, s_hh = sem("gate_up_T"), sem("gate_sigmoid"), sem("gate_silu"), sem("hidden")
        s_yp, s_ye = sem("block_out"), sem("block_out_scaled")
        s_ov = {n: sem("ov_" + n) for n in ("w", "ix", "g", "xt", "xe", "gu", "ge", "gt", "sg", "h1", "h", "y", "ye", "sc", "free")}
        s_l2 = sem("ln2_loaded")
        s_xr = sem("x1_again")
        s_nr, s_nz, s_y2, s_y3 = sem("ln2_factors"), sem("ln2_normal"), sem("ln2_scaled"), sem("y_ready")
        s_yo = [sem(f"y_stored{n}") for n in range(2)]
        d_c, p_c = sem("dve_order"), sem("pool_order")

        block = ctx.enter_context(nc.Block())

        def dmas(hc):
            return {"q": 4, "ao": 4}.get(TILES[2 * hc][0], 1)

        def raw_full(t):
            hc = t // 2
            return s_raw[hc % 3], 16 * sum(dmas(n) for n in range(hc % 3, hc + 1, 3))

        def emptied(t):
            who = LAST[TILES[t][0]]
            n = sum(LAST[TILES[m][0]] == who for m in range(t + 1))
            return (s_eva if who == "act" else s_evd), n

        def wcol(t, buf):
            return buf[(t // 2) % 3][:, :, (t % 2) * P:(t % 2 + 1) * P]

        def whi(t):
            return wh[t % (AHEAD + 1)][:, :, :]

        def halves(ap):
            return ap.rearrange("p (a b) -> p a b", a=2)

        def sample_cols(ap):
            return ap[:, SEQ + 3:XCW + 3:CONV] if False else ap[:, XS:XCW:CONV]

        NUNIT = len(_UNITS)

        def uses(i, c, r):
            return i * (BODY // r) + c // r + 1

        @block.sync
        def _(sp):
            sp.dma_start(xrow[0][:, :], A["x_prompt"][0, 0:P, :]).then_inc(s_x[0], 16)

            w_in = A["w_in"].rearrange("(k p) n -> p k n", p=P)
            w_q = A["w_in"][:, 2 * D:3 * D].rearrange("(k p) (P a m) -> p k P a m", p=P, P=2, a=2)
            w_lo = A["w_lru_out"].rearrange("(k p) n -> p k n", p=P)
            w_ao = A["w_attn_out"].rearrange("(P a h c) n -> P a c h n", P=2, a=2, h=4)
            w_o = A["w_o"].rearrange("(k p) n -> p k n", p=P)

            def half_chunk(hc):
                kind, i = TILES[2 * hc]
                dst, s = raw[hc % 3], s_raw[hc % 3]
                if hc >= 3:
                    sp.wait_ge(s_proj, 2 * (hc - 3) + 2)
                if kind == "q":
                    p2, m = i // 4, (i % 4) // 2
                    for a in range(2):
                        for h in range(2):
                            sp.dma_start(dst[:, :, h * P + a * HD:h * P + (a + 1) * HD],
                                         w_q[:, :, p2, a, m * P + h * HD:m * P + (h + 1) * HD]).then_inc(s, 16)
                elif kind == "ao":
                    for p2 in range(2):
                        for a in range(2):
                            sp.dma_start(dst[a * HD:(a + 1) * HD, 4 * p2:4 * p2 + 4, :],
                                         w_ao[p2, a, :, :, i * P:i * P + 256]).then_inc(s, 16)
                else:
                    w = w_lo if kind == "lo" else w_in
                    c = W_IN_COL.get(kind, 0) + i * P
                    sp.dma_start(dst[:, :, :], w[:, :, c:c + 256]).then_inc(s, 16)

            for n in range(1, 4):
                sp.dma_start(xrow[n][:, :], A["x_prompt"][0, n * P:(n + 1) * P, :]).then_inc(s_x[n], 16)
            sp.dma_start(xrow[4][0:NS, :], A["x_sample"][:, 0, :]).then_inc(s_x[4], 16)
            half_chunk(0)
            b_rows = A["b_in"].rearrange("(r c) -> r c", c=P)
            sp.dma_start(vec[0:16, :], b_rows[0:16, :]).then_inc(s_vec, 16)
            bq = A["b_in"][2 * D:3 * D].rearrange("(P a h c) -> P a h c", P=2, a=2, h=4)
            for p2 in range(2):
                for a in range(2):
                    sp.dma_start(vec[16 + 4 * p2:20 + 4 * p2, a * HD:(a + 1) * HD], bq[p2, a, :, :]).then_inc(s_vec, 16)
            sp.dma_start(vec[24:44, :], b_rows[24:44, :]).then_inc(s_vec, 16)
            sp.dma_start(vec[R_WCONV:R_BCONV, :], A["w_conv"].rearrange("j (k c) -> (j k) c", c=P)).then_inc(s_vec, 16)
            sp.dma_start(vec[R_BCONV:R_BRG, :], A["b_conv"].rearrange("(k c) -> k c", c=P)).then_inc(s_vec, 16)
            sp.dma_start(vec[R_BRG:R_BIG, :], A["b_rg"].rearrange("(k a) c -> k (a c)", a=2)).then_inc(s_vec, 16)
            sp.dma_start(vec[R_BIG:R_LAM, :], A["b_ig"].rearrange("(k a) c -> k (a c)", a=2)).then_inc(s_vec, 16)
            sp.dma_start(vec[R_LAM:NVEC, :], A["lru_lambda"].rearrange("(k c) -> k c", c=P)).then_inc(s_vec, 16)
            sp.dma_start(st[0:24, :], A["state_conv"].rearrange("b j d -> (b j) d")).then_inc(s_st, 16)
            sp.dma_start(st[24:32, :], A["state_lru_h"]).then_inc(s_st, 16)
            half_chunk(1)
            sp.wait_ge(s_cst, 2)
            for dst, src in ((wrg, A["w_rg"]), (wig, A["w_ig"])):
                blocks = src.rearrange("(k a) i j -> a i k j", a=2)
                for a in range(2):
                    sp.dma_start(dst[a * HD:(a + 1) * HD, :, a * HD:(a + 1) * HD], blocks[a, :, :, :]).then_inc(s_wg, 16)
            sp.dma_start(sk8[:, :], A["sinks"].rearrange("(a n) -> a n", a=1).to_broadcast([P, NQ])).then_inc(s_snk, 16)

            def chunk(c, e, j):
                n = 3 * j + c
                if c < 2:
                    src = A["w_gate" if c == 0 else "w_up"][bass.ds(e, 1), :, :]
                    src = src.rearrange("e (h p j) f -> p (e h) (j f)", h=2, p=P)
                    dst = slot[n][:, :, :].rearrange("p (h j) f -> p h (j f)", h=2)
                else:
                    src = A["w_down"][bass.ds(e, 1), :, :].rearrange("e (p j) d -> p (e j d)", p=P)
                    dst = slot[n][:, :, :].rearrange("p a b -> p (a b)")
                sp.dma_start(dst, src).then_inc(s_wx[n], 16)

            for hc in range(2, NT // 2):
                half_chunk(hc)
                if hc == 24:
                    sp.wait_ge(s_proj, FIRST["lo"] + 12)
                    for n in range(2):
                        sp.dma_start(wo_raw[0][:, 2 * n:2 * n + 2, :], w_o[:, 2 * n:2 * n + 2, :]).then_inc(s_wo, 16)
            sp.wait_ge(s_pv, NUNIT)
            sp.wait_ge(s_pa, 2 * NUNIT)
            for n in range(2):
                sp.dma_start(wo_raw[1][:, 2 * n:2 * n + 2, :], w_o[:, 4 + 2 * n:6 + 2 * n, :]).then_inc(s_wo, 16)
            for dst, src in ((lnG, A["ln1_g"]), (lnB, A["ln1_b"])):
                sp.dma_start(dst[:, :], src.rearrange("(a n) -> a n", a=1).to_broadcast([P, D])).then_inc(s_ln, 16)
            sp.wait_ge(s_rec, 8)
            sp.dma_start(wr[:, :, 0:NG], A["w_group"].rearrange("(k p) n -> p k n", p=P)).then_inc(s_ln, 16)
            sp.dma_start(wr[:, :, NG:], A["w_router"].rearrange("(k p) n -> p k n", p=P)).then_inc(s_ln, 16)
            sp.dma_start(rb[:, 0:NG], A["b_group"].rearrange("(a n) -> a n", a=1).to_broadcast([P, NG])).then_inc(s_ln, 16)
            sp.dma_start(rb[:, NG:], A["b_router"].rearrange("(a n) -> a n", a=1).to_broadcast([P, NE])).then_inc(s_ln, 16)

            def rows(ap, n):
                return ap[n * P:n * P + ROWS[n], :]

            def x_again(m):
                n = ORDER[m]
                src = A["x_prompt"][0, n * P:(n + 1) * P, :] if n < 4 else A["x_sample"][:, 0, :]
                sp.dma_start(xre[m % 2][0:ROWS[n], :], src).then_inc(s_x[n], 16)

            sp.wait_ge(s_mg, 8)
            x_again(0)
            x_again(1)
            chunk(2, 0, 0)
            chunk(0, 1, 1)
            for m, n in enumerate(ORDER):
                if m + 2 < TT:
                    sp.wait_ge(s_z, m + 1)
                    x_again(m + 2)
                if m == TT - 1:
                    sp.wait_ge(s_mix, TT)
                    chunk(0, 0, 0)
                    chunk(1, 0, 0)
                sp.wait_ge(s_x1, m + 1)
                sp.dma_start(rows(x1_rows, n), x1[m % 2][0:ROWS[n], :]).then_inc(s_x1o[m % 2], 16)
            for e, c in ((1, 1), (1, 2), (2, 0)):
                chunk(c, e, e)
            sp.wait_ge(s_g[0], 16)
            chunk(1, 2, 2)
            chunk(2, 2, 2)

            def next_chunks(i, c):
                e = i * BODY + c
                sp.wait_ge(s_gup, e - 2)
                chunk(0, e, c % 3)
                chunk(1, e, c % 3)
                sp.wait_ge(s_yp, e - 2)
                chunk(2, e, c % 3)

            for c in range(3, E_LOOP):
                next_chunks(0, c)
            with sp.Fori(0, (E_TAIL - E_LOOP) // BODY) as i:
                for c in range(E_LOOP, E_LOOP + BODY):
                    next_chunks(i, c)
            for c in range(E_TAIL, NE):
                next_chunks(0, c)

            for dst, src in ((ln2G, A["ln2_g"]), (ln2B, A["ln2_b"])):
                sp.dma_start(dst[:, :], src.rearrange("(a n) -> a n", a=1).to_broadcast([P, D])).then_inc(s_l2, 16)
            sp.wait_ge(s_gup, NE - 2)
            for n in ORDER:
                sp.dma_start(xr2[n][0:ROWS[n], :], rows(x1_rows, n)).then_inc(s_xr, 16)

            sp.wait_ge(s_tabo, 1)
            n_over = sp.value_load(ovT[0:1, NOV:NOV + 1], min_val=0, max_val=NOV)
            with sp.If(n_over > 0):
                with sp.Fori(0, NOV) as i:
                    ex = sp.value_load(ovT[0:1, bass.ds(i, 1)], min_val=0, max_val=NE - 1)
                    sp.wait_ge(s_ov["free"], i + 1)
                    for c in range(2):
                        src = A["w_gate" if c == 0 else "w_up"][bass.ds(ex, 1), :, :]
                        sp.dma_start(slot[c][:, :, :].rearrange("p (h j) f -> p h (j f)", h=2),
                                     src.rearrange("e (h p j) f -> p (e h) (j f)", h=2, p=P)).then_inc(s_ov["w"], 16)
                    sp.dma_start(slot[2][:, :, :].rearrange("p a b -> p (a b)"),
                                 A["w_down"][bass.ds(ex, 1), :, :].rearrange("e (p j) d -> p (e j d)", p=P)).then_inc(s_ov["w"], 16)
                sp.wait_ge(s_ov["free"], NOV + 1)

            for j in range(3):
                sp.wait_ge(s_sct[j], 16 * len(range(j, NE, 3)))
            for n in ORDER:
                sp.dma_start(f0[n][0:ROWS[n], :], rows(ff_rows[0], n)).then_inc(s_x[n], 16)
                sp.dma_start(f1[n][0:ROWS[n], :], rows(ff_rows[1], n)).then_inc(s_x[n], 16)
            for m, n in enumerate(ORDER):
                if m < TT - 1:
                    sp.wait_ge(s_y3, m + 1)
                else:
                    sp.wait_ge(s_y2, TT)
                dst = O["y_prompt"][0, n * P:(n + 1) * P, :] if n < 4 else O["y_sample"][:, 0, :]
                sp.dma_start(dst, y_out[m % 2][0:ROWS[n], :]).then_inc(s_yo[m % 2], 16)
            sp.wait_ge(s_yo[0], 48)
            sp.wait_ge(s_yo[1], 32)
            sp.wait_ge(s_x1o[0], 48)
            sp.wait_ge(s_x1o[1], 32)
            sp.wait_ge(s_kv_out, 64)
            sp.wait_ge(s_copy, 32)
            sp.wait_ge(s_oc_out, 16 * 9)
            sp.wait_ge(s_oh_out, 32)

        @block.gpsimd
        def _(pool):
            gp = nc.gpsimd
            pc = [0]

            def link(ins):
                pc[0] += 1
                ins.then_inc(p_c, 1)
                pool.wait_ge(p_c, pc[0])

            def turn():
                pool.sem_inc(s_turn, 1)

            gp.memset(wrg[:, :, :], 0.0).then_inc(s_cst, 1)
            gp.memset(wig[:, :, :], 0.0).then_inc(s_cst, 1)
            link(gp.memset(ident[:, :], 0.0))
            gp.affine_select(out=ident[:, :], in_=ident[:, :], compare_op=ALU.not_equal, fill=1.0, base=0,
                             pattern=[[-1, P]], channel_multiplier=1).then_inc(s_cst, 1)
            gp.memset(xp[:, :, 0:3], 0.0).then_inc(s_cst, 1)
            gp.memset(epsT[:, :], EPS).then_inc(s_cst, 1)
            link(gp.memset(mask[:, :], 0.0))
            link(gp.affine_select(out=mask[:, :], in_=mask[:, :], compare_op=ALU.is_gt, fill=-BIG * 8, base=0,
                                  pattern=[[1, 256]], channel_multiplier=-1))
            gp.affine_select(out=mask[:, :], in_=mask[:, :], compare_op=ALU.is_ge, fill=-BIG * 8, base=WIN,
                             pattern=[[-1, 256]], channel_multiplier=1).then_inc(s_cst, 1)
            pool.wait_ge(s_cst, 6)
            gp.memset(kz[0:HD, :, 1, :], 0.0).then_inc(s_cst, 1)
            pool.wait_ge(s_cst, 7)
            gp.memset(kz[HD:P, :, 0, :], 0.0).then_inc(s_cst, 1)
            pool.wait_ge(s_cst, 8)
            link(gp.memset(sks[:, :], 0.0))
            for g in range(4):
                src = A["sinks"][(g % 2) * 8:(g % 2) * 8 + 8].rearrange("(n a) -> n a", a=1)
                with nc.allow_non_contiguous_dma(reason="eight words"):
                    pool.dma_start(sks[32 * g:32 * g + 8, :], src).then_inc(s_snr, 16)
            pool.dma_start(O["k_win_sample"][:, 0:WIN - 1, :, :].rearrange("b w k d -> b (w k d)"),
                           A["cache_k"][:, 1:WIN, :, :].rearrange("b w k d -> b (w k d)")).then_inc(s_copy, 16)
            pool.dma_start(O["v_win_sample"][:, 0:WIN - 1, :, :].rearrange("b w k d -> b (w k d)"),
                           A["cache_v"][:, 1:WIN, :, :].rearrange("b w k d -> b (w k d)")).then_inc(s_copy, 16)
            pool.wait_ge(s_kva, 1)
            pool.dma_start(O["v_win_prompt"][0, :, :, :].rearrange("w k d -> w (k d)"), vtok[:, NB - 1, :]).then_inc(s_kv_out, 16)
            pool.wait_ge(s_kvd, 2)
            pool.dma_start(O["k_win_prompt"][0, :, :, :].rearrange("w k d -> w (k d)"), kwin[:, :]).then_inc(s_kv_out, 16)
            pool.dma_start(O["k_win_sample"][:, WIN - 1, :, :].rearrange("b k d -> b (k d)"), snew[:, 0:256]).then_inc(s_kv_out, 16)
            pool.dma_start(O["v_win_sample"][:, WIN - 1, :, :].rearrange("b k d -> b (k d)"), snew[:, 256:512]).then_inc(s_kv_out, 16)
            pool.wait_ge(s_cv, 8)
            pool.wait_ge(s_ocT, 1)
            pool.dma_start(cK[:, :, :], A["cache_k"].rearrange("b w k d -> w b (k d)")).then_inc(s_ck, 16)
            pool.dma_start(cV[1:P, :, :], A["cache_v"][:, 1:WIN, :, :].rearrange("b w k d -> w b (k d)")).then_inc(s_cv_ld, 16)
            pool.dma_start(cV[0:1, :, :], snew[:, 256:512]).then_inc(s_cv_ld, 16)
            pool.wait_ge(s_ocv, 2)
            pool.dma_start(O["conv_prompt"][0, :, :], oc[0:3, :]).then_inc(s_oc_out, 16)
            for b in range(NS):
                pool.dma_start(O["conv_sample"][b, :, :], oc[4 + 4 * b:7 + 4 * b, :]).then_inc(s_oc_out, 16)
            pool.wait_ge(s_oc_out, 16 * 9)
            gp.memset(qz[:, :, :], 0.0).then_inc(s_qz, 1)
            pool.wait_ge(s_ohv, 2)
            pool.dma_start(O["h_prompt"], oh[0:1, :]).then_inc(s_oh_out, 16)
            pool.dma_start(O["h_sample"], oh[1:NS + 1, :]).then_inc(s_oh_out, 16)

            pool.wait_ge(s_proj, NT)
            gp.memset(lgG[:, :, :], 0.0).then_inc(s_rcst, 1)
            gp.memset(lgE[:, :, :], 0.0).then_inc(s_rcst, 1)
            gp.iota(io4[:, :], [[1, NG]], base=0, channel_multiplier=0, allow_small_or_imprecise_dtypes=True).then_inc(s_rcst, 1)
            gp.iota(io32[:, :], [[1, NE]], base=0, channel_multiplier=0, allow_small_or_imprecise_dtypes=True).then_inc(s_rcst, 1)
            gp.iota(io128[:, :].rearrange("p (a b) -> p a b", a=2), [[0, 2], [1, CAP]], base=0, channel_multiplier=0,
                    allow_small_or_imprecise_dtypes=True).then_inc(s_rcst, 1)
            gp.iota(io48[:, :], [[1, NBLK]], base=0, channel_multiplier=0, allow_small_or_imprecise_dtypes=True).then_inc(s_rcst, 1)
            gp.iota(tokv[:, :, 0:1], [[0, 2], [0, 1]], base=2 * SEQ - FARAWAY, channel_multiplier=2,
                    allow_small_or_imprecise_dtypes=True).then_inc(s_rcst, 1)
            gp.iota(tokv[:, :, 1:TT], [[0, 2], [2 * P, TT - 1]], base=-FARAWAY, channel_multiplier=2,
                    allow_small_or_imprecise_dtypes=True).then_inc(s_rcst, 1)
            link(gp.memset(tri[:, :], 1.0))
            link(gp.affine_select(out=tri[:, :], in_=tri[:, :], compare_op=ALU.is_gt, fill=0.0, base=0,
                                  pattern=[[1, P]], channel_multiplier=-1))
            gp.tensor_copy(triB[:, :], tri[:, :]).then_inc(s_rcst, 1)
            gp.memset(oneB[:, :], 1.0).then_inc(s_rcst, 1)
            link(gp.memset(valid[:, :], 1.0))
            gp.affine_select(out=valid[:, 0:1], in_=valid[:, 0:1], compare_op=ALU.is_gt, fill=0.0, base=NS,
                             pattern=[[0, 1]], channel_multiplier=-1).then_inc(s_rcst, 1)
            pool.wait_ge(s_rcst, 11)
            gp.memset(off[0:CAP, :], float(FARAWAY)).then_inc(s_rcst, 1)
            pool.wait_ge(s_rcst, 12)
            gp.memset(off[CAP:P, :], float(FARAWAY + 1)).then_inc(s_rcst, 1)

            pool.wait_ge(s_rcst, 13)
            pool.wait_ge(s_x1o[0], 48)
            pool.wait_ge(s_x1o[1], 32)
            pool.wait_ge(s_lg, TT)
            for j in range(BODY):
                link(gp.memset(xg[j][:, :], 0.0))
            pool.wait_ge(s_tabc, 3)

            def fetch(dst, index, signal):
                pool.indirect_dma_start(out=dst[:, :], out_offset=None, in_=x1_half,
                                        in_offset=bass.IndirectOffsetOnAxis(ap=index[:, 0:1], axis=0),
                                        bounds_check=2 * T - 1, oob_is_err=False).then_inc(signal, 16)

            def store(src, index, signal):
                pool.indirect_dma_start(out=ff_half, out_offset=bass.IndirectOffsetOnAxis(ap=index[:, 0:1], axis=0),
                                        in_=src[:, :], in_offset=None,
                                        bounds_check=4 * T - 1, oob_is_err=False).then_inc(signal, 16)

            def gather(i, c, first=False):
                e, j = i * BODY + c, c % BODY
                if not first:
                    pool.wait_ge(s_xtp, e - 5)
                gp.tensor_copy(idG[j][:, :], tabG[:, bass.ds(e, 1)]).then_inc(s_ig, 1)
                pool.wait_ge(s_ig, e + 1)
                turn()
                fetch(xg[j], idG[j], s_g[j])

            def scatter(i, c):
                e, j = i * BODY + c, c % 3
                if c >= 3:
                    pool.wait_ge(s_sct[j], uses(i, c - 3, 3) * 16)
                gp.tensor_copy(idD[j][:, :], tabD[:, bass.ds(e, 1)]).then_inc(s_id, 1)
                pool.wait_ge(s_id, e + 1)
                pool.wait_ge(s_ye, e + 1)
                turn()
                store(ys[j], idD[j], s_sct[j])

            for e in range(4):
                gather(0, e, True)
            for e in range(E_LOOP):
                gather(0, e + 4, e < 2)
                if e:
                    scatter(0, e - 1)
            with pool.Fori(0, (E_TAIL - E_LOOP) // BODY) as i:
                for c in range(E_LOOP, E_LOOP + BODY):
                    gather(i, c + 4)
                    scatter(i, c - 1)
            for e in range(E_TAIL, NE + 1):
                scatter(0, e - 1)

            pool.wait_ge(s_tabo, 1)
            n_over = pool.value_load(ovT[0:1, NOV:NOV + 1], min_val=0, max_val=NOV)
            with pool.If(n_over > 0):
                for j in range(3):
                    pool.wait_ge(s_sct[j], 16 * len(range(j, NE, 3)))
                pool.sem_inc(s_ov["free"], 1)
                with pool.Fori(0, NOV) as i:
                    pool.wait_ge(s_ov["free"], i + 1)
                    gp.tensor_copy(idG[0][:, :], tabG[:, bass.ds(i + NE, 1)]).then_inc(s_ov["ix"], 1)
                    gp.tensor_copy(idD[0][:, :], tabD[:, bass.ds(i + NE, 1)]).then_inc(s_ov["ix"], 1)
                    pool.wait_ge(s_ov["ix"], i * 2 + 2)
                    turn()
                    fetch(xg[0], idG[0], s_ov["g"])
                    pool.wait_ge(s_ov["ye"], i + 1)
                    turn()
                    store(ys[0], idD[0], s_ov["sc"])
                    pool.wait_ge(s_ov["sc"], i * 16 + 16)
                    pool.sem_inc(s_ov["free"], 1)

            for m, n in enumerate(ORDER[:-1]):
                r = ROWS[n]
                pool.wait_ge(s_l2, 32)
                pool.wait_ge(s_y2, m + 1)
                if m == 1:
                    pool.wait_ge(s_y3, 1)
                if m >= 2:
                    pool.wait_ge(s_yo[m % 2], 16 * (m // 2))
                gp.tensor_tensor(y_out[m % 2][0:r, :], z2[m % 3][0:r, :], ln2B[0:r, :], ALU.add).then_inc(s_y3, 1)

        @block.tensor
        def _(pe):
            mm = nc.tensor.matmul

            def passes(out_of, hi, lo, rhs_h, rhs_l):
                last = None
                for k in range(KT):
                    for n, (w, x) in enumerate(((hi, rhs_h), (hi, rhs_l), (lo, rhs_h))):
                        for a in range(2):
                            last = mm(out_of[:, a, 0:HT], w[:, k, :], x[:, k, a * HT:(a + 1) * HT],
                                      start=(k == 0 and n == 0), stop=(k == KT - 1 and n == 2))
                return last

            pe.wait_ge(s_cst, 3)
            for n in range(TT):
                r = ROWS[n]
                pe.wait_ge(s_x[n], 16)
                if n >= 2:
                    pe.wait_ge(s_xl, n - 1)
                for k in range(KT):
                    last = nc.tensor.transpose(flat[n % 2][:, k * P:k * P + r], xrow[n][0:r, k * P:(k + 1) * P], ident[0:r, 0:r])
                last.then_inc(s_xT, 1)
            def tile(t):
                kind, i = TILES[t]
                rhs_h, rhs_l = {"lo": (recH, recL), "ao": (attH, attL)}.get(kind, (xTh, xTl))
                if t == 0:
                    pe.wait_ge(s_xl, TT)
                if kind == "lo" and i == 0:
                    pe.wait_ge(s_rec, 8)
                if kind == "ao" and i == 0:
                    pe.wait_ge(s_attl, NUNIT)
                    pe.wait_ge(s_sal, 2)
                    pe.wait_ge(s_sah, 2)
                pe.wait_ge(s_hi, t + 1)
                pe.wait_ge(s_lo, t + 1)
                if t >= 2:
                    pe.wait_ge(*emptied(t - 2))
                passes(pair[t % 2], wh[t % (AHEAD + 1)], wcol(t, rawL), rhs_h, rhs_l).then_inc(s_proj, 1)

            def gate(i):
                if i == 0:
                    pe.wait_ge(s_wg, 64)
                    pe.wait_ge(s_stc, 2)
                    pe.wait_ge(s_col, 1)
                else:
                    pe.wait_ge(s_sig, 3 * i - 1)
                pe.wait_ge(s_cv, i + 1)
                for w, out in ((wrg, pair[2]), (wig, pair[3])):
                    for a in range(2):
                        last = mm(out[:, a, 0:XCW // 2], w[:, i, :], xc[i % 2][:, a * (XCW // 2):(a + 1) * (XCW // 2)],
                                  start=True, stop=True)
                last.then_inc(s_gate, 1)

            def kv():
                pe.wait_ge(s_sig, 3 * 7 + 2)
                pe.wait_ge(*emptied(11))
                for n in range(NB):
                    for p2 in range(2):
                        nc.tensor.transpose(flat[3][:, n * 256 + p2 * P:n * 256 + (p2 + 1) * P], vT[:, p2, n * P:(n + 1) * P], ident[:, :])
                for p2 in range(2):
                    nc.tensor.transpose(bank[4][:, p2 * P:(p2 + 1) * P], kl[:, p2, 0:P], ident[:, :])
                    nc.tensor.transpose(bank[5][0:NS, p2 * P:(p2 + 1) * P], kl[:, p2, P:P + NS], ident[:, :])
                    last = nc.tensor.transpose(bank[5][0:NS, 256 + p2 * P:256 + (p2 + 1) * P], vT[:, p2, SEQ:T], ident[:, :])
                last.then_inc(s_kvT, 1)

            def conv_state():
                pe.wait_ge(s_kvd, 2)
                for k in range(KT):
                    last = nc.tensor.transpose(flat[2][0:XPW - SEQ, k * P:(k + 1) * P], xp[:, k, SEQ:XPW], ident[:, :])
                last.then_inc(s_ocT, 1)

            def h_state():
                pe.wait_ge(s_h, 16)
                pe.wait_ge(s_ttr, 8)
                for k in range(KT):
                    last = nc.tensor.transpose(flat[2][0:NS + 1, k * P:(k + 1) * P], hL[:, k, SEQ - 1:T], ident[:, :])
                last.then_inc(s_ohT, 1)

            def scores(u, par):
                p2, n = _UNITS[u]
                if par == 0:
                    if n == 0:
                        pe.wait_ge(*emptied(FIRST["q"] + 4 * p2 + 3))
                    if u == 0:
                        pe.wait_ge(s_ocv, 2)
                    elif u == 1:
                        pe.wait_ge(s_ohv, 2)
                        pe.wait_ge(s_sm, 1)
                    else:
                        pe.wait_ge(s_ttr, 4 * 2 * u)
                else:
                    pe.wait_ge(s_ttr, 4 * (2 * u + 1))
                lo = 0 if n else P
                for h in range(GRP):
                    last = mm(pair[2][:, h // 2, (h % 2) * 256 + lo:(h % 2) * 256 + 256], qT[:, 4 * p2 + h, n * P:(n + 1) * P],
                              kz[:, p2, par, (n - 1) * P + lo:(n + 1) * P], start=True, stop=True)
                last.then_inc(s_sc, 1)

            def probs_t(u, par):
                p2, n = _UNITS[u]
                pe.wait_ge(s_nrm, 4 * (2 * u + par + 1))
                m = 2 * u + par
                if m == 0:
                    pe.wait_ge(s_kva, 1)
                elif m == 2:
                    pe.wait_ge(s_sah, 2)
                    pe.wait_ge(s_sal, 2)
                    pe.wait_ge(s_spc, 1)
                if u >= 1 and par == 0:
                    pe.wait_ge(s_attl, u)
                if m >= 1:
                    pe.wait_ge(s_pa, m)
                    pe.wait_ge(s_pd, m)
                for kt in range(2):
                    if n == 0 and kt == 0:
                        continue
                    for h in range(GRP):
                        to = 6 + (kt if n else h // 2)
                        last = nc.tensor.transpose(bank[to][:, h * P:(h + 1) * P], sS[par][:, h, kt * P:(kt + 1) * P], ident[:, :])
                last.then_inc(s_tr, 1)

            def attend(u):
                p2, n = _UNITS[u]
                pe.wait_ge(s_pa, 2 * u + 2)
                pe.wait_ge(s_pd, 2 * u + 2)
                kts = (1,) if n == 0 else (0, 1)
                for kt in kts:
                    for par in range(2):
                        last = mm(bank[6][par * HD:(par + 1) * HD, :], vtok[:, n - 1 + kt, (2 * p2 + par) * HD:(2 * p2 + par + 1) * HD],
                                  pT[:, par, kt, :], start=(kt == kts[0]), stop=(kt == 1))
                last.then_inc(s_pv, 1)

            def cache_t(r):
                if r == 0:
                    pe.wait_ge(s_ck, 16)
                    pe.wait_ge(s_attl, 1)
                    pe.wait_ge(s_pd, 2)
                else:
                    pe.wait_ge(s_ska, 1)
                    pe.wait_ge(s_skd, 1)
                for b in range(4 * r, 4 * r + 4):
                    for p2 in range(2):
                        last = nc.tensor.transpose(bank[6 + p2][:, (b % 4) * P:(b % 4 + 1) * P], cK[:, b, p2 * P:(p2 + 1) * P], ident[:, :])
                last.then_inc(s_skT, 1)

            def sample_scores():
                pe.wait_ge(s_skd, 6)
                pe.wait_ge(s_ska, 2)
                pe.wait_ge(s_qz, 5)
                pe.wait_ge(s_ohv, 2)
                for m in range(16):
                    last = mm(bank[4][32 * (m % 4):32 * (m % 4) + 32, (m // 4) * P:(m // 4 + 1) * P], qz[:, m, :],
                              kS[:, m % 2, m // 2, :], start=True, stop=True)
                last.then_inc(s_ss, 1)

            def sample_t():
                pe.wait_ge(s_sn, 4)
                for m in range(4):
                    last = nc.tensor.transpose(bank[7][:, m * P:(m + 1) * P], sSm[:, m, :], ident[:, :])
                last.then_inc(s_spT, 1)

            def sample_pv():
                pe.wait_ge(s_spc, 1)
                pe.wait_ge(s_cv_ld, 32)
                for m in range(16):
                    last = mm(bank[6][:, m * 8:(m + 1) * 8], cV[:, m // 2, (m % 2) * P:(m % 2 + 1) * P],
                              pTs[:, m // 4, 32 * (m % 4):32 * (m % 4) + 8], start=True, stop=True)
                last.then_inc(s_spv, 1)

            def vectors_t():
                pe.wait_ge(s_vec, 16 * 11)
                nc.tensor.transpose(bank[4][:, 0:NVEC], vec[:, :], ident[0:NVEC, 0:NVEC]).then_inc(s_vT, 1)
                pe.wait_ge(s_st, 32)
                for k in range(KT):
                    last = nc.tensor.transpose(bank[5][:, k * 32:(k + 1) * 32], st[:, k * P:(k + 1) * P], ident[0:32, 0:32])
                last.then_inc(s_stT, 1)

            vectors_t()
            for step in STEPS:
                what, args = step[0], step[1:]
                if what == "tile":
                    tile(*args)
                elif what == "gate":
                    gate(*args)
                elif what == "kv":
                    kv()
                elif what == "oc":
                    conv_state()
                elif what == "oh":
                    h_state()
                elif what == "sc":
                    scores(*args)
                elif what == "tr":
                    probs_t(*args)
                elif what == "pv":
                    attend(*args)
                elif what == "sk":
                    cache_t(*args)
                elif what == "ss":
                    sample_scores()
                elif what == "st":
                    sample_t()
                elif what == "sp":
                    sample_pv()

            def mix(m, ks=range(KT)):
                n = ORDER[m]
                cols = slice(n * P, n * P + ROWS[n])
                out = pair[m % 2]
                if ks[0] == 0 and m < 2:
                    pe.wait_ge(*emptied(NT - 2 + m))
                elif ks[0] == 0:
                    pe.wait_ge(s_z, m - 1)
                for k in ks:
                    if m == 0:
                        pe.wait_ge(s_mg, k + 1)
                        pe.wait_ge(s_hi, NT + k + 1)
                        pe.wait_ge(s_lo, NT + k + 1)
                    lo = woL[k // 4][:, k % 4, :]
                    for p, (x, w) in enumerate(((mgH, woH[:, k, :]), (mgH, lo), (mgL, woH[:, k, :]))):
                        for h in range(2):
                            last = mm(out[0:ROWS[n], h, :], x[:, k, cols], w[:, h * 512:(h + 1) * 512],
                                      start=(k == 0 and p == 0), stop=(k == KT - 1 and p == 2))
                if ks[-1] == KT - 1:
                    last.then_inc(s_mix, 1)

            def x1_t(m):
                r, k2 = ROWS[ORDER[m]], m % 2
                pe.wait_ge(s_x1, m + 1)
                if m >= 1:
                    pe.wait_ge(s_x1c, m)
                for k in range(KT):
                    last = nc.tensor.transpose(flat[2][:, k * P:k * P + r], x1[k2][0:r, k * P:(k + 1) * P], ident[0:r, 0:r])
                last.then_inc(s_x1T, 1)

            def logits(m):
                r, k2 = ROWS[ORDER[m]], m % 2
                pe.wait_ge(s_x1c, m + 1)
                if m >= 2:
                    pe.wait_ge(s_lgc, 2 * m - 2)
                for k in range(KT):
                    last = mm(bank[6 + k2][0:r, 0:NG + NE], x1T[k2][:, k, 0:r], wr[:, k, :], start=(k == 0), stop=(k == KT - 1))
                last.then_inc(s_lg, 1)

            mix(0)
            mix(1)
            x1_t(0)
            mix(2)
            logits(0)
            x1_t(1)
            mix(3)
            logits(1)
            x1_t(2)
            mix(4, range(KT // 2))
            logits(2)
            x1_t(3)
            mix(4, range(KT // 2, KT))
            logits(3)
            x1_t(4)
            logits(4)

            pe.wait_ge(s_rcst, 13)
            pe.wait_ge(s_hot, 2)
            for n in range(TT):
                mm(bank[7][:, n * NE:(n + 1) * NE], triB[:, :], hotB[:, n, :], start=True, stop=(n == 0))
                for m in range(n):
                    mm(bank[7][:, n * NE:(n + 1) * NE], oneB[:, :], hotB[:, m, :], start=False, stop=(m == n - 1))
            for m in range(TT):
                last = mm(bank[7][:, TT * NE:(TT + 1) * NE], oneB[:, :], hotB[:, m, :], start=(m == 0), stop=(m == TT - 1))
            last.then_inc(s_pre, 1)
            for m in range(2 * TT):
                if m % TT == 0:
                    pe.wait_ge(s_oh10, m // TT + 1)
                last = mm(bank[6][:, 0:3 * NBLK], rk[:, m, :], bk[:, m, :, :].rearrange("p a b -> p (a b)"),
                          start=(m == 0), stop=(m == 2 * TT - 1))
            last.then_inc(s_tab, 1)

            def block_t(i, c):
                pe.wait_ge(s_g[c % BODY], uses(i, c, BODY) * 16)
                if c:
                    pe.wait_ge(s_xte, i * BODY + c)
                transpose_x(xg[c % BODY], s_xtp)

            def transpose_x(src, signal):
                for q in range(4):
                    last = nc.tensor.transpose(bank[0][:, q * P:(q + 1) * P], src[:, q:512:4], ident[:, :])
                last.then_inc(signal, 1)

            def gate_up(i, c):
                e, j = i * BODY + c, c % 3
                pe.wait_ge(s_xte, e + 1)
                pe.wait_ge(s_wx[3 * j], uses(i, c, 3) * 16)
                pe.wait_ge(s_wx[3 * j + 1], uses(i, c, 3) * 16)
                if c >= 3:
                    pe.wait_ge(s_gue, e - 2)
                product_gu(bank[1 + j], xt[j], slot[3 * j], slot[3 * j + 1], s_gup)

            def product_gu(out, x, w_gate, w_up, signal):
                for k in range(8):
                    w = x[:, (k % 4) * P + (k // 4) * CAP:(k % 4) * P + (k // 4) * CAP + CAP]
                    mm(out[0:CAP, :], w, w_gate[:, k, :], start=(k == 0), stop=(k == 7))
                    last = mm(out[CAP:P, :], w, w_up[:, k, :], start=(k == 0), stop=(k == 7))
                last.then_inc(signal, 1)

            def gate_up_t(i, c):
                e = i * BODY + c
                pe.wait_ge(s_gue, e + 1)
                if c:
                    pe.wait_ge(s_hh, e)
                transpose_gu(gu[c % 3], s_gt)

            def transpose_gu(src, signal):
                for q in range(4):
                    last = nc.tensor.transpose(bank[4][:, q * P:(q + 1) * P], src[:, q:512:4], ident[:, :])
                last.then_inc(signal, 1)

            def down(i, c):
                e, j = i * BODY + c, c % 3
                pe.wait_ge(s_hh, e + 1)
                pe.wait_ge(s_wx[3 * j + 2], uses(i, c, 3) * 16)
                if c >= 3:
                    pe.wait_ge(s_ye, e - 2)
                product_down(bank[5 + j], hT[j], slot[3 * j + 2], s_yp)

            def product_down(out, h, w_down, signal):
                for q in range(4):
                    for a in range(2):
                        last = mm(out[a * CAP:(a + 1) * CAP, :], h[:, q, :], w_down[:, 2 * q + a, :],
                                  start=(q == 0), stop=(q == 3))
                last.then_inc(signal, 1)

            def expert(i, c):
                gate_up(i, c)
                if not (isinstance(i, int) and c + 1 == NE):
                    block_t(i, c + 1)
                if c:
                    down(i, c - 1)
                gate_up_t(i, c)

            pe.wait_ge(s_tabc, 3)
            block_t(0, 0)
            for e in range(E_LOOP):
                expert(0, e)
            with pe.Fori(0, (E_TAIL - E_LOOP) // BODY) as i:
                for c in range(E_LOOP, E_LOOP + BODY):
                    expert(i, c)
            for e in range(E_TAIL, NE):
                expert(0, e)
            down(0, NE - 1)

            pe.wait_ge(s_tabo, 1)
            n_over = pe.value_load(ovT[0:1, NOV:NOV + 1], min_val=0, max_val=NOV)
            with pe.If(n_over > 0):
                with pe.Fori(0, NOV) as i:
                    pe.wait_ge(s_ov["free"], i + 1)
                    pe.wait_ge(s_ov["g"], i * 16 + 16)
                    transpose_x(xg[0], s_ov["xt"])
                    pe.wait_ge(s_ov["xe"], i + 1)
                    pe.wait_ge(s_ov["w"], i * 48 + 48)
                    product_gu(bank[1], xt[0], slot[0], slot[1], s_ov["gu"])
                    pe.wait_ge(s_ov["ge"], i + 1)
                    transpose_gu(gu[0], s_ov["gt"])
                    pe.wait_ge(s_ov["h"], i + 1)
                    product_down(bank[5], hT[0], slot[2], s_ov["y"])

            for m, n in enumerate(ORDER):
                r = ROWS[n]
                if m == 0:
                    pe.wait_ge(s_ye, NE)
                    continue
                pe.wait_ge(s_x[n], 64)
                if m >= 3:
                    pe.wait_ge(s_z, TT + m - 1)
                for h in range(2):
                    for k, f in enumerate((f0, f1)):
                        last = mm(pair[m % 2][0:r, h, :], ident[0:r, 0:r], f[n][0:r, h * 512:(h + 1) * 512], start=(k == 0), stop=(k == 1))
                last.then_inc(s_mix, 1)

        @block.scalar
        def _(act):
            sc = nc.scalar
            for n in range(TT):
                r = ROWS[n]
                act.wait_ge(s_xT, n + 1)
                sc.activation(xTh[:, :, n * P:n * P + r], flat[n % 2].rearrange("p (k c) -> p k c", k=KT)[:, :, 0:r],
                              ACT.Copy).then_inc(s_xh, 1)

            def w_hi(t):
                act.wait_ge(*raw_full(t))
                if t > AHEAD:
                    act.wait_ge(s_proj, t - AHEAD)
                sc.activation(whi(t), wcol(t, raw), ACT.Copy).then_inc(s_hi, 1)

            def read_tile(t):
                kind, i = TILES[t]
                ps = pair[t % 2]
                both = ps[:, :, 0:HT]
                if LAST[kind] == "act":
                    act.wait_ge(s_proj, t + 1)
                if kind in BROW:
                    bias = col[:, BROW[kind] + i:BROW[kind] + i + 1]
                if kind == "lx":
                    if i == 0:
                        act.wait_ge(s_cst, 4)
                        act.wait_ge(s_col, 1)
                    sc.activation(xp[:, i, 3:3 + HT], ps[:, 0, 0:HT], ACT.Identity, bias=bias)
                    sc.activation(xp[:, i, 3 + HT:3 + SEQ], ps[:, 1, 0:SEQ - HT], ACT.Identity, bias=bias)
                    sc.activation(xp[:, i, 3 + SEQ + 3:XPW:CONV], ps[:, 1, SEQ - HT:HT], ACT.Identity, bias=bias).then_inc(s_eva, 1)
                elif kind == "k":
                    if i == 0:
                        act.wait_ge(s_cst, 8)
                    for a in range(2):
                        half = slice(a * HD, (a + 1) * HD)
                        sc.activation(halves(kz[half, i, a, :]), both[half], ACT.Identity, bias=bias[half])
                    lo = SEQ - P - HT
                    sc.activation(kl[:, i, :], ps[:, 1, lo:HT], ACT.Identity, bias=bias).then_inc(s_eva, 1)
                elif kind == "v":
                    sc.activation(halves(vT[:, i, :]), both, ACT.Identity, bias=bias).then_inc(s_eva, 1)
                elif kind == "q":
                    if i == 6:
                        act.wait_ge(s_kvT, 1)
                    sc.activation(halves(qT[:, i, :]), both, ACT.Identity, bias=bias).then_inc(s_eva, 1)
                elif kind == "ly":
                    if i >= 1:
                        act.wait_ge(s_rec, i)
                    sc.activation(yb[:, :].rearrange("p (a b) -> p a b", a=2), both, ACT.Identity, bias=bias).then_inc(s_y, 1)
                    sc.activation(y2[:, :].rearrange("p (a b) -> p a b", a=2), both, ACT.Square, bias=bias).then_inc(s_eva, 1)
                    act.wait_ge(s_yq, 2 * (i + 1))
                    sc.activation(y2[:, :], y2[:, :], ACT.Tanh, scale=0.7978845608028654).then_inc(s_yt, 1)
                elif kind in ("gl", "ga"):
                    if kind == "gl" and i == 0:
                        act.wait_ge(s_oh_out, 32)
                        act.wait_ge(s_ss, 1)
                    if kind == "gl" and i == 4:
                        act.wait_ge(*emptied(FIRST["lo"] + 3))
                    if kind == "ga" and i == 0:
                        act.wait_ge(*emptied(FIRST["ga"] - 1))
                    if kind == "ga" and i == 4:
                        act.wait_ge(s_mg, 4)
                    b2 = colh[:, BROW[kind] - 28 + i:BROW[kind] - 28 + i + 1]
                    sc.activation(halves(sg[:, i % 4, :]), both, ACT.Tanh, bias=b2, scale=0.5).then_inc(s_eva, 1)

            def wo_hi(k):
                if k == 0:
                    act.wait_ge(s_wo, 64)
                    act.wait_ge(s_proj, FIRST["ga"] + 12)
                sc.activation(woH[:, k, :], wo_raw[k // 4][:, k % 4, :], ACT.Copy, scale=0.5).then_inc(s_hi, 1)

            def gate(i):
                act.wait_ge(s_gate, i + 1)
                if i == 0:
                    act.wait_ge(s_cf, 1)
                if i >= 2:
                    act.wait_ge(s_gx, i - 1)
                sc.activation(aL[:, i, :].rearrange("p (a b) -> p a b", a=2), pair[2][:, :, 0:XCW // 2], ACT.Sigmoid,
                              bias=col[:, R_BRG + i:R_BRG + i + 1]).then_inc(s_sig, 1)
                sc.activation(si[i % 2][:, :].rearrange("p (a b) -> p a b", a=2), pair[3][:, :, 0:XCW // 2], ACT.Sigmoid,
                              bias=col[:, R_BIG + i:R_BIG + i + 1]).then_inc(s_sig, 1)
                act.wait_ge(s_sig, 3 * i + 1)
                sc.activation(hL[:, i, :], aL[:, i, :], ACT.Tanh, scale=ncf[:, i:i + 1]).then_inc(s_sig, 1)

            def decay(first):
                for i in range(first, first + 4):
                    act.wait_ge(s_sig, 3 * (i + 1))
                    sc.activation(aL[:, i, :], aL[:, i, :], ACT.Exp, scale=cf[:, i:i + 1]).then_inc(s_a, 1)

            def root():
                for i in range(8):
                    act.wait_ge(s_om, 2 * (i + 1))
                    sc.activation(hL[:, i, :], hL[:, i, :], ACT.Sqrt).then_inc(s_rt, 1)

            def kv():
                act.wait_ge(s_kvT, 1)
                sc.activation(vtok[:, :, :].rearrange("p n c -> p (n c)"), flat[3], ACT.Copy).then_inc(s_kva, 1)

            def exps(u, par):
                p2, n = _UNITS[u]
                lo = 0 if n else P
                m = 2 * u + par
                act.wait_ge(s_nm, 2 * m + 2)
                for h in range(GRP):
                    sc.activation(sS[par][:, h, lo:256], sS[par][:, h, lo:256], ACT.Exp, bias=nm[:, par, h:h + 1],
                                  accum_out=dn[:, par, h:h + 1]).then_inc(s_ex, 1)
                sc.activation(es[:, par, :], es[:, par, :], ACT.Exp).then_inc(s_ex, 1)

            def probs_t(u, par):
                p2, n = _UNITS[u]
                act.wait_ge(s_tr, 2 * u + par + 1)
                if u >= 1:
                    act.wait_ge(s_pv, u)
                if u == 1:
                    act.wait_ge(s_spv, 1)
                if n:
                    sc.activation(pT[:, par, 0, :], bank[6], ACT.Copy).then_inc(s_pa, 1)
                else:
                    sc.activation(pT[:, par, 1, 0:256], bank[6][:, 0:256], ACT.Copy).then_inc(s_pa, 1)

            def attend(u):
                p2, n = _UNITS[u]
                act.wait_ge(s_pv, u + 1)
                sc.activation(attH[:, 4 * p2:4 * p2 + 4, n * P:(n + 1) * P], bank[6].rearrange("p (h q) -> p h q", h=4),
                              ACT.Copy).then_inc(s_atth, 1)

            def cache_t(r):
                act.wait_ge(s_skT, r + 1)
                sc.activation(kS[:, 0, 4 * r:4 * r + 4, :], bank[6].rearrange("p (b w) -> p b w", b=4), ACT.Copy).then_inc(s_ska, 1)

            def sample_exps():
                act.wait_ge(s_sm, 7)
                for m in range(4):
                    sc.activation(sSm[:, m, :], sSm[:, m, :], ACT.Exp, bias=smx[:, 1, m:m + 1],
                                  accum_out=smx[:, 3, m:m + 1]).then_inc(s_se, 1)
                sc.activation(smx[:, 2, :], smx[:, 2, :], ACT.Exp).then_inc(s_se, 1)

            def sample_att():
                act.wait_ge(s_spv, 1)
                o = bank[6][:, 0:P].rearrange("p (b P a h) -> p P a h b", b=NS, P=2, a=2)
                for a in range(2):
                    half = slice(a * HD, (a + 1) * HD)
                    for p2 in range(2):
                        ins = sc.activation(attH[half, 4 * p2:4 * p2 + 4, SEQ:T], o[half, p2, a, :, :], ACT.Copy)
                    ins.then_inc(s_sah, 1)

            for t in range(AHEAD):
                w_hi(t)
            act.wait_ge(s_lam, 1)
            sc.activation(lam[:, 1, :], lam[:, 0, :], ACT.Exp, scale=-1.0).then_inc(s_lamE, 1)
            for step in STEPS:
                what, args = step[0], step[1:]
                if what == "tile":
                    t = args[0]
                    if t + AHEAD < NT:
                        w_hi(t + AHEAD)
                    if LAST[TILES[t][0]] == "act":
                        read_tile(t)
                elif what == "gate":
                    gate(*args)
                elif what == "exp":
                    decay(*args)
                elif what == "root":
                    root()
                elif what == "kv":
                    kv()
                elif what == "sc":
                    exps(*args)
                elif what == "tr":
                    probs_t(*args)
                elif what == "pv":
                    attend(*args)
                elif what == "sk":
                    cache_t(*args)
                elif what == "ss":
                    sample_exps()
                elif what == "sp":
                    sample_att()
                elif what == "wo":
                    wo_hi(*args)

            def root_of(m, before):
                r = ROWS[ORDER[m]]
                act.wait_ge(s_z, before + m + 1)
                sc.activation(mv[0:r, m % 3, 2:3], mv[0:r, m % 3, 1:2], ACT.Sqrt, bias=epsT[0:r, :]).then_inc(s_sd, 1)

            def x1_t(m):
                r = ROWS[ORDER[m]]
                act.wait_ge(s_x1T, m + 1)
                if m >= 2:
                    act.wait_ge(s_lg, m - 1)
                sc.activation(x1T[m % 2][:, :, 0:r], flat[2].rearrange("p (k c) -> p k c", k=KT)[:, :, 0:r], ACT.Copy).then_inc(s_x1c, 1)

            act.wait_ge(s_cst, 5)
            def routing_exps(part, ts):
                act.wait_ge(s_rd, 2 * part + 1)
                sc.activation(g20[0][:, ts, :], g20[0][:, ts, :], ACT.Exp).then_inc(s_re, 1)
                act.wait_ge(s_rd, 2 * part + 2)
                sc.activation(w5[3][:, ts], w5[3][:, ts], ACT.Exp).then_inc(s_re, 1)

            root_of(0, 0)
            for m in range(TT):
                x1_t(m)
                if m == TT - 2:
                    routing_exps(0, EARLY)
                if m + 1 < TT:
                    root_of(m + 1, 0)
            routing_exps(1, LATE)
            def copy_gu(i, c):
                e, j = i * BODY + c, c % 3
                act.wait_ge(s_gup, e + 1)
                if c >= 3:
                    act.wait_ge(s_gt, e - 2)
                sc.activation(gu[j][:, :], bank[1 + j], ACT.Copy).then_inc(s_gue, 1)

            def scale_out(i, c):
                e, j = i * BODY + c, c % 3
                act.wait_ge(s_yp, e + 1)
                if c >= 3:
                    act.wait_ge(s_sct[j], uses(i, c - 3, 3) * 16)
                sc.activation(ys[j][:, :], bank[5 + j], ACT.Copy, scale=tabW[:, bass.ds(e, 1)]).then_inc(s_ye, 1)

            def sigmoid(i, c):
                e, j = i * BODY + c, c % 3
                act.wait_ge(s_gt, e + 1)
                if c >= 3:
                    act.wait_ge(s_hh, e - 2)
                sc.activation(sgm[j][:, :, :], bank[4].rearrange("p (q s) -> p q s", q=4)[:, :, 0:CAP], ACT.Sigmoid).then_inc(s_sgm, 1)

            def expert(i, c):
                copy_gu(i, c)
                if c:
                    scale_out(i, c - 1)
                sigmoid(i, c)

            act.wait_ge(s_tabc, 3)
            for e in range(E_LOOP):
                expert(0, e)
            with act.Fori(0, (E_TAIL - E_LOOP) // BODY) as i:
                for c in range(E_LOOP, E_LOOP + BODY):
                    expert(i, c)
            for e in range(E_TAIL, NE):
                expert(0, e)
            scale_out(0, NE - 1)

            act.wait_ge(s_tabo, 1)
            n_over = act.value_load(ovT[0:1, NOV:NOV + 1], min_val=0, max_val=NOV)
            with act.If(n_over > 0):
                with act.Fori(0, NOV) as i:
                    act.wait_ge(s_ov["free"], i + 1)
                    act.wait_ge(s_ov["gu"], i + 1)
                    sc.activation(gu[0][:, :], bank[1], ACT.Copy).then_inc(s_ov["ge"], 1)
                    act.wait_ge(s_ov["gt"], i + 1)
                    sc.activation(sgm[0][:, :, :], bank[4].rearrange("p (q s) -> p q s", q=4)[:, :, 0:CAP], ACT.Sigmoid).then_inc(s_ov["sg"], 1)
                    act.wait_ge(s_ov["y"], i + 1)
                    sc.activation(ys[0][:, :], bank[5], ACT.Copy, scale=tabW[:, bass.ds(i + NE, 1)]).then_inc(s_ov["ye"], 1)

            def normalise(m):
                r = ROWS[ORDER[m]]
                act.wait_ge(s_nr, m + 1)
                sc.activation(z2[m % 3][0:r, :], z2[m % 3][0:r, :], ACT.Identity, scale=mv[0:r, m % 3, 3:4],
                              bias=mv[0:r, m % 3, 0:1]).then_inc(s_nz, 1)

            root_of(0, TT)
            for m in range(TT):
                if m + 1 < TT:
                    normalise(m)
                if m + 1 < TT:
                    root_of(m + 1, TT)

        @block.vector
        def _(dve):
            v = nc.vector
            dc = [0]

            def mark(ins):
                dc[0] += 1
                ins.then_inc(d_c, 1)
                return dc[0]

            def link(ins):
                dve.wait_ge(d_c, mark(ins))

            def split_x(n):
                r = ROWS[n]
                dve.wait_ge(s_xh, n + 1)
                v.tensor_tensor(xTl[:, :, n * P:n * P + r], flat[n % 2].rearrange("p (k c) -> p k c", k=KT)[:, :, 0:r],
                                xTh[:, :, n * P:n * P + r].bitcast(F32), ALU.subtract).then_inc(s_xl, 1)

            def w_lo(t):
                dve.wait_ge(s_hi, t + 1)
                v.tensor_tensor(wcol(t, rawL), wcol(t, raw), whi(t).bitcast(F32), ALU.subtract).then_inc(s_lo, 1)

            for n in range(TT):
                split_x(n)
            for t in range(2):
                w_lo(t)
            dve.wait_ge(s_vT, 1)
            v.tensor_copy(col[:, :], bank[4][:, 0:NVEC]).then_inc(s_col, 1)
            dve.wait_ge(s_col, 1)
            dve.wait_ge(s_cst, 4)
            link(v.tensor_scalar(colh[:, :], col[:, 28:44], 0.5, None, ALU.mult))
            la = col[:, R_LAM:R_LAM + 8]
            link(v.tensor_scalar(lam[:, 2, :], la, -1.0, None, ALU.mult))
            v.tensor_tensor(lam[:, 0, :], lam[:, 2, :], la, ALU.max).then_inc(s_lam, 1)
            dve.wait_ge(s_stT, 1)
            stp = bank[5][:, 0:256].rearrange("p (k r) -> p k r", k=KT)
            for j in range(3):
                ins = v.tensor_copy(xp[:, :, 3 + SEQ + j:XPW:CONV], stp[:, :, j:24:3])
            ins.then_inc(s_stc, 1)
            v.tensor_copy(h0[:, :, :], stp[:, :, 24:32]).then_inc(s_stc, 1)

            def decay_rates():
                dve.wait_ge(s_lamE, 1)
                z_, s_, q_, p_ = lam[:, 1, :], lam[:, 0, :], lam[:, 3, :], cf[:, :]
                link(v.tensor_scalar(s_, z_, 2.0, None, ALU.add))
                link(v.reciprocal(s_, s_))
                link(v.tensor_tensor(s_, s_, z_, ALU.mult))
                link(v.tensor_tensor(q_, s_, s_, ALU.mult))
                link(v.tensor_scalar(p_, q_, 1.0 / 17, 1.0 / 15, ALU.mult, ALU.add))
                for n in (13, 11, 9, 7, 5, 3, 1):
                    link(v.tensor_tensor(p_, p_, q_, ALU.mult))
                    link(v.tensor_scalar(p_, p_, 1.0 / n, None, ALU.add))
                link(v.tensor_tensor(p_, p_, s_, ALU.mult))
                link(v.tensor_scalar(lam[:, 2, :], lam[:, 2, :], 0.0, None, ALU.max))
                link(v.scalar_tensor_tensor(out=q_, in0=p_, scalar=2.0, in1=lam[:, 2, :], op0=ALU.mult, op1=ALU.add))
                link(v.tensor_scalar(cf[:, :], q_, -8.0, None, ALU.mult))
                v.tensor_scalar(ncf[:, :], q_, 8.0, None, ALU.mult).then_inc(s_cf, 1)

            def wo_lo(k):
                dve.wait_ge(s_hi, NT + k + 1)
                v.scalar_tensor_tensor(out=woL[k // 4][:, k % 4, :], in0=wo_raw[k // 4][:, k % 4, :], scalar=0.5,
                                       in1=woH[:, k, :].bitcast(F32), op0=ALU.mult, op1=ALU.subtract).then_inc(s_lo, 1)

            def conv(i):
                dve.wait_ge(*emptied(i))
                if i == 0:
                    dve.wait_ge(s_stc, 2)
                if i >= 2:
                    dve.wait_ge(s_gate, i - 1)
                    dve.wait_ge(s_gx, i - 1)
                x = xc[i % 2]
                link(v.tensor_scalar(x[:, :], xp[:, i, 0:XCW], col[:, R_WCONV + i:R_WCONV + i + 1],
                                     col[:, R_BCONV + i:R_BCONV + i + 1], ALU.mult, ALU.add))
                for j in range(1, CONV):
                    r = R_WCONV + 8 * j + i
                    ins = v.scalar_tensor_tensor(out=x[:, :], in0=xp[:, i, j:j + XCW], scalar=col[:, r:r + 1], in1=x[:, :],
                                                 op0=ALU.mult, op1=ALU.add)
                    if j < CONV - 1:
                        link(ins)
                ins.then_inc(s_cv, 1)

            def gated(i):
                dve.wait_ge(s_cv, i + 1)
                dve.wait_ge(s_sig, 3 * i + 2)
                v.tensor_tensor(gT[:, i, :], si[i % 2][:, :], xc[i % 2][:, :], ALU.mult).then_inc(s_gx, 1)

            def square(first):
                for i in range(first, first + 4):
                    dve.wait_ge(s_a, i + 1)
                    if i:
                        dve.wait_ge(s_om, 2 * i)
                    v.tensor_tensor(a2[:, :], aL[:, i, :], aL[:, i, :], ALU.mult).then_inc(s_om, 1)
                    dve.wait_ge(s_om, 2 * i + 1)
                    v.scalar_tensor_tensor(out=hL[:, i, :], in0=a2[:, :], scalar=1.0, in1=hL[:, i, :],
                                           op0=ALU.add, op1=ALU.mult).then_inc(s_om, 1)

            def scan(first):
                for i in range(first, first + 4):
                    dve.wait_ge(s_rt, i + 1)
                    dve.wait_ge(s_gx, 8)
                    link(v.tensor_tensor(gT[:, i, :], gT[:, i, :], hL[:, i, :], ALU.mult))
                    v.tensor_tensor_scan(hL[:, i, 0:SEQ], aL[:, i, 0:SEQ], gT[:, i, 0:SEQ], 0.0, ALU.mult, ALU.add).then_inc(s_h, 1)
                    link(v.tensor_tensor(h0[:, i, :], h0[:, i, :], sample_cols(aL[:, i, :]), ALU.mult))
                    v.tensor_tensor(hL[:, i, SEQ:T], h0[:, i, :], sample_cols(gT[:, i, :]), ALU.add).then_inc(s_h, 1)

            def kv():
                dve.wait_ge(s_kvT, 1)
                v.tensor_copy(kwin[:, :], bank[4][:, 0:256]).then_inc(s_kvd, 1)
                v.tensor_copy(snew[:, :], bank[5][0:NS, :]).then_inc(s_kvd, 1)

            def conv_state():
                dve.wait_ge(s_ocT, 1)
                for n in range(2):
                    v.tensor_copy(oc[:, n * 512:(n + 1) * 512], pair[2][0:XPW - SEQ, n, :]).then_inc(s_ocv, 1)

            def h_state():
                dve.wait_ge(s_ohT, 1)
                for n in range(2):
                    v.tensor_copy(oh[:, n * 512:(n + 1) * 512], pair[2][0:NS + 1, n, :]).then_inc(s_ohv, 1)

            def masked(u, par):
                p2, n = _UNITS[u]
                lo = 0 if n else P
                m = 2 * u + par
                dve.wait_ge(s_sc, m + 1)
                if m == 0:
                    dve.wait_ge(s_snk, 16)
                    dve.wait_ge(s_cst, 6)
                if m >= 2:
                    dve.wait_ge(s_tr, m - 1)
                    dve.wait_ge(s_nrm, 4 * (m - 1))
                for h in range(GRP):
                    head = (2 * p2 + par) * GRP + h
                    v.tensor_tensor_reduce(out=sS[par][:, h, lo:256], in0=pair[2][:, h // 2, (h % 2) * 256 + lo:(h % 2) * 256 + 256],
                                           in1=mask[:, lo:256], scale=HD ** -0.5, scalar=sk8[:, head:head + 1],
                                           op0=ALU.add, op1=ALU.max, accum_out=mx[:, par, h:h + 1]).then_inc(s_ttr, 1)
                dve.wait_ge(s_ttr, 4 * (m + 1))
                v.tensor_scalar(nm[:, par, :], mx[:, par, :], -1.0, None, ALU.mult).then_inc(s_nm, 1)
                g = (2 * p2 + par) * GRP
                v.tensor_tensor(es[:, par, :], sk8[:, g:g + GRP], mx[:, par, :], ALU.subtract).then_inc(s_nm, 1)

            def normal(u, par):
                p2, n = _UNITS[u]
                lo = 0 if n else P
                m = 2 * u + par
                dve.wait_ge(s_ex, 5 * (m + 1))
                link(v.tensor_tensor(dn[:, par, :], dn[:, par, :], es[:, par, :], ALU.add))
                link(v.reciprocal(dn[:, par, :], dn[:, par, :]))
                for h in range(GRP):
                    v.tensor_scalar(sS[par][:, h, lo:256], sS[par][:, h, lo:256], dn[:, par, h:h + 1], None, ALU.mult).then_inc(s_nrm, 1)

            def probs_t(u, par):
                p2, n = _UNITS[u]
                dve.wait_ge(s_tr, 2 * u + par + 1)
                if u == 0:
                    dve.wait_ge(s_kv_out, 64)
                    dve.wait_ge(s_cv_ld, 32)
                else:
                    dve.wait_ge(s_pv, u)
                if u == 1:
                    dve.wait_ge(s_spv, 1)
                if n:
                    v.tensor_copy(pT[:, par, 1, :], bank[7]).then_inc(s_pd, 1)
                else:
                    v.tensor_copy(pT[:, par, 1, 256:512], bank[7][:, 256:512]).then_inc(s_pd, 1)

            def attend(u):
                p2, n = _UNITS[u]
                dve.wait_ge(s_atth, u + 1)
                if u == 0:
                    dve.wait_ge(s_h, 16)
                v.tensor_tensor(attL[:, 4 * p2:4 * p2 + 4, n * P:(n + 1) * P], bank[6].rearrange("p (h q) -> p h q", h=4),
                                attH[:, 4 * p2:4 * p2 + 4, n * P:(n + 1) * P].bitcast(F32), ALU.subtract).then_inc(s_attl, 1)

            def cache_t(r):
                dve.wait_ge(s_skT, r + 1)
                v.tensor_copy(kS[:, 1, 4 * r:4 * r + 4, :], bank[7].rearrange("p (b w) -> p b w", b=4)).then_inc(s_skd, 1)
                if r == 1:
                    dve.wait_ge(s_ska, 2)
                    dve.wait_ge(s_skd, 2)
                    for p2 in range(2):
                        for a in range(2):
                            half = slice(a * HD, (a + 1) * HD)
                            v.tensor_copy(kS[half, p2, :, 0], kz[half, p2, a, SEQ:T]).then_inc(s_skd, 1)
                    dve.wait_ge(s_qz, 1)
                    dve.wait_ge(*emptied(FIRST["q"] + 7))
                    q4 = qz[:, :, :].rearrange("p (b P) (z a h) -> p P z a h b", P=2, a=2, h=4)
                    for p2 in range(2):
                        for a in range(2):
                            half = slice(a * HD, (a + 1) * HD)
                            v.tensor_copy(q4[half, p2, 0, a, :, :], qT[half, 4 * p2:4 * p2 + 4, SEQ:T]).then_inc(s_qz, 1)

            def sample_max():
                dve.wait_ge(s_ss, 1)
                dve.wait_ge(s_snr, 64)
                dve.wait_ge(s_pv, 1)
                s4 = bank[4].rearrange("p (m w) -> p m w", m=4)
                v.tensor_scalar(sSm[:, :, :], s4, HD ** -0.5, None, ALU.mult).then_inc(s_sm, 1)
                dve.wait_ge(s_sm, 1)
                v.tensor_reduce(smx[:, 0, :], sSm[:, :, :], AX.X, ALU.max).then_inc(s_sm, 1)
                dve.wait_ge(s_sm, 2)
                v.tensor_scalar(smx[:, 0, :], smx[:, 0, :], sks[:, 0:1], None, ALU.max).then_inc(s_sm, 1)
                dve.wait_ge(s_sm, 3)
                v.tensor_scalar(smx[:, 1, :], smx[:, 0, :], -1.0, None, ALU.mult).then_inc(s_sm, 1)
                dve.wait_ge(s_sm, 4)
                v.tensor_scalar(smx[:, 2, :], smx[:, 1, :], sks[:, 0:1], None, ALU.add).then_inc(s_sm, 1)
                link(v.tensor_copy(smx[:, 3, :], smx[:, 0, :]))
                v.tensor_copy(mx[:, 0, :], smx[:, 0, :]).then_inc(s_sm, 1)
                v.tensor_copy(mx[:, 1, :], smx[:, 0, :]).then_inc(s_sm, 1)

            def sample_normal():
                dve.wait_ge(s_se, 5)
                link(v.tensor_tensor(smx[:, 3, :], smx[:, 3, :], smx[:, 2, :], ALU.add))
                link(v.reciprocal(smx[:, 3, :], smx[:, 3, :]))
                for m in range(4):
                    v.tensor_scalar(sSm[:, m, :], sSm[:, m, :], smx[:, 3, m:m + 1], None, ALU.mult).then_inc(s_sn, 1)

            def sample_t():
                dve.wait_ge(s_spT, 1)
                v.tensor_copy(pTs[:, :, :].rearrange("p a b -> p (a b)"), bank[7]).then_inc(s_spc, 1)

            def sample_att():
                dve.wait_ge(s_sah, 2)
                o = bank[6][:, 0:P].rearrange("p (b P a h) -> p P a h b", b=NS, P=2, a=2)
                for a in range(2):
                    half = slice(a * HD, (a + 1) * HD)
                    for p2 in range(2):
                        ins = v.tensor_tensor(attL[half, 4 * p2:4 * p2 + 4, SEQ:T], o[half, p2, a, :, :],
                                              attH[half, 4 * p2:4 * p2 + 4, SEQ:T].bitcast(F32), ALU.subtract)
                    ins.then_inc(s_sal, 1)

            def read_tile(t):
                kind, i = TILES[t]
                if kind == "ly":
                    dve.wait_ge(*emptied(t))
                    v.tensor_scalar(y2[:, :], y2[:, :], 0.044715, 1.0, ALU.mult, ALU.add).then_inc(s_yq, 1)
                    dve.wait_ge(s_yq, 2 * i + 1)
                    v.tensor_tensor(y2[:, :], y2[:, :], yb[:, :], ALU.mult).then_inc(s_yq, 1)
                    dve.wait_ge(s_yt, i + 1)
                    dve.wait_ge(s_h, 16)
                    dve.wait_ge(s_ohT, 1)
                    link(v.scalar_tensor_tensor(out=yb[:, :], in0=y2[:, :], scalar=1.0, in1=yb[:, :], op0=ALU.add, op1=ALU.mult))
                    link(v.scalar_tensor_tensor(out=yb[:, :], in0=yb[:, :], scalar=0.5, in1=hL[:, i, 0:T], op0=ALU.mult, op1=ALU.mult))
                    link(v.tensor_copy(recH[:, i, 0:T], yb[:, :]))
                    v.tensor_tensor(recL[:, i, 0:T], yb[:, :], recH[:, i, 0:T].bitcast(F32), ALU.subtract).then_inc(s_rec, 1)
                elif kind == "lo":
                    dve.wait_ge(s_proj, t + 1)
                    dve.wait_ge(*emptied(FIRST["gl"] + i if i < 4 else FIRST["gl"] + 8 + i - 4))
                    if i == 0:
                        dve.wait_ge(s_spv, 1)
                    v.scalar_tensor_tensor(out=halves(m1[:, i, :]), in0=halves(sg[:, i % 4, :]), scalar=1.0,
                                           in1=pair[t % 2][:, :, 0:HT], op0=ALU.add, op1=ALU.mult).then_inc(s_evd, 1)
                elif kind == "ao":
                    dve.wait_ge(s_proj, t + 1)
                    dve.wait_ge(*emptied(FIRST["ga"] + i if i < 4 else FIRST["ga"] + 8 + i - 4))
                    v.scalar_tensor_tensor(out=halves(sg[:, i % 4, :]), in0=halves(sg[:, i % 4, :]), scalar=1.0,
                                           in1=pair[t % 2][:, :, 0:HT], op0=ALU.add, op1=ALU.mult).then_inc(s_evd, 1)
                    dve.wait_ge(*emptied(t))
                    link(v.tensor_tensor(sg[:, i % 4, :], sg[:, i % 4, :], m1[:, i, :], ALU.add))
                    link(v.tensor_copy(mgH[:, i, :], sg[:, i % 4, :]))
                    v.tensor_tensor(mgL[:, i, 0:T], sg[:, i % 4, :], mgH[:, i, :].bitcast(F32), ALU.subtract).then_inc(s_mg, 1)

            for t in range(2, AHEAD):
                w_lo(t)
            for step in STEPS:
                what, args = step[0], step[1:]
                if what == "tile":
                    t = args[0]
                    if t + AHEAD < NT:
                        w_lo(t + AHEAD)
                    kind, i = TILES[t]
                    if kind == "lx":
                        conv(i)
                    if t == 0:
                        decay_rates()
                    if kind in ("ly", "lo", "ao"):
                        read_tile(t)
                elif what == "gate":
                    gated(*args)
                elif what == "sq":
                    square(*args)
                elif what == "kv":
                    kv()
                elif what == "scan":
                    scan(*args)
                elif what == "oc":
                    conv_state()
                elif what == "oh":
                    h_state()
                elif what == "sc":
                    masked(*args)
                elif what == "nrm":
                    normal(*args)
                elif what == "tr":
                    probs_t(*args)
                elif what == "pv":
                    attend(*args)
                elif what == "sk":
                    cache_t(*args)
                elif what == "ss":
                    sample_max()
                elif what == "sn":
                    sample_normal()
                elif what == "st":
                    sample_t()
                elif what == "sp":
                    sample_att()
                elif what == "wo":
                    wo_lo(*args)

            def norm_stats(z, r, k):
                v.bn_stats(st6[0:r, k % 2, 0, :], z[0:r, 0:512]).then_inc(d_c, 1)
                dc[0] += 1
                link(v.bn_stats(st6[0:r, k % 2, 1, :], z[0:r, 512:D]))
                v.bn_aggr(mv[0:r, k, 0:2], st6[0:r, k % 2, :, :]).then_inc(s_z, 1)

            def stats1(m):
                n = ORDER[m]
                r = ROWS[n]
                z, k = z1[m % 2], m % 3
                dve.wait_ge(s_mix, m + 1)
                dve.wait_ge(s_x[n], 32)
                if m == 0:
                    dve.wait_ge(s_proj, NT)
                link(v.scalar_tensor_tensor(out=z[0:r, :], in0=xre[m % 2][0:r, :], scalar=ALPHA, in1=flat[m % 2][0:r, :],
                                            op0=ALU.mult, op1=ALU.add))
                norm_stats(z, r, k)

            def scale1(m):
                r, z, k = ROWS[ORDER[m]], z1[m % 2], m % 3
                dve.wait_ge(s_ln, 96)
                dve.wait_ge(s_z, m + 1)
                link(v.scalar_tensor_tensor(out=z[0:r, :], in0=z[0:r, :], scalar=mv[0:r, k, 0:1], in1=lnG[0:r, :],
                                            op0=ALU.subtract, op1=ALU.mult))
                dve.wait_ge(s_sd, m + 1)
                link(v.reciprocal(mv[0:r, k, 3:4], mv[0:r, k, 2:3]))
                if m >= 2:
                    dve.wait_ge(s_x1o[m % 2], 16 * (m // 2))
                    dve.wait_ge(s_x1T, m - 1)
                v.scalar_tensor_tensor(out=x1[m % 2][0:r, :], in0=z[0:r, :], scalar=mv[0:r, k, 3:4], in1=lnB[0:r, :],
                                       op0=ALU.mult, op1=ALU.add).then_inc(s_x1, 1)

            def keep_logits(m):
                r = ROWS[ORDER[m]]
                dve.wait_ge(s_lg, m + 1)
                dve.wait_ge(s_rcst, 13)
                v.tensor_tensor(lgG[0:r, m, :], bank[6 + m % 2][0:r, 0:NG], rb[0:r, 0:NG], ALU.add).then_inc(s_lgc, 1)
                v.tensor_tensor(lgE[0:r, m, :], bank[6 + m % 2][0:r, NG:NG + NE], rb[0:r, NG:], ALU.add).then_inc(s_lgc, 1)

            def wide(ap, n):
                return ap.rearrange("p (t a) -> p t a", a=1).to_broadcast([P, ap.shape[1], n])

            def first_hot(x, n, io, best, idx, out):
                link(v.tensor_reduce(best, x, AX.X, ALU.max))
                link(v.tensor_tensor(out, x, wide(best, n), ALU.is_equal))
                link(v.tensor_scalar(out, out, -64.0, 64.0, ALU.mult, ALU.add))
                io3 = io[:, :].rearrange("p (a n) -> p a n", a=1).to_broadcast([P, x.shape[1], n])
                link(v.tensor_tensor(out, out, io3, ALU.add))
                link(v.tensor_reduce(idx, out, AX.X, ALU.min))
                link(v.tensor_tensor(out, io3, wide(idx, n), ALU.is_equal))

            k0, k1 = hot[:, 0, :, :], hot[:, 1, :, :]

            def choose(ts):
                nt = ts.stop - ts.start
                grp = lgG[:, ts, :]
                link(v.tensor_reduce(w5[0][:, ts], grp, AX.X, ALU.max))
                v.tensor_tensor(g20[0][:, ts, :], grp, wide(w5[0][:, ts], NG), ALU.subtract).then_inc(s_rd, 1)
                first_hot(grp, NG, io4, w5[1][:, ts], w5[2][:, ts], g20[1][:, ts, :])
                link(v.tensor_scalar(g20[2][:, ts, :], g20[1][:, ts, :], BIG, -BIG, ALU.mult, ALU.add))

                def per_expert(ap):
                    return ap.rearrange("p t (g a) -> p (t g) a", a=1).to_broadcast([P, nt * NG, EPG])

                e3 = lgE[:, ts, :].rearrange("p t (g e) -> p (t g) e", g=NG)
                sel3 = esel[:, ts, :].rearrange("p t (g e) -> p (t g) e", g=NG)
                link(v.tensor_tensor(sel3, e3, per_expert(g20[1][:, ts, :]), ALU.mult))
                link(v.tensor_tensor(sel3, sel3, per_expert(g20[2][:, ts, :]), ALU.add))
                first_hot(esel[:, ts, :], NE, io32, w5[1][:, ts], w10[0][:, 0, ts], k0[:, ts, :])
                link(v.scalar_tensor_tensor(out=esel[:, ts, :], in0=k0[:, ts, :], scalar=-2.0 * BIG, in1=esel[:, ts, :],
                                            op0=ALU.mult, op1=ALU.add))
                first_hot(esel[:, ts, :], NE, io32, w5[2][:, ts], w10[0][:, 1, ts], k1[:, ts, :])
                v.tensor_tensor(w5[3][:, ts], w5[2][:, ts], w5[1][:, ts], ALU.subtract).then_inc(s_rd, 1)
                link(v.tensor_tensor(e160[0][:, ts, :], k0[:, ts, :], k1[:, ts, :], ALU.add))
                v.tensor_tensor(hotB[:, ts, :], e160[0][:, ts, :], wide(valid[:, ts], NE), ALU.mult).then_inc(s_hot, 1)

            for m in range(TT - 1):
                stats1(m)
                scale1(m)
                if m >= 2:
                    keep_logits(m - 2)
            keep_logits(2)
            dve.wait_ge(s_lgc, 6)
            choose(EARLY)
            for k in range(2):
                link(v.tensor_tensor(w10[2][:, k, :], tokv[:, k, :], valid[:, :], ALU.mult))
            link(v.tensor_copy(w10[3][:, 0, :], w10[2][:, 0, :]))
            link(v.scalar_tensor_tensor(out=w10[3][:, 1, :], in0=valid[:, :], scalar=2.0 * T, in1=w10[2][:, 1, :], op0=ALU.mult, op1=ALU.add))
            stats1(TT - 1)
            scale1(TT - 1)
            keep_logits(3)
            keep_logits(4)
            dve.wait_ge(s_lgc, 2 * TT)
            choose(LATE)
            dve.wait_ge(s_re, 4)
            link(v.tensor_reduce(w5[4][:, :], g20[0][:, :, :], AX.X, ALU.add))
            link(v.scalar_tensor_tensor(out=w5[4][:, :], in0=w5[3][:, :], scalar=1.0, in1=w5[4][:, :], op0=ALU.add, op1=ALU.mult))
            link(v.reciprocal(w5[4][:, :], w5[4][:, :]))
            link(v.tensor_tensor(w10[1][:, 0, :], w5[4][:, :], valid[:, :], ALU.mult))
            link(v.tensor_tensor(w10[1][:, 1, :], w10[1][:, 0, :], w5[3][:, :], ALU.mult))

            dve.wait_ge(s_pre, 1)
            link(v.tensor_copy(cum[:, 0, :], bank[7][:, TT * NE:(TT + 1) * NE]))

            def floor64(x):
                link(v.tensor_scalar(x, x, 1.0 / CAP, 0.5 / CAP - 0.5, ALU.mult, ALU.add))
                link(v.tensor_scalar(x, x, 12582912.0, None, ALU.add))
                link(v.tensor_scalar(x, x, -12582912.0, None, ALU.add))

            link(v.tensor_scalar(cum[:, 1, :], cum[:, 0, :], 1.0, -1.0, ALU.max, ALU.add))
            floor64(cum[:, 1, :])
            link(v.memset(cum[:, 3, :], 1.0))
            link(v.tensor_tensor_scan(cum[:, 2, :], cum[:, 3, :], cum[:, 1, :], 0.0, ALU.mult, ALU.add))
            link(v.tensor_tensor(cum[:, 3, :], cum[:, 2, :], cum[:, 1, :], ALU.subtract))
            pre = bank[7][:, 0:TT * NE].rearrange("p (a n) -> p a n", a=1).to_broadcast([P, 2, TT * NE])
            base3 = cum[:, 3, :].rearrange("p (a e) -> p a e", a=1).to_broadcast([P, 2 * TT, NE])
            hot10 = hot[:, :, :, :].rearrange("p k t e -> p (k t) e")
            f45 = [w10[n][:, :, :].rearrange("p k t -> p (k t)") for n in (4, 5)]
            v.tensor_tensor(e320[0][:, :, :].rearrange("p (k t) e -> p k (t e)", k=2),
                            hot[:, :, :, :].rearrange("p k t e -> p k (t e)"), pre, ALU.mult).then_inc(d_c, 1)
            dc[0] += 1
            link(v.tensor_tensor(e320[1][:, :, :], hot10, base3, ALU.mult))
            v.tensor_reduce(f45[0], e320[0][:, :, :], AX.X, ALU.add).then_inc(d_c, 1)
            dc[0] += 1
            link(v.tensor_reduce(f45[1], e320[1][:, :, :], AX.X, ALU.add))
            f = [w[:, :, :].rearrange("p k t -> p (k t)") for w in w10]
            link(v.tensor_copy(f[6], f[4]))
            floor64(f[6])
            link(v.scalar_tensor_tensor(out=f[4], in0=f[6], scalar=-float(CAP), in1=f[4], op0=ALU.mult, op1=ALU.add))
            link(v.tensor_scalar(f[7], f[6], 1.0, None, ALU.min))
            link(v.scalar_tensor_tensor(out=f[5], in0=f[5], scalar=float(NE - 1), in1=f[6], op0=ALU.add, op1=ALU.add))
            link(v.tensor_tensor(f[5], f[5], f[0], ALU.subtract))
            link(v.tensor_tensor(f[5], f[5], f[7], ALU.mult))
            link(v.tensor_tensor(f[5], f[5], f[0], ALU.add))
            def along(x, n):
                return x.rearrange("p (t a) -> p t a", a=1).to_broadcast([P, TT, n])

            def of_tokens(io, n):
                return io.rearrange("p (a n) -> p a n", a=1).to_broadcast([P, TT, n])

            dve.wait_ge(s_x1o[1], 32)
            for k in range(2):
                ts = slice(k * TT, (k + 1) * TT)
                v.tensor_tensor(rk[:, ts, :], of_tokens(io128[:, :], P), along(f[4][:, ts], P), ALU.is_equal).then_inc(d_c, 1)
                dc[0] += 1
                link(v.tensor_tensor(bkE[:, ts, :], of_tokens(io48[:, :], NBLK), along(f[5][:, ts], NBLK), ALU.is_equal))
                for n, val in enumerate((f[2], f[3], f[1])):
                    ins = v.tensor_tensor(bk[:, ts, n, :], bkE[:, ts, :], along(val[:, ts], NBLK), ALU.mult)
                ins.then_inc(s_oh10, 1)
            inc = cum[:, 2, :].rearrange("p (a e) -> p a e", a=1).to_broadcast([P, NOV, NE])
            i16 = io48[:, 0:NOV].rearrange("p (n a) -> p n a", a=1).to_broadcast([P, NOV, NE])
            link(v.tensor_tensor(ov16[:, :, :], inc, i16, ALU.is_le))
            link(v.tensor_reduce(ovf[:, 0:NOV], ov16[:, :, :], AX.X, ALU.add))
            link(v.tensor_scalar(ovf[:, 0:NOV], ovf[:, 0:NOV], float(NE - 1), None, ALU.min))
            link(v.tensor_copy(ovf[:, NOV:NOV + 1], cum[:, 2, NE - 1:NE]))
            v.tensor_copy(ovT[:, :], ovf[:, :]).then_inc(s_tabo, 1)
            dve.wait_ge(s_tab, 1)
            v.tensor_scalar(tabG[:, :], bank[6][:, 0:NBLK], off[:, 0:1], None, ALU.add).then_inc(s_tabc, 1)
            v.tensor_scalar(tabD[:, :], bank[6][:, NBLK:2 * NBLK], off[:, 0:1], None, ALU.add).then_inc(s_tabc, 1)
            v.tensor_copy(tabW[:, :], bank[6][:, 2 * NBLK:3 * NBLK]).then_inc(s_tabc, 1)

            def copy_xt(i, c):
                e, j = i * BODY + c, c % 3
                dve.wait_ge(s_xtp, e + 1)
                if c >= 3:
                    dve.wait_ge(s_gup, e - 2)
                v.tensor_copy(xt[j][:, :], bank[0]).then_inc(s_xte, 1)

            def hidden(i, c):
                e, j = i * BODY + c, c % 3
                dve.wait_ge(s_sgm, e + 1)
                v.tensor_tensor(sgm[j][:, :, :], sgm[j][:, :, :], t4[:, :, 0:CAP], ALU.mult).then_inc(s_h1, 1)
                dve.wait_ge(s_h1, e + 1)
                if c >= 3:
                    dve.wait_ge(s_yp, e - 2)
                v.tensor_tensor(hT[j][:, :, :], sgm[j][:, :, :], t4[:, :, CAP:P], ALU.mult).then_inc(s_hh, 1)

            def expert(i, c):
                if not (isinstance(i, int) and c + 1 == NE):
                    copy_xt(i, c + 1)
                hidden(i, c)

            t4 = bank[4].rearrange("p (q s) -> p q s", q=4)
            copy_xt(0, 0)
            for e in range(E_LOOP):
                expert(0, e)
            with dve.Fori(0, (E_TAIL - E_LOOP) // BODY) as i:
                for c in range(E_LOOP, E_LOOP + BODY):
                    expert(i, c)
            for e in range(E_TAIL, NE):
                expert(0, e)

            dve.wait_ge(s_tabo, 1)
            n_over = dve.value_load(ovT[0:1, NOV:NOV + 1], min_val=0, max_val=NOV)
            with dve.If(n_over > 0):
                with dve.Fori(0, NOV) as i:
                    dve.wait_ge(s_ov["xt"], i + 1)
                    v.tensor_copy(xt[0][:, :], bank[0]).then_inc(s_ov["xe"], 1)
                    dve.wait_ge(s_ov["sg"], i + 1)
                    v.tensor_tensor(sgm[0][:, :, :], sgm[0][:, :, :], t4[:, :, 0:CAP], ALU.mult).then_inc(s_ov["h1"], 1)
                    dve.wait_ge(s_ov["h1"], i + 1)
                    v.tensor_tensor(hT[0][:, :, :], sgm[0][:, :, :], t4[:, :, CAP:P], ALU.mult).then_inc(s_ov["h"], 1)

            def stats2(m):
                n = ORDER[m]
                r, z, k = ROWS[n], z2[m % 3], m % 3
                dve.wait_ge(s_xr, 16 * TT)
                if m >= 3:
                    dve.wait_ge(s_y3, m - 2)
                if m:
                    dve.wait_ge(s_mix, TT + m)
                    rows_sum = flat[m % 2][0:r, :]
                else:
                    dve.wait_ge(s_x[n], 64)
                    link(v.tensor_tensor(f0[n][0:r, :], f0[n][0:r, :], f1[n][0:r, :], ALU.add))
                    rows_sum = f0[n][0:r, :]
                link(v.scalar_tensor_tensor(out=z[0:r, :], in0=xr2[n][0:r, :], scalar=ALPHA, in1=rows_sum,
                                            op0=ALU.mult, op1=ALU.add))
                norm_stats(z, r, k)

            def factors(m):
                r, k = ROWS[ORDER[m]], m % 3
                dve.wait_ge(s_sd, TT + m + 1)
                link(v.reciprocal(mv[0:r, k, 3:4], mv[0:r, k, 2:3]))
                v.scalar_tensor_tensor(out=mv[0:r, k, 0:1], in0=mv[0:r, k, 0:1], scalar=-1.0, in1=mv[0:r, k, 3:4],
                                       op0=ALU.mult, op1=ALU.mult).then_inc(s_nr, 1)

            def scale2(m):
                r, z = ROWS[ORDER[m]], z2[m % 3]
                dve.wait_ge(s_l2, 32)
                dve.wait_ge(s_nz, m + 1)
                v.tensor_tensor(z[0:r, :], z[0:r, :], ln2G[0:r, :], ALU.mult).then_inc(s_y2, 1)

            def finish(m):
                r, z, k = ROWS[ORDER[m]], z2[m % 3], m % 3
                dve.wait_ge(s_z, TT + m + 1)
                link(v.scalar_tensor_tensor(out=z[0:r, :], in0=z[0:r, :], scalar=mv[0:r, k, 0:1], in1=ln2G[0:r, :],
                                            op0=ALU.subtract, op1=ALU.mult))
                dve.wait_ge(s_sd, TT + m + 1)
                link(v.reciprocal(mv[0:r, k, 3:4], mv[0:r, k, 2:3]))
                dve.wait_ge(s_yo[m % 2], 16 * (m // 2))
                v.scalar_tensor_tensor(out=y_out[m % 2][0:r, :], in0=z[0:r, :], scalar=mv[0:r, k, 3:4], in1=ln2B[0:r, :],
                                       op0=ALU.mult, op1=ALU.add).then_inc(s_y2, 1)

            stats2(0)
            factors(0)
            for m in range(TT - 1):
                stats2(m + 1)
                if m + 1 < TT - 1:
                    factors(m + 1)
                scale2(m)
            finish(TT - 1)


_INS = ["x_prompt", "x_sample", "cache_k", "cache_v", "state_conv", "state_lru_h", "w_in", "b_in", "w_conv", "b_conv",
        "w_rg", "b_rg", "w_ig", "b_ig", "lru_lambda", "sinks", "w_lru_out", "w_attn_out", "w_o", "ln1_g", "ln1_b",
        "w_group", "b_group", "w_router", "b_router", "w_gate", "w_up", "w_down", "ln2_g", "ln2_b"]
_OUTS = [("y_prompt", (1, SEQ, D)), ("y_sample", (NS, 1, D)),
         ("k_win_prompt", (1, WIN, NKV, HD)), ("v_win_prompt", (1, WIN, NKV, HD)),
         ("conv_prompt", (1, CONV - 1, D)), ("h_prompt", (1, D)),
         ("k_win_sample", (NS, WIN, NKV, HD)), ("v_win_sample", (NS, WIN, NKV, HD)),
         ("conv_sample", (NS, CONV - 1, D)), ("h_sample", (NS, D))]


def kernel(**inputs):
    import numpy as np
    import concourse.bacc as bacc
    from concourse.bass_utils import run_bass_kernel_spmd

    nc = bacc.Bacc("TRN2", target_bir_lowering=False, num_devices=1)
    arrays = {"in_" + name: np.ascontiguousarray(inputs[name]) for name in _INS}
    ins = {name: nc.dram_tensor("in_" + name, arrays["in_" + name].shape, F32, kind="ExternalInput").ap() for name in _INS}
    outs = {name: nc.dram_tensor("out_" + name, shape, F32, kind="ExternalOutput").ap() for name, shape in _OUTS}
    build(nc, ins, outs)
    results = run_bass_kernel_spmd(nc, [arrays], core_ids=[0]).results[0]
    return tuple(results["out_" + name] for name, _ in _OUTS)
```
